# Optimizing a Trainium2 kernel written in Bass

```python
import math
import numpy as np
import jax
import jax.numpy as jnp
from jax import lax

D_MODEL = 1024
BATCH = 1
SEQ = 512
DEPTH = 1

HEAD_DIM = 64
NSA_HEADS = 8
NSA_KV_HEADS = 2
NSA_GROUP = NSA_HEADS // NSA_KV_HEADS
CMP_BLOCK = 32
CMP_STRIDE = 16
CMP_HIDDEN = 256
SLC_BLOCK = 64
N_SELECT = 16
WINDOW = 512
NSA_Q_BLOCK = 64
N_BRANCH = 3
CONV_CHANNELS = 256
CONV_WIDTH = 31
GLA_HEADS = 4
GLA_KEY_DIM = 128
GLA_VALUE_DIM = 256
GLA_GATE_RANK = 16
GLA_TAU = 16.0
GLA_CHUNK = 64
REL_BUCKETS = 32
REL_MAX_DIST = 128
D_FF = -(-8 * D_MODEL // (3 * 256)) * 256
PLE_DIM = 256
EPS = 1e-6
NEG = -1e30
BIG = 1e30

D_MIX = NSA_HEADS * HEAD_DIM + CONV_CHANNELS + GLA_VALUE_DIM
IN_SPLITS = (
    NSA_HEADS * HEAD_DIM,
    NSA_KV_HEADS * HEAD_DIM, NSA_KV_HEADS * HEAD_DIM,
    NSA_KV_HEADS * HEAD_DIM, NSA_KV_HEADS * HEAD_DIM,
    NSA_KV_HEADS * HEAD_DIM, NSA_KV_HEADS * HEAD_DIM,
    NSA_HEADS * N_BRANCH,
    2 * CONV_CHANNELS,
    GLA_KEY_DIM, GLA_KEY_DIM, GLA_VALUE_DIM,
    GLA_GATE_RANK,
    GLA_VALUE_DIM,
)
D_IN = sum(IN_SPLITS)


def rms_norm(x, g):
    x32 = x.astype(jnp.float32)
    y = x32 * lax.rsqrt(jnp.mean(x32 * x32, axis=-1, keepdims=True) + EPS)
    return (y * g.astype(jnp.float32)).astype(x.dtype)

def layer_norm(x, g, b):
    x32 = x.astype(jnp.float32)
    mu = jnp.mean(x32, axis=-1, keepdims=True)
    xc = x32 - mu
    y = xc * lax.rsqrt(jnp.mean(xc * xc, axis=-1, keepdims=True) + EPS)
    return (y * g.astype(jnp.float32) + b.astype(jnp.float32)).astype(x.dtype)

def t5_bucket(dist):
    n = jnp.maximum(dist, 0)
    max_exact = REL_BUCKETS // 2
    nf = jnp.maximum(n, 1).astype(jnp.float32)
    large = max_exact + (jnp.log(nf / max_exact) / math.log(REL_MAX_DIST / max_exact)
                         * (REL_BUCKETS - max_exact)).astype(jnp.int32)
    large = jnp.minimum(large, REL_BUCKETS - 1)
    return jnp.where(n < max_exact, n, large)

def masked_softmax(s, mask):
    p = jax.nn.softmax(jnp.where(mask, s, NEG), axis=-1)
    return jnp.where(mask, p, 0.0)

def compress_kv(kv, pos, w1, b1, w2):
    B, S, Hk, D = kv.shape
    r = CMP_BLOCK // CMP_STRIDE
    nsub = S // CMP_STRIDE
    ncmp = nsub - r + 1
    sub = kv.reshape(B, nsub, CMP_STRIDE, Hk, D)
    blocks = jnp.concatenate([sub[:, j:ncmp + j] for j in range(r)], axis=2)
    blocks = blocks + pos[None, None, :, None, :]
    flat = blocks.transpose(0, 1, 3, 2, 4).reshape(B, ncmp, Hk, CMP_BLOCK * D)
    return jax.nn.silu(flat @ w1 + b1) @ w2

def nsa_attention(q, kc, vc, ks, vs, kw, vw, gates, rel_bias):
    B, S = q.shape[0], q.shape[1]
    Hk, G, D = NSA_KV_HEADS, NSA_GROUP, HEAD_DIM
    ncmp = kc.shape[1]
    nsel = S // SLC_BLOCK
    n_top = min(N_SELECT, nsel)
    q = q.reshape(B, S, Hk, G, D) * (D ** -0.5)
    gates = gates.reshape(B, S, Hk, G, N_BRANCH)
    bias_h = rel_bias.T.astype(jnp.float32)
    bias_hkg = bias_h.reshape(Hk, G, REL_BUCKETS).transpose(0, 2, 1)
    cmp_end = jnp.arange(ncmp, dtype=jnp.int32) * CMP_STRIDE + (CMP_BLOCK - 1)
    rs, rc = SLC_BLOCK // CMP_STRIDE, CMP_BLOCK // CMP_STRIDE
    agg = (np.arange(nsel)[:, None, None] * rs + np.arange(rs)[None, :, None]
           - np.arange(rc)[None, None, :]).reshape(nsel, rs * rc)
    agg_valid = jnp.asarray((agg >= 0) & (agg < ncmp))
    agg_idx = jnp.asarray(np.clip(agg, 0, ncmp - 1), dtype=jnp.int32)
    ks_blk = ks.reshape(B, nsel, SLC_BLOCK, Hk, D).transpose(0, 3, 1, 2, 4)
    vs_blk = vs.reshape(B, nsel, SLC_BLOCK, Hk, D).transpose(0, 3, 1, 2, 4)
    kw_pad = jnp.pad(kw, ((0, 0), (WINDOW, 0), (0, 0), (0, 0)))
    vw_pad = jnp.pad(vw, ((0, 0), (WINDOW, 0), (0, 0), (0, 0)))
    b_idx = jnp.arange(B)[:, None, None, None]
    h_idx = jnp.arange(Hk)[None, :, None, None]
    blk_ids = jnp.arange(nsel, dtype=jnp.int32)
    offs = jnp.arange(SLC_BLOCK, dtype=jnp.int32)
    win_offs = jnp.arange(NSA_Q_BLOCK + WINDOW, dtype=jnp.int32)
    Q = NSA_Q_BLOCK

    def head_bias(dist):
        return bias_h[:, t5_bucket(dist)].reshape(Hk, G, *dist.shape)

    def block_fn(c):
        q0 = c * Q
        t = q0 + jnp.arange(Q, dtype=jnp.int32)
        qc = lax.dynamic_slice_in_dim(q, q0, Q, axis=1)
        gc = lax.dynamic_slice_in_dim(gates, q0, Q, axis=1)
        dist_c = t[:, None] - cmp_end[None, :]
        s_c = jnp.einsum('bqhgd,bnhd->bhgqn', qc, kc).astype(jnp.float32) + head_bias(dist_c)
        p_c = masked_softmax(s_c, dist_c >= 0)
        o_c = jnp.einsum('bhgqn,bnhd->bqhgd', p_c.astype(vc.dtype), vc)
        imp = p_c.sum(axis=2)
        imp = jnp.where(agg_valid, jnp.take(imp, agg_idx, axis=-1), 0.0).sum(-1)
        cur = t // SLC_BLOCK
        forced = ((blk_ids[None, :] == 0) | (blk_ids[None, :] == cur[:, None])
                  | (blk_ids[None, :] == cur[:, None] - 1))
        causal_blk = blk_ids[None, :] * SLC_BLOCK <= t[:, None]
        score = jnp.where(causal_blk, jnp.where(forced, BIG, imp), NEG)
        top_val, top_idx = lax.top_k(score, n_top)
        sel_ok = top_val > 0.5 * NEG
        k_sel = ks_blk[b_idx, h_idx, top_idx]
        v_sel = vs_blk[b_idx, h_idx, top_idx]
        key_pos = top_idx[..., None] * SLC_BLOCK + offs
        dist_s = t[None, None, :, None, None] - key_pos
        s_s = jnp.einsum('bqhgd,bhqnkd->bhgqnk', qc, k_sel).astype(jnp.float32)
        bias_s = bias_hkg[h_idx[..., None], t5_bucket(dist_s)]
        s_s = s_s + jnp.moveaxis(bias_s, -1, 2)
        mask_s = (sel_ok[..., None] & (dist_s >= 0))[:, :, None]
        p_s = masked_softmax(s_s.reshape(B, Hk, G, Q, n_top * SLC_BLOCK),
                             mask_s.reshape(B, Hk, 1, Q, n_top * SLC_BLOCK)).reshape(s_s.shape)
        o_s = jnp.einsum('bhgqnk,bhqnkd->bqhgd', p_s.astype(v_sel.dtype), v_sel)
        kwc = lax.dynamic_slice_in_dim(kw_pad, q0, Q + WINDOW, axis=1)
        vwc = lax.dynamic_slice_in_dim(vw_pad, q0, Q + WINDOW, axis=1)
        key_pos_w = q0 - WINDOW + win_offs
        dist_w = t[:, None] - key_pos_w[None, :]
        mask_w = (dist_w >= 0) & (dist_w < WINDOW) & (key_pos_w[None, :] >= 0)
        s_w = jnp.einsum('bqhgd,bkhd->bhgqk', qc, kwc).astype(jnp.float32) + head_bias(dist_w)
        p_w = masked_softmax(s_w, mask_w)
        o_w = jnp.einsum('bhgqk,bkhd->bqhgd', p_w.astype(vwc.dtype), vwc)
        return gc[..., 0:1] * o_c + gc[..., 1:2] * o_s + gc[..., 2:3] * o_w

    out = lax.map(block_fn, jnp.arange(S // Q, dtype=jnp.int32))
    return out.transpose(1, 0, 2, 3, 4, 5).reshape(B, S, NSA_HEADS * HEAD_DIM)

def conformer_conv(u, w_dw, b_dw, ln_g, ln_b):
    a, g = jnp.split(u, 2, axis=-1)
    h = a * jax.nn.sigmoid(g)
    h = lax.conv_general_dilated(h, w_dw[:, None, :], window_strides=(1,),
                                 padding=[(CONV_WIDTH - 1, 0)],
                                 dimension_numbers=('NWC', 'WIO', 'NWC'),
                                 feature_group_count=CONV_CHANNELS) + b_dw
    return jax.nn.silu(layer_norm(h, ln_g, ln_b))

def gla_chunked(q, k, v, log_a):
    B, S, H, dk = q.shape
    dv = v.shape[-1]
    C = GLA_CHUNK
    N = S // C

    def chunks(a):
        return a.astype(jnp.float32).reshape(B, N, C, H, a.shape[-1]).transpose(0, 3, 1, 2, 4)

    q, k, v, la = chunks(q), chunks(k), chunks(v), chunks(log_a)
    b = jnp.cumsum(la, axis=3)
    b_last = b[:, :, :, -1:]
    q_t = q * (dk ** -0.5) * jnp.exp(b)
    k_t = k * jnp.exp(-b)
    k_d = k * jnp.exp(b_last - b)
    causal = jnp.tril(jnp.ones((C, C), dtype=bool))
    attn = jnp.where(causal, jnp.einsum('bhncd,bhnsd->bhncs', q_t, k_t), 0.0)
    o_intra = jnp.einsum('bhncs,bhnsv->bhncv', attn, v)

    def step(state, xs):
        qn, kn, vn, dn = xs
        o = jnp.einsum('bhcd,bhdv->bhcv', qn, state)
        state = dn[..., None] * state + jnp.einsum('bhcd,bhcv->bhdv', kn, vn)
        return state, o

    xs = (jnp.moveaxis(q_t, 2, 0), jnp.moveaxis(k_d, 2, 0), jnp.moveaxis(v, 2, 0),
          jnp.moveaxis(jnp.exp(b_last[:, :, :, 0]), 2, 0))
    _, o_inter = lax.scan(step, jnp.zeros((B, H, dk, dv), jnp.float32), xs)
    o = o_intra + jnp.moveaxis(o_inter, 0, 2)
    return o.transpose(0, 2, 3, 1, 4).reshape(B, S, H, dv)

def first_inputs(seed: int = 0) -> dict:
    key = jax.random.key(seed)
    ks = jax.random.split(key, 32)
    L = DEPTH

    def nrm(k, shape, scale):
        return jax.random.normal(k, shape, jnp.float32) * scale

    def gain(k, shape):
        return 1.0 + 0.05 * jax.random.normal(k, shape, jnp.float32)

    return {
        "x": nrm(ks[0], (BATCH, SEQ, D_MODEL), 1.0),
        "p": nrm(ks[1], (DEPTH, BATCH, SEQ, PLE_DIM), 1.0),
        "rel_bias": nrm(ks[2], (REL_BUCKETS, NSA_HEADS), 0.5),
        "mix_norm_g": gain(ks[3], (L, D_MODEL)),
        "w_in": nrm(ks[4], (L, D_MODEL, D_IN), D_MODEL ** -0.5),
        "w_out": nrm(ks[5], (L, D_MIX, D_MODEL), D_MIX ** -0.5),
        "cmp_pos_k": nrm(ks[6], (L, CMP_BLOCK, HEAD_DIM), 0.1),
        "cmp_w1_k": nrm(ks[7], (L, CMP_BLOCK * HEAD_DIM, CMP_HIDDEN), (CMP_BLOCK * HEAD_DIM) ** -0.5),
        "cmp_b1_k": nrm(ks[8], (L, CMP_HIDDEN), 0.02),
        "cmp_w2_k": nrm(ks[9], (L, CMP_HIDDEN, HEAD_DIM), CMP_HIDDEN ** -0.5),
        "cmp_pos_v": nrm(ks[10], (L, CMP_BLOCK, HEAD_DIM), 0.1),
        "cmp_w1_v": nrm(ks[11], (L, CMP_BLOCK * HEAD_DIM, CMP_HIDDEN), (CMP_BLOCK * HEAD_DIM) ** -0.5),
        "cmp_b1_v": nrm(ks[12], (L, CMP_HIDDEN), 0.02),
        "cmp_w2_v": nrm(ks[13], (L, CMP_HIDDEN, HEAD_DIM), CMP_HIDDEN ** -0.5),
        "conv_w": nrm(ks[14], (L, CONV_WIDTH, CONV_CHANNELS), CONV_WIDTH ** -0.5),
        "conv_b": nrm(ks[15], (L, CONV_CHANNELS), 0.02),
        "conv_ln_g": gain(ks[16], (L, CONV_CHANNELS)),
        "conv_ln_b": nrm(ks[17], (L, CONV_CHANNELS), 0.02),
        "gla_w_alpha": nrm(ks[18], (L, GLA_GATE_RANK, GLA_KEY_DIM), GLA_GATE_RANK ** -0.5),
        "gla_b_alpha": nrm(ks[19], (L, GLA_KEY_DIM), 0.02),
        "gla_norm_g": gain(ks[20], (L, GLA_VALUE_DIM)),
        "ffn_norm_g": gain(ks[21], (L, D_MODEL)),
        "ffn_w_gate": nrm(ks[22], (L, D_MODEL, D_FF), D_MODEL ** -0.5),
        "ffn_w_up": nrm(ks[23], (L, D_MODEL, D_FF), D_MODEL ** -0.5),
        "ffn_w_down": nrm(ks[24], (L, D_FF, D_MODEL), D_FF ** -0.5),
        "ple_norm_g": gain(ks[25], (L, D_MODEL)),
        "ple_w_gate": nrm(ks[26], (L, D_MODEL, D_MODEL), D_MODEL ** -0.5),
        "ple_w_proj": nrm(ks[27], (L, PLE_DIM, D_MODEL), PLE_DIM ** -0.5),
        "final_norm_g": gain(ks[28], (D_MODEL,)),
    }

def first_block(x, p, rel_bias, mix_norm_g, w_in, w_out,
              cmp_pos_k, cmp_w1_k, cmp_b1_k, cmp_w2_k,
              cmp_pos_v, cmp_w1_v, cmp_b1_v, cmp_w2_v,
              conv_w, conv_b, conv_ln_g, conv_ln_b,
              gla_w_alpha, gla_b_alpha, gla_norm_g,
              ffn_norm_g, ffn_w_gate, ffn_w_up, ffn_w_down,
              ple_norm_g, ple_w_gate, ple_w_proj, final_norm_g):
    B, S, _ = x.shape
    split_at = np.cumsum(IN_SPLITS)[:-1].tolist()

    def heads(a, n):
        return a.reshape(B, S, n, -1)

    for i in range(DEPTH):
        h = rms_norm(x, mix_norm_g[i])
        z = h @ w_in[i]
        (nq, kc, vc, ks_, vs_, kw, vw, ng, cu, gq, gk, gv, ga, gr) = jnp.split(z, split_at, axis=-1)
        kc = compress_kv(heads(kc, NSA_KV_HEADS), cmp_pos_k[i], cmp_w1_k[i], cmp_b1_k[i], cmp_w2_k[i])
        vc = compress_kv(heads(vc, NSA_KV_HEADS), cmp_pos_v[i], cmp_w1_v[i], cmp_b1_v[i], cmp_w2_v[i])
        y_nsa = nsa_attention(heads(nq, NSA_HEADS), kc, vc,
                              heads(ks_, NSA_KV_HEADS), heads(vs_, NSA_KV_HEADS),
                              heads(kw, NSA_KV_HEADS), heads(vw, NSA_KV_HEADS),
                              jax.nn.sigmoid(ng).reshape(B, S, NSA_HEADS, N_BRANCH), rel_bias)
        y_conv = conformer_conv(cu, conv_w[i], conv_b[i], conv_ln_g[i], conv_ln_b[i])
        log_a = jax.nn.log_sigmoid((ga @ gla_w_alpha[i] + gla_b_alpha[i]).astype(jnp.float32)) / GLA_TAU
        o = gla_chunked(heads(gq, GLA_HEADS), heads(gk, GLA_HEADS), heads(gv, GLA_HEADS),
                        heads(log_a, GLA_HEADS))
        o = rms_norm(o, gla_norm_g[i].reshape(GLA_HEADS, -1)).reshape(B, S, GLA_VALUE_DIM)
        y_gla = (o * jax.nn.silu(gr)).astype(x.dtype)
        x = x + jnp.concatenate([y_nsa, y_conv, y_gla], axis=-1) @ w_out[i]
        h = rms_norm(x, ffn_norm_g[i])
        x = x + (jax.nn.silu(h @ ffn_w_gate[i]) * (h @ ffn_w_up[i])) @ ffn_w_down[i]
        gate = jax.nn.sigmoid(rms_norm(x, ple_norm_g[i]) @ ple_w_gate[i])
        x = x + (p[i] @ ple_w_proj[i]) * gate
    return rms_norm(x, final_norm_g)


CTX_LEN = 256
GRID_W = 64
FOURIER_W = 512
FOURIER_GROUPS = 8
RWKV_W = D_MODEL - FOURIER_W
HEAD = 64
N_HEADS = RWKV_W // HEAD
N_DIR = 2
DECAY_RANK = 64
ICLR_RANK = 64
GATE_RANK = 128
D_FF_2 = 2816
RWKV_PROJ_W = 3 * RWKV_W + N_DIR * DECAY_RANK + N_DIR * ICLR_RANK + GATE_RANK
PROJ_W = FOURIER_W + RWKV_PROJ_W
NORM_EPS = 1e-6
GN_EPS = 64e-5
KK_EPS = 1e-12


def rms_norm_2(x, g):
    xf = x.astype(jnp.float32)
    y = xf * lax.rsqrt(jnp.mean(xf * xf, axis=-1, keepdims=True) + NORM_EPS)
    return (y * g.astype(jnp.float32)).astype(x.dtype)

def modulate(h, shift, scale):
    return h * (1 + scale) + shift

def conv1d_centred(u, w):
    up = jnp.pad(u, ((0, 0), (1, 1), (0, 0)))
    return up[:, :-2] * w[0] + up[:, 1:-1] * w[1] + up[:, 2:] * w[2]

def conv2d_grid(u, w, rows):
    b, t, ch = u.shape
    g = u.reshape(b, rows, GRID_W, ch)
    y = lax.conv_general_dilated(g, w[:, :, None, :].astype(u.dtype), (1, 1), "SAME",
                                 dimension_numbers=("NHWC", "HWIO", "NHWC"),
                                 feature_group_count=ch)
    return y.reshape(b, t, ch)

def fourier_mix(u, g):
    b, t, _ = u.shape
    uf = u.astype(jnp.float32).reshape(b, t, FOURIER_GROUPS, FOURIER_W // FOURIER_GROUPS)
    y = jnp.fft.fft2(uf, axes=(1, 3), norm="ortho").real
    return rms_norm_2(y.reshape(b, t, FOURIER_W), g).astype(u.dtype)

def rwkv_inputs(u, conv_w, w0, w2, a0, a2, k_k, k_a):
    b, t, _ = u.shape
    rkv = conv1d_centred(u[..., :3 * RWKV_W], conv_w)
    r, k, v = jnp.split(rkv, 3, axis=-1)
    o = 3 * RWKV_W
    wd = u[..., o:o + N_DIR * DECAY_RANK].reshape(b, t, N_DIR, DECAY_RANK)
    o += N_DIR * DECAY_RANK
    ad = u[..., o:o + N_DIR * ICLR_RANK].reshape(b, t, N_DIR, ICLR_RANK)
    o += N_DIR * ICLR_RANK
    gd = u[..., o:]
    w_lora = (w0 + jnp.einsum("btdr,drc->btdc", jnp.tanh(wd), w2)).astype(jnp.float32)
    decay = jnp.exp(-jnp.exp(-jax.nn.softplus(-w_lora) - 0.5))
    a = jax.nn.sigmoid((a0 + jnp.einsum("btdr,drc->btdc", ad, a2)).astype(jnp.float32))
    kk = (k * k_k).astype(jnp.float32).reshape(b, t, N_HEADS, HEAD)
    kk = kk * lax.rsqrt(jnp.sum(kk * kk, axis=-1, keepdims=True) + KK_EPS)
    kk = kk.reshape(b, t, RWKV_W)
    kd = k.astype(jnp.float32)[:, :, None] * (1 + (a - 1) * k_a)
    return r, kd, v, kk, a, decay, gd

def _heads_time_major(x2):
    d, b, t, _ = x2.shape
    return x2.astype(jnp.float32).reshape(d, b, t, N_HEADS, HEAD).transpose(2, 0, 1, 3, 4)

def shared_dirs(x):
    return _heads_time_major(jnp.stack([x, jnp.flip(x, axis=1)], axis=0))

def per_dir(x):
    return _heads_time_major(jnp.stack([x[:, :, 0], jnp.flip(x[:, :, 1], axis=1)], axis=0))

def merge_dirs(y):
    y = y.transpose(1, 2, 0, 3, 4)
    return y[0] + jnp.flip(y[1], axis=1)

def rwkv_scan(prep, state0, readout):
    r, kd, v, kk, a, decay, _ = prep
    xs = (shared_dirs(r), per_dir(kd), shared_dirs(v), shared_dirs(kk), per_dir(a), per_dir(decay))

    def step(s, inp):
        r_t, k_t, v_t, kk_t, a_t, w_t = inp
        sa = jnp.einsum("dbhij,dbhj->dbhi", s, kk_t)
        s = (s * w_t[..., None, :] - sa[..., :, None] * (kk_t * a_t)[..., None, :]
             + v_t[..., :, None] * k_t[..., None, :])
        y = jnp.einsum("dbhij,dbhj->dbhi", s, r_t) if readout else None
        return s, y

    return lax.scan(step, state0, xs)

def rwkv_output(y, prep, g2, r_k, gn_g, gn_b):
    r, kd, v, _, _, _, gd = prep
    b, t = r.shape[:2]
    mu = jnp.mean(y, axis=-1, keepdims=True)
    var = jnp.mean(jnp.square(y - mu), axis=-1, keepdims=True)
    yn = ((y - mu) * lax.rsqrt(var + GN_EPS)).reshape(b, t, RWKV_W)
    yn = yn * gn_g.astype(jnp.float32) + gn_b.astype(jnp.float32)
    rh = r.astype(jnp.float32).reshape(b, t, N_HEADS, HEAD)
    vh = v.astype(jnp.float32).reshape(b, t, N_HEADS, HEAD)
    kdh = kd.reshape(b, t, N_DIR, N_HEADS, HEAD)
    bonus = jnp.einsum("bthn,btdhn,hn->bth", rh, kdh, r_k.astype(jnp.float32))[..., None] * vh
    gate = jax.nn.sigmoid(gd.astype(jnp.float32)) @ g2.astype(jnp.float32)
    return (yn + bonus.reshape(b, t, RWKV_W)) * gate

def token_mixer(h, hc, w_in, conv_w, w0, w2, a0, a2, g2, k_k, k_a, r_k, gn_g, gn_b,
                f_g, w_out, ctx_out):
    u = h @ w_in
    uc = hc @ (w_in if ctx_out else w_in[:, FOURIER_W:])
    uc_r = uc[..., FOURIER_W:] if ctx_out else uc
    prep_l = rwkv_inputs(u[..., FOURIER_W:], conv_w, w0, w2, a0, a2, k_k, k_a)
    prep_c = rwkv_inputs(uc_r, conv_w, w0, w2, a0, a2, k_k, k_a)
    state0 = jnp.zeros((N_DIR, hc.shape[0], N_HEADS, HEAD, HEAD), jnp.float32)
    state_c, y_c = rwkv_scan(prep_c, state0, ctx_out)
    _, y_l = rwkv_scan(prep_l, state_c, True)
    rw_l = rwkv_output(merge_dirs(y_l), prep_l, g2, r_k, gn_g, gn_b).astype(h.dtype)
    out = jnp.concatenate([fourier_mix(u[..., :FOURIER_W], f_g).astype(h.dtype), rw_l], axis=-1) @ w_out
    out_c = None
    if ctx_out:
        rw_c = rwkv_output(merge_dirs(y_c), prep_c, g2, r_k, gn_g, gn_b).astype(hc.dtype)
        out_c = jnp.concatenate([fourier_mix(uc[..., :FOURIER_W], f_g).astype(hc.dtype), rw_c], axis=-1) @ w_out
    return out, out_c

def conv_ffn(h, w_up, conv_w, conv_b, w_down, rows):
    u = h @ w_up
    if rows is None:
        u = conv1d_centred(u, conv_w[1]) + conv_b
    else:
        u = conv2d_grid(u, conv_w, rows) + conv_b
    gate, val = jnp.split(u, 2, axis=-1)
    return (jax.nn.silu(gate) * val) @ w_down

def second_inputs(seed: int = 0) -> dict:
    key = jax.random.key(seed)
    ks = jax.random.split(key, 27)
    L, D, C, F2 = DEPTH, D_MODEL, RWKV_W, 2 * D_FF_2

    def nrm(i, shape, s=1.0):
        return s * jax.random.normal(ks[i], shape, jnp.float32)

    def near_one(i, shape):
        return 1.0 + nrm(i, shape, 0.05)

    centre3 = jnp.zeros((3,), jnp.float32).at[1].set(1.0)
    centre33 = jnp.zeros((3, 3), jnp.float32).at[1, 1].set(1.0)
    return {
        "x": nrm(0, (BATCH, SEQ, D)),
        "c": nrm(1, (BATCH, D)),
        "ctx": nrm(2, (BATCH, CTX_LEN, D)),
        "c_ctx": nrm(3, (D,)),
        "ada_w": nrm(4, (L, D, 6 * D), 0.5 * D ** -0.5),
        "ada_b": nrm(5, (L, 6 * D), 0.02),
        "norm1_g": near_one(6, (L, D)),
        "norm2_g": near_one(7, (L, D)),
        "w_in": nrm(8, (L, D, PROJ_W), D ** -0.5),
        "rwkv_conv_w": centre3[None, :, None] + nrm(9, (L, 3, 3 * C), 0.1),
        "decay_w0": -1.0 + nrm(10, (L, N_DIR, C), 1.5),
        "decay_w2": nrm(11, (L, N_DIR, DECAY_RANK, C), 0.1 * DECAY_RANK ** -0.5),
        "iclr_a0": nrm(12, (L, N_DIR, C), 0.5),
        "iclr_a2": nrm(13, (L, N_DIR, ICLR_RANK, C), 0.1 * ICLR_RANK ** -0.5),
        "gate_g2": nrm(14, (L, GATE_RANK, C), GATE_RANK ** -0.5),
        "k_k": 0.85 + nrm(15, (L, C), 0.05),
        "k_a": near_one(16, (L, C)),
        "r_k": nrm(17, (L, N_HEADS, HEAD), 0.1),
        "gn_g": near_one(18, (L, C)),
        "gn_b": nrm(19, (L, C), 0.02),
        "fourier_g": near_one(20, (L, FOURIER_W)),
        "w_out": nrm(21, (L, D, D), D ** -0.5),
        "ffn_w_up": nrm(22, (L, D, F2), D ** -0.5),
        "ffn_conv_w": centre33[None, :, :, None] + nrm(23, (L, 3, 3, F2), 0.1),
        "ffn_conv_b": nrm(24, (L, F2), 0.02),
        "ffn_w_down": nrm(25, (L, D_FF_2, D), D_FF_2 ** -0.5),
        "final_g": near_one(26, (D,)),
    }

def second_block(x, c, ctx, c_ctx, ada_w, ada_b, norm1_g, norm2_g, w_in, rwkv_conv_w,
              decay_w0, decay_w2, iclr_a0, iclr_a2, gate_g2, k_k, k_a, r_k, gn_g, gn_b,
              fourier_g, w_out, ffn_w_up, ffn_conv_w, ffn_conv_b, ffn_w_down, final_g):
    rows = x.shape[1] // GRID_W
    for l in range(DEPTH):
        last = l == DEPTH - 1
        mod_x = jax.nn.silu(c) @ ada_w[l] + ada_b[l]
        mod_c = jax.nn.silu(c_ctx) @ ada_w[l] + ada_b[l]
        sh1, sc1, g1, sh2, sc2, g2 = [m[:, None, :] for m in jnp.split(mod_x, 6, axis=-1)]
        sh1c, sc1c, g1c, sh2c, sc2c, g2c = jnp.split(mod_c, 6, axis=-1)

        h = modulate(rms_norm_2(x, norm1_g[l]), sh1, sc1)
        hc = modulate(rms_norm_2(ctx, norm1_g[l]), sh1c, sc1c)
        y, yc = token_mixer(h, hc, w_in[l], rwkv_conv_w[l], decay_w0[l], decay_w2[l],
                            iclr_a0[l], iclr_a2[l], gate_g2[l], k_k[l], k_a[l], r_k[l],
                            gn_g[l], gn_b[l], fourier_g[l], w_out[l], not last)
        x = x + g1 * y
        h = modulate(rms_norm_2(x, norm2_g[l]), sh2, sc2)
        x = x + g2 * conv_ffn(h, ffn_w_up[l], ffn_conv_w[l], ffn_conv_b[l], ffn_w_down[l], rows)
        if not last:
            ctx = ctx + g1c * yc
            hc = modulate(rms_norm_2(ctx, norm2_g[l]), sh2c, sc2c)
            ctx = ctx + g2c * conv_ffn(hc, ffn_w_up[l], ffn_conv_w[l], ffn_conv_b[l],
                                       ffn_w_down[l], None)
    return rms_norm_2(x, final_g)


def setup_inputs(seed=0):
    out = dict(first_inputs(seed))
    for name, value in second_inputs(seed + 1).items():
        if name != "x":
            out[name + "_2"] = value
    return out


def reference(
    x, p, rel_bias, mix_norm_g, w_in, w_out, cmp_pos_k, cmp_w1_k, cmp_b1_k, cmp_w2_k, cmp_pos_v,
    cmp_w1_v, cmp_b1_v, cmp_w2_v, conv_w, conv_b, conv_ln_g, conv_ln_b, gla_w_alpha,
    gla_b_alpha, gla_norm_g, ffn_norm_g, ffn_w_gate, ffn_w_up, ffn_w_down, ple_norm_g,
    ple_w_gate, ple_w_proj, final_norm_g, c_2, ctx_2, c_ctx_2, ada_w_2, ada_b_2, norm1_g_2,
    norm2_g_2, w_in_2, rwkv_conv_w_2, decay_w0_2, decay_w2_2, iclr_a0_2, iclr_a2_2, gate_g2_2,
    k_k_2, k_a_2, r_k_2, gn_g_2, gn_b_2, fourier_g_2, w_out_2, ffn_w_up_2, ffn_conv_w_2,
    ffn_conv_b_2, ffn_w_down_2, final_g_2,
):
    x = first_block(
        x, p, rel_bias, mix_norm_g, w_in, w_out, cmp_pos_k, cmp_w1_k, cmp_b1_k, cmp_w2_k,
        cmp_pos_v, cmp_w1_v, cmp_b1_v, cmp_w2_v, conv_w, conv_b, conv_ln_g, conv_ln_b,
        gla_w_alpha, gla_b_alpha, gla_norm_g, ffn_norm_g, ffn_w_gate, ffn_w_up, ffn_w_down,
        ple_norm_g, ple_w_gate, ple_w_proj, final_norm_g,
    )
    return second_block(
        x, c_2, ctx_2, c_ctx_2, ada_w_2, ada_b_2, norm1_g_2, norm2_g_2, w_in_2, rwkv_conv_w_2,
        decay_w0_2, decay_w2_2, iclr_a0_2, iclr_a2_2, gate_g2_2, k_k_2, k_a_2, r_k_2, gn_g_2,
        gn_b_2, fourier_g_2, w_out_2, ffn_w_up_2, ffn_conv_w_2, ffn_conv_b_2, ffn_w_down_2,
        final_g_2,
    )


_drawn_inputs = setup_inputs


def setup_inputs(seed=0):
    import zlib

    import numpy as np

    out = dict(_drawn_inputs(seed))
    spreads = {}
    factors = {'cmp_pos_k': 24.436,
     'cmp_b1_k': 64.0,
     'cmp_pos_v': 3.146,
     'cmp_b1_v': 8.0,
     'conv_b': 5.1,
     'conv_ln_g': 3.04,
     'conv_ln_b': 8.0,
     'gla_b_alpha': 8.0,
     'gla_norm_g': 3.86,
     'ple_norm_g': 6.85,
     'ctx_2': 3.646,
     'c_ctx_2': 5.158,
     'norm1_g_2': 3.135,
     'norm2_g_2': 15.519,
     'decay_w2_2': 46.031,
     'iclr_a2_2': 7.875,
     'k_k_2': 200.0,
     'k_a_2': 5.39,
     'gn_g_2': 64.0,
     'gn_b_2': 200.0,
     'fourier_g_2': 40.168,
     'ffn_conv_b_2': 38.456}
    for name, (base, spread) in spreads.items():
        noise = np.random.default_rng([zlib.crc32(name.encode()), seed]).standard_normal(out[name].shape)
        drawn = base * np.exp(spread * noise) if base else spread * noise
        out[name] = jnp.asarray(drawn.astype(out[name].dtype))
    for name, factor in factors.items():
        out[name] = (out[name] * factor).astype(out[name].dtype)
    return out
```

```python
import math
from contextlib import ExitStack, contextmanager

import numpy as np

import concourse.bass as bass
from concourse import mybir

F32 = mybir.dt.float32
ALU = mybir.AluOpType
ACT = mybir.ActivationFunctionType
AX = mybir.AxisListType

P = 128
D = 1024
KT = D // P
S = 512
CTX = 256
T2 = CTX + S
EPS = 1e-6
NEG = -1e30
NPAIR = 4
QT = S // P
NCMP = S // 16 - 1
CONV_W = 31
FT = 2816 // P
C = 64
NCH = S // C
TOEP = 639

STREAM = [("in1", 17), ("out1", 8), ("ffn1", 2 * FT), ("down1", 24), ("pleproj", 2), ("ple", 8),
          ("ada", 48), ("in2", 19), ("out2", 8), ("ffn2", 2 * FT), ("down2", 24)]
UNIT0, NUNITS = {}, 0
for _n, _c in STREAM:
    UNIT0[_n] = NUNITS
    NUNITS += _c
NUNITS_PAD = -(-NUNITS // 4) * 4

COLS = [("mix_g", 8), ("ffn_g", 8), ("ple_g", 8), ("fin_g", 8), ("b1k", 2), ("b1v", 2),
        ("posk", 16), ("posv", 16), ("conv_b", 2), ("ln_g", 2), ("ln_b", 2), ("conv_w", 2 * CONV_W),
        ("gla_b", 1), ("gla_g", 2), ("n1_g", 8), ("n2_g", 8), ("fin2_g", 8), ("ada_b", 48),
        ("c", 16), ("rconv", 36), ("w0", 8), ("a0", 8), ("k_k", 4), ("k_a", 4), ("r_k", 4),
        ("gn_g", 4), ("gn_b", 4), ("fc_w", 44 * 9), ("fc_b", 44), ("fo_g", 4)]
COL0, NCOLS = {}, 0
for _n, _c in COLS:
    COL0[_n] = NCOLS
    NCOLS += _c


LOADS = {"start": 6, "compress": 4, "gla": 3, "fourier": 2, "low_rank": 2, "rwkv": 4}


class Steps:

    def __init__(self, eng, sem):
        self.eng, self.sem, self.total, self.index, self.per = eng, sem, 0, None, 0

    def did(self, ins):
        ins.then_inc(self.sem, 1)
        self.total += 1

    def wait(self, engine=None):
        value = self.total if self.index is None else self.index * self.per + self.total
        (engine or self.eng).wait_ge(self.sem, value)

    def did_but(self, n, make):
        value = self.total - n
        self.eng.wait_ge(self.sem, value if self.index is None else self.index * self.per + value)
        self.did(make())

    def link(self, ins):
        self.did(ins)
        self.wait()

    @contextmanager
    def loop(self, n, per):
        with self.eng.Fori(0, n) as i:
            start, self.index, self.per = self.total, i, per
            yield i
            assert self.total - start == per, (self.total - start, per)
        self.index, self.total = None, start + n * per


class Events:

    def __init__(self, sem, tag, orders, alone=()):
        self.sem_of, self.first, self.given = {}, {}, {}
        for engine, order in orders.items():
            n = 0
            for name, count in order:
                self.sem_of[name], self.first[name] = sem(f"{tag}_{engine}"), n
                self.given[name] = [engine, 0, count]
                n += count
        for name in alone:
            self.sem_of[name], self.first[name] = sem(f"{tag}_{name}"), 0
        self.totals = {engine: 0 for engine in orders}

    def of(self, name):
        if name in self.given:
            g = self.given[name]
            assert self.totals[g[0]] == self.first[name] + g[1] and g[1] < g[2], name
            self.totals[g[0]] += 1
            g[1] += 1
        return self.sem_of[name]

    def __call__(self, name, k):
        return self.sem_of[name], self.first[name] + k


def view(ap, offset, dims):
    return bass.AP(ap.tensor, ap.offset + offset, [list(ap.ap[0])] + [list(d) for d in dims])


def build(nc, A, out, upto=99, dump=None, nunits=NUNITS_PAD):
    with ExitStack() as ctx:
        sem_of = {}

        def sem(name):
            if name not in sem_of:
                sem_of[name] = ctx.enter_context(nc.semaphore(name))
            return sem_of[name]

        SB_COLS = 53000
        mem = ctx.enter_context(nc.sbuf_tensor("mem", [P, SB_COLS], F32))
        psum = ctx.enter_context(nc.psum_tensor("psum", [P, 8, 512], F32))
        ps = [psum[:, b, :] for b in range(8)]
        bias_dram = nc.dram_tensor("bias_scratch", [8, TOEP + 1], F32, kind="Internal").ap()
        x_dram = nc.dram_tensor("x_scratch", [P, KT * S], F32, kind="Internal").ap()
        bias_tiles = nc.dram_tensor("bias_tiles", [8, P, S], F32, kind="Internal").ap()

        class Region:
            def __init__(self, start, end):
                self.at, self.end = start, end

            def take(self, *dims):
                n = int(np.prod(dims))
                assert self.at + n <= self.end, (self.at, n, self.end)
                ap = mem[:, self.at:self.at + n]
                self.at += n
                if len(dims) == 1:
                    return ap
                names = "abcd"[:len(dims)]
                return ap.rearrange(f"p ({' '.join(names)}) -> p {' '.join(names)}",
                                    **dict(zip(names, dims)))

            def remainder(self):
                return Region(self.at, self.end)

        base = Region(0, SB_COLS)
        ring = base.take(4, 8, P)
        ident = base.take(P)
        ones = base.take(P)
        ones64 = base.take(P)
        cols = base.take(NCOLS)
        xT = base.take(KT, S)
        hT = base.take(KT, T2)
        sqr = base.take(KT, S)
        mod = base.take(48, 2)
        gains = base.take(3, KT)
        omka = base.take(4)
        rstd = base.take(512)
        rstd2 = base.take(512)

        def col(name, i=0, n=1):
            return cols[:, COL0[name] + i:COL0[name] + i + n]

        r1 = base.remainder()
        assert base.at < 21600, base.at
        zT = r1.take(17, S)
        ZKS, ZKW, ZKC, ZVC, ZGQ, ZGK, ZGA, ZQ, ZCU, ZGR = 0, 1, 2, 3, 4, 5, 6, 7, 11, 15
        znat = r1.take(QT, 512)
        gates = r1.take(QT, 8, 3)
        mixT = r1.take(KT, S)
        mixT_nsa, mixT_conv, mixT_gla = mixT[:, 0:4], mixT[:, 4:6], mixT[:, 6:8]
        kcmpT = r1.take(32)
        vcmp = r1.take(P)
        wn = r1.take(8, 536)
        r_cmp = r1.remainder()
        cw1 = [r_cmp.take(16, 256), r_cmp.take(16, 256)]
        cw2 = [r_cmp.take(2, 64), r_cmp.take(2, 64)]
        swapped = r_cmp.take(2, S)
        blocks = [r_cmp.take(16, 2, NCMP), r_cmp.take(16, 2, NCMP)]
        hid = [r_cmp.take(2, 2 * NCMP), r_cmp.take(2, 2 * NCMP)]
        r_bias = Region(mixT.offset, mixT.offset + KT * S)
        onehot = r_bias.take(640)
        negmask = r_bias.take(640)
        relb = r_bias.take(8)
        bvec = r_bias.take(640)
        assert r_cmp.at <= SB_COLS
        r_att = Region(wn.offset, SB_COLS)
        qs = r_att.take(S)
        bias = r_att.take(2, S)
        sc = [[r_att.take(64), r_att.take(512), r_att.take(512)] for _ in range(2)]
        pt = [[r_att.take(P), r_att.take(512), r_att.take(512)] for _ in range(2)]
        stat = [r_att.take(16) for _ in range(2)]
        r_cv = Region(wn.offset, SB_COLS)
        cvh = r_cv.take(2, 544)
        cva = r_cv.take(2, S)
        cvx = r_cv.take(2, S)
        cvt = r_cv.take(2, S)
        r_gl = r_cv.remainder()
        gl_wa = r_gl.take(P)
        gl_t = [r_gl.take(S) for _ in range(3)]
        gl_reset = r_gl.take(S)
        gl_cum = r_gl.take(S)
        gl_q = r_gl.take(S)
        gl_k = r_gl.take(S)
        gl_dn = r_gl.take(NCH)
        gl_kn = r_gl.take(QT, P)
        gl_mask = r_gl.take(C)
        gl_at4 = r_gl.take(4, QT, C)
        gl_st = r_gl.take(C)
        gl_o = r_gl.take(2, S)

        units = A["units"]
        units_done = sem("units_done")
        landed = [sem(f"landed{j}") for j in range(4)]
        stage_done = sem("stage_done")
        loaded = {}
        now = [0]

        block = ctx.enter_context(nc.Block())

        stages = []

        def stage(f):
            if len(stages) < upto:
                stages.append(f())
            return f

        def run(eng, key, steps):
            for n, st in enumerate(stages):
                now[0] = n
                if n:
                    eng.wait_ge(stage_done, 4 * n)
                if key in st:
                    st[key](eng, steps)
                eng.drain().then_inc(stage_done, 1)

        def passed(eng, name):
            eng.sem_inc(sem("passed_" + name), 1)

        def load(eng, name, dst, src):
            eng.dma_start(dst, src).then_inc(sem("ld_" + name), 16)
            loaded[name] = True

        def arrived(eng, *names):
            for name in names:
                eng.wait_ge(sem("ld_" + name), 16 * LOADS.get(name, 1))

        def per_unit(pe, u0, count, use, body=4):
            def one(j, i):
                slot = (u0 + j) % 4
                pe.wait_ge(landed[slot], 16 * ((u0 + j) // 4 + 1 + i * (body // 4)))
                use(slot, j, i).then_inc(units_done, 1)
            looped = 0
            if count // body > 1:
                looped = count // body * body
                with pe.Fori(0, count // body) as i:
                    for j in range(body):
                        one(j, i)
            for j in range(looped, count):
                one(j, 0)

        def product(pe, slot, rhs, dst, ks=range(8)):
            for k in ks:
                last = pe.matmul(dst, ring[:, slot, k, :], rhs(k), start=(k == ks[0]), stop=(k == ks[-1]))
            return last

        def linear_pe(pe, u0, count, rhs, bank_free, banks=4):
            def use(slot, j, i):
                pe.wait_ge(bank_free, 4 * i + j + 1)
                return product(pe, slot, rhs, ps[j % banks])
            per_unit(pe, u0, count, use)

        norms, residuals = [0], [0]

        def norm(src, dst, g, n=S, shift=None):
            squared, summed, varied, rooted, scaled = (sem("norm_" + x) for x in
                                                       ("squared", "summed", "varied", "rooted", "scaled"))
            r = norms[0]
            norms[0] += 1

            def act(eng, steps):
                for k in range(KT):
                    eng.activation(sqr[:, k, 0:n], src(k), ACT.Square).then_inc(squared, 1)
                eng.wait_ge(varied, r + 1)
                eng.activation(rstd2[:, 0:n], rstd[:, 0:n], ACT.Sqrt).then_inc(rooted, 1)
                if shift is not None:
                    for k in range(KT):
                        eng.wait_ge(scaled, KT * r + k + 1)
                        eng.activation(dst(k), dst(k), ACT.Identity, bias=shift(k))

            def pe(eng, steps):
                for k in range(KT):
                    eng.wait_ge(squared, KT * r + k + 1)
                    last = eng.matmul(ps[0][:, 0:n], ones, sqr[:, k, 0:n], start=(k == 0), stop=(k == KT - 1))
                last.then_inc(summed, 1)

            def dve(eng, steps):
                eng.wait_ge(summed, r + 1)
                eng.tensor_scalar(rstd[:, 0:n], ps[0][:, 0:n], 1.0 / D, EPS, ALU.mult,
                                  ALU.add).then_inc(varied, 1)
                eng.wait_ge(rooted, r + 1)
                steps.link(eng.reciprocal(rstd[:, 0:n], rstd2[:, 0:n]))
                for k in range(KT):
                    eng.scalar_tensor_tensor(dst(k), src(k), g(k), rstd[:, 0:n], ALU.mult,
                                             ALU.mult).then_inc(scaled, 1)

            return dict(act=act, pe=pe, dve=dve)

        @stage
        def start():
            biased, bias_put = sem("biased"), sem("bias_put")

            def act(eng, steps):
                load(eng, "start", mem[:, ident.offset:ident.offset + 3 * P], A["consts"])
                load(eng, "start", xT, A["xT"])
                load(eng, "start", cols, A["cols"])
                load(eng, "start", onehot[0:32, :], A["onehot"])
                load(eng, "start", relb[0:32, :], A["rel_bias"])
                load(eng, "start", negmask[0:8, :], A["negmask"])
                load(eng, "wn", wn, A["wn"])
                for n in range(2):
                    load(eng, "compress", cw1[n], A["cw1"][n])
                    load(eng, "compress", cw2[n], A["cw2"][n])
                eng.wait_ge(bias_put, 1)
                load(eng, "bias_dram", bias_dram, bvec[0:8, :])
                arrived(eng, "bias_dram")
                load(eng, "bias_tiles", bias_tiles,
                     bass.AP(bias_dram.tensor, bias_dram.offset + 127, [[TOEP + 1, 8], [-1, P], [1, S]]))

            def pe(eng, steps):
                arrived(eng, "start")
                for n in range(2):
                    last = eng.matmul(ps[1 + n][0:8, 0:320], relb[0:32, :], onehot[0:32, 320 * n:320 * n + 320],
                                      start=True, stop=True)
                last.then_inc(biased, 1)

            def dve(eng, steps):
                arrived(eng, "start")
                eng.wait_ge(biased, 1)
                for n in range(2):
                    steps.did(eng.tensor_tensor(bvec[0:8, 320 * n:320 * n + 320], ps[1 + n][0:8, 0:320],
                                                negmask[0:8, 320 * n:320 * n + 320], ALU.add))
                steps.wait()
                eng.sem_inc(bias_put, 1)
                arrived(eng, "start")

            return dict(act=act, pe=pe, dve=dve)

        @stage
        def norm1():
            return norm(lambda k: xT[:, k, :], lambda k: hT[:, k, 0:S], lambda k: col("mix_g", k))

        @stage
        def project1():
            free, nat = sem("in1_free"), sem("in1_nat")
            nat_copied, gates_read = sem("in1_nat_copied"), sem("in1_gates_read")
            u0 = UNIT0["in1"]

            def pe(eng, steps):
                linear_pe(eng, u0, 17, lambda k: hT[:, k, 0:S], free)
                arrived(eng, "wn")
                for t in range(QT):
                    if t >= 2:
                        eng.wait_ge(nat_copied, t - 1)
                        eng.wait_ge(gates_read, t - 1)
                    for k in range(8):
                        eng.matmul(ps[4 + 2 * (t % 2)], hT[:, k, t * P:(t + 1) * P], wn[:, k, 0:512],
                                   start=(k == 0), stop=(k == 7))
                    for k in range(8):
                        last = eng.matmul(ps[5 + 2 * (t % 2)][:, 0:24], hT[:, k, t * P:(t + 1) * P],
                                          wn[:, k, 512:536], start=(k == 0), stop=(k == 7))
                    last.then_inc(nat, 1)

            def act(eng, steps):
                eng.sem_inc(free, 4)
                with eng.Fori(0, 4) as i:
                    for j in range(4):
                        eng.wait_ge(units_done, u0 + 1 + j + 4 * i)
                        eng.copy(zT[:, 4 * i + j, :], ps[j]).then_inc(free, 1)
                eng.wait_ge(units_done, u0 + 17)
                eng.copy(zT[:, 16, :], ps[0])
                for t in range(QT):
                    eng.wait_ge(nat, t + 1)
                    eng.activation(gates[:, t].rearrange("p h b -> p (h b)"), ps[5 + 2 * (t % 2)][:, 0:24],
                                   ACT.Sigmoid).then_inc(gates_read, 1)

            def dve(eng, steps):
                for t in range(QT):
                    eng.wait_ge(nat, t + 1)
                    eng.tensor_copy(znat[:, t, :], ps[4 + 2 * (t % 2)]).then_inc(nat_copied, 1)

            return dict(pe=pe, act=act, dve=dve)

        @stage
        def compress():
            swap, laid, hidden, acted, small = (sem("cmp_" + x) for x in ("swap", "laid", "hidden", "acted", "small"))

            def act(eng, steps):
                for n, z in enumerate((ZKC, ZVC)):
                    eng.dma_start(swapped[0:64, n, :], zT[64:128, z, :]).then_inc(swap, 16)
                    eng.dma_start(swapped[64:128, n, :], zT[0:64, z, :]).then_inc(swap, 16)
                for n in range(2):
                    eng.wait_ge(hidden, n + 1)
                    for m in range(2):
                        eng.activation(hid[n][:, m, :], ps[2 * n + m][:, 0:2 * NCMP], ACT.Silu,
                                       bias=col("b1" + "kv"[n], m)).then_inc(acted, 1)

            def dve(eng, steps):
                eng.wait_ge(swap, 64)
                for n, z in enumerate((ZKC, ZVC)):
                    pos = "pos" + "kv"[n]
                    for par in range(2):
                        lo = 64 * par
                        for g in range(2):
                            src = zT[lo:lo + 64, z, :] if par == g else swapped[lo:lo + 64, n, :]
                            eng.tensor_tensor(blocks[n][lo:lo + 64, :, g, :], view(src, par, [[2, 16], [16, NCMP]]),
                                              view(col(pos)[lo:lo + 64], 0, [[1, 16], [0, NCMP]]),
                                              ALU.add).then_inc(laid, 1)
                eng.wait_ge(small, 1)
                eng.tensor_copy(kcmpT[:, 0:NCMP], ps[4][:, 0:NCMP])
                eng.tensor_copy(vcmp[0:NCMP, :], ps[5][0:NCMP, 0:P])

            def pe(eng, steps):
                arrived(eng, "compress")
                for n in range(2):
                    eng.wait_ge(laid, 4 * n + 4)
                    for m in range(2):
                        for jj in range(16):
                            last = eng.matmul(ps[2 * n + m][:, 0:2 * NCMP], cw1[n][:, jj, m * P:(m + 1) * P],
                                              blocks[n][:, jj].rearrange("p g n -> p (g n)"),
                                              start=(jj == 0), stop=(jj == 15))
                    last.then_inc(hidden, 1)
                eng.wait_ge(acted, 4)
                for g in range(2):
                    for m in range(2):
                        eng.matmul(ps[4][64 * g:64 * g + 64, 0:NCMP], cw2[0][:, m, :],
                                   hid[0][:, m, g * NCMP:(g + 1) * NCMP], start=(m == 0), stop=(m == 1))
                for g in range(2):
                    for m in range(2):
                        last = eng.matmul(ps[5][0:NCMP, 64 * g:64 * g + 64], hid[1][:, m, g * NCMP:(g + 1) * NCMP],
                                          cw2[1][:, m, :], start=(m == 0), stop=(m == 1))
                last.then_inc(small, 1)

            return dict(act=act, dve=dve, pe=pe)

        @stage
        def attention():
            qs_ready, bias_in, scored, read_s, neg, exped, coef, scaled, scaled_sel, turned, kept, kept_sel, summed, y_free = (
                sem("at_" + x) for x in ("qs", "bias", "scored", "read", "neg", "exped", "coef",
                                         "scaled", "scaled_sel", "turned", "kept", "kept_sel", "summed", "yfree"))
            order = [(g, i) for i in range(QT) for g in range(2)]
            NU = len(order)

            def nkeys(i):
                return [8 * i + 7, (i + 1) * P, (i + 1) * P]

            def score_bank(u, b):
                par = u % 2
                return ps[4][:, 64 * par:64 * par + 32] if b == 0 else ps[2 * par + b - 1]

            def pe(eng, steps):
                keys = [kcmpT, zT[:, ZKS, :], zT[:, ZKW, :]]

                def scores(u, j):
                    g, i = order[u]
                    eng.wait_ge(read_s, NU * j + u + 1)
                    eng.wait_ge(kept, NU * j + max(u - 1, 0) + 1)
                    eng.wait_ge(scored, NU * j + u + 1)
                    for b in range(3):
                        n = nkeys(i)[b]
                        last = eng.matmul(score_bank(u, b)[:, 0:n], qs[64 * g:64 * g + 64, i * P:(i + 1) * P],
                                          keys[b][64 * g:64 * g + 64, 0:n], start=True, stop=True)
                    last.then_inc(scored, 1)

                def turn(u, j):
                    g, i = order[u]
                    for s in (scaled, scaled_sel):
                        eng.wait_ge(s, NU * j + u + 1)
                    for s in (kept, kept_sel):
                        eng.wait_ge(s, NU * j + u + 1)
                    eng.wait_ge(read_s, NU * j + min(u + 2, NU) + 1)
                    eng.transpose(ps[4][0:nkeys(i)[0], P:2 * P], sc[u % 2][0][:, 0:nkeys(i)[0]], ident)
                    for b in (1, 2):
                        for kb in range(i + 1):
                            last = eng.transpose(ps[4 + b][:, kb * P:(kb + 1) * P],
                                                 sc[u % 2][b][:, kb * P:(kb + 1) * P], ident)
                    last.then_inc(turned, 1)

                def weigh(u, j):
                    g, i = order[u]
                    for s in (kept, kept_sel):
                        eng.wait_ge(s, NU * j + u + 2)
                    if u == 0:
                        eng.wait_ge(y_free, j + 1)
                    dst = ps[7][64 * g:64 * g + 64, i * P:(i + 1) * P]
                    n = nkeys(i)[0]
                    eng.matmul(dst, vcmp[0:n, 64 * g:64 * g + 64], pt[u % 2][0][0:n, :], start=True, stop=False)
                    for b in (1, 2):
                        for kb in range(i + 1):
                            last = eng.matmul(dst, znat[:, kb, P * (b - 1) + 64 * g:P * (b - 1) + 64 * g + 64],
                                              pt[u % 2][b][:, kb * P:(kb + 1) * P], start=False,
                                              stop=(b == 2 and kb == i))
                    last.then_inc(summed, 1)

                for s in (scored, turned, summed):
                    eng.sem_inc(s, 1)
                with eng.Fori(0, NPAIR) as j:
                    eng.wait_ge(qs_ready, j + 1)
                    for u in range(NU + 2):
                        if u < NU:
                            scores(u, j)
                        if u >= 2:
                            weigh(u - 2, j)
                        if 1 <= u <= NU:
                            turn(u - 1, j)

            def dve(eng, steps):
                def maxima(u, j):
                    g, i = order[u]
                    st = stat[u % 2]
                    eng.wait_ge(scored, NU * j + u + 2)
                    eng.wait_ge(turned, NU * j + max(u - 1, 0) + 1)
                    passed(eng, "dve")
                    for b in range(3):
                        n = nkeys(i)[b]
                        at = 415 - 128 * i
                        bb = bias[:, g, at:at + 16 * (n - 1) + 1:16] if b == 0 else bias[:, g, 128 * (3 - i):512]
                        last = eng.tensor_tensor_reduce(sc[u % 2][b][:, 0:n], score_bank(u, b)[:, 0:n], bb, 1.0,
                                                        -1e20, ALU.add, ALU.max, st[:, b:b + 1])
                    last.then_inc(read_s, 1)
                    eng.wait_ge(read_s, NU * j + u + 2)
                    eng.tensor_scalar(st[:, 3:6], st[:, 0:3], -1.0, None, ALU.mult).then_inc(neg, 1)

                def weights(u, j):
                    g, i = order[u]
                    st, n = stat[u % 2], nkeys(i)
                    eng.wait_ge(exped, NU * j + u + 1)
                    steps.link(eng.tensor_scalar(st[:, 9:12], st[:, 6:9], 1e-30, None, ALU.max))
                    steps.link(eng.reciprocal(st[:, 12:15], st[:, 9:12]))
                    eng.tensor_tensor(st[:, 9:12], st[:, 12:15], gates[:, i, 4 * g + j, :], ALU.mult).then_inc(coef, 1)
                    eng.wait_ge(coef, NU * j + u + 1)
                    eng.tensor_scalar(sc[u % 2][0][:, 0:n[0]], sc[u % 2][0][:, 0:n[0]], st[:, 9:10], None, ALU.mult)
                    eng.tensor_scalar(sc[u % 2][2][:, 0:n[2]], sc[u % 2][2][:, 0:n[2]], st[:, 11:12], None,
                                      ALU.mult).then_inc(scaled, 1)

                def keep(u, j):
                    n = nkeys(order[u][1])
                    eng.wait_ge(turned, NU * j + u + 2)
                    eng.wait_ge(summed, NU * j + max(u - 1, 0) + 1)
                    eng.tensor_copy(pt[u % 2][0][0:n[0], :], ps[4][0:n[0], P:2 * P])
                    eng.tensor_copy(pt[u % 2][2][:, 0:n[2]], ps[6][:, 0:n[2]]).then_inc(kept, 1)

                for s in (read_s, kept):
                    eng.sem_inc(s, 1)
                with steps.loop(NPAIR, 2 * NU) as j:
                    eng.wait_ge(bias_in, 32 * j + 32)
                    for u in range(NU + 2):
                        if u >= 2:
                            keep(u - 2, j)
                        if u < NU:
                            maxima(u, j)
                        if 1 <= u <= NU:
                            weights(u - 1, j)

            def pool(eng, steps):
                with eng.Fori(0, NPAIR) as j:
                    for u in range(NU):
                        n = nkeys(order[u][1])[1]
                        eng.wait_ge(coef, NU * j + u + 1)
                        passed(eng, "pool")
                        eng.tensor_scalar(sc[u % 2][1][:, 0:n], sc[u % 2][1][:, 0:n], stat[u % 2][:, 10:11], None,
                                          ALU.mult).then_inc(scaled_sel, 1)

            def act(eng, steps):
                arrived(eng, "bias_tiles")
                for s in (kept_sel, y_free):
                    eng.sem_inc(s, 1)
                with eng.Fori(0, NPAIR) as j:
                    eng.wait_ge(read_s, NU * j + 1)
                    eng.wait_ge(scored, NU * j + 1)
                    for g in range(2):
                        eng.dma_start(bias[:, g, :], bias_tiles[4 * g + j]).then_inc(bias_in, 16)
                    eng.activation(qs[:, :], zT[:, ZQ + j, :], ACT.Copy, scale=0.125).then_inc(qs_ready, 1)
                    for u in range(NU + 2):
                        if u >= 2:
                            n = nkeys(order[u - 2][1])[1]
                            eng.wait_ge(turned, NU * j + u)
                            eng.wait_ge(summed, NU * j + max(u - 3, 0) + 1)
                            eng.copy(pt[u % 2][1][:, 0:n], ps[5][:, 0:n]).then_inc(kept_sel, 1)
                        if u < NU:
                            g, i = order[u]
                            st = stat[u % 2]
                            eng.wait_ge(neg, NU * j + u + 1)
                            for b in range(3):
                                n = nkeys(i)[b]
                                last = eng.activation(sc[u % 2][b][:, 0:n], sc[u % 2][b][:, 0:n], ACT.Exp,
                                                      bias=st[:, 3 + b:4 + b], accum_out=st[:, 6 + b:7 + b])
                            last.then_inc(exped, 1)
                    eng.wait_ge(summed, NU * j + NU + 1)
                    eng.copy(mixT[:, j, :], ps[7]).then_inc(y_free, 1)

            return dict(pe=pe, dve=dve, act=act, pool=pool)


        @stage
        def convolution():
            e = Events(sem, "conv", {
                "act": (("gated", 2), ("squared", 2), ("rooted", 1),),
                "pe": (("meaned", 1), ("summed", 1),),
                "dve": (("convolved", 2), ("centred", 2), ("varied", 1), ("scaled", 2),),
            })

            def act(eng, steps):
                for m in range(2):
                    eng.activation(cvt[:, m, :], zT[:, ZCU + 2 + m, :], ACT.Sigmoid).then_inc(e.of("gated"), 1)
                for m in range(2):
                    eng.wait_ge(*e("centred", m + 1))
                    eng.activation(cvt[:, m, :], cvx[:, m, :], ACT.Square).then_inc(e.of("squared"), 1)
                eng.wait_ge(*e("varied", 1))
                eng.activation(rstd2, rstd, ACT.Sqrt).then_inc(e.of("rooted"), 1)
                for m in range(2):
                    eng.wait_ge(*e("scaled", m + 1))
                    eng.activation(mixT[:, 4 + m, :], cvx[:, m, :], ACT.Silu, bias=col("ln_b", m))

            def pe(eng, steps):
                for b, src, ready, done in ((0, cva, "convolved", "meaned"), (1, cvt, "squared", "summed")):
                    for m in range(2):
                        eng.wait_ge(*e(ready, m + 1))
                        last = eng.matmul(ps[b], ones, src[:, m, :], start=(m == 0), stop=(m == 1))
                    last.then_inc(e.of(done), 1)

            def dve(eng, steps):
                for m in range(2):
                    eng.memset(cvh[:, m, 0:CONV_W - 1], 0.0)
                    eng.wait_ge(*e("gated", m + 1))
                    steps.did(eng.tensor_tensor(cvh[:, m, CONV_W - 1:CONV_W - 1 + S], zT[:, ZCU + m, :], cvt[:, m, :],
                                                ALU.mult))
                steps.wait()
                for k in range(CONV_W):
                    for m in range(2):
                        w = col("conv_w", 2 * k + m)
                        if k == 0:
                            ins = eng.tensor_scalar(cva[:, m, :], cvh[:, m, 0:S], w, col("conv_b", m), ALU.mult, ALU.add)
                        else:
                            ins = eng.scalar_tensor_tensor(cva[:, m, :], cvh[:, m, k:k + S], w, cva[:, m, :],
                                                           ALU.mult, ALU.add)
                        if k == CONV_W - 1:
                            ins.then_inc(e.of("convolved"), 1)
                        else:
                            steps.did(ins)
                    steps.wait()
                eng.wait_ge(*e("convolved", 2))
                eng.wait_ge(*e("meaned", 1))
                for m in range(2):
                    eng.scalar_tensor_tensor(cvx[:, m, :], ps[0], -1.0 / 256, cva[:, m, :], ALU.mult,
                                             ALU.add).then_inc(e.of("centred"), 1)
                eng.wait_ge(*e("summed", 1))
                eng.tensor_scalar(rstd, ps[1], 1.0 / 256, EPS, ALU.mult, ALU.add).then_inc(e.of("varied"), 1)
                eng.wait_ge(*e("rooted", 1))
                eng.wait_ge(*e("centred", 2))
                steps.link(eng.reciprocal(rstd, rstd2))
                for m in range(2):
                    eng.scalar_tensor_tensor(cvx[:, m, :], cvx[:, m, :], col("ln_g", m), rstd, ALU.mult,
                                             ALU.mult).then_inc(e.of("scaled"), 1)

            return dict(act=act, pe=pe, dve=dve)

        @stage
        def gla():
            e = Events(sem, "gla", {
                "act": (("logged", 1), ("eq", 1), ("decays", 1), ("ek", 1), ("kept", 1), ("silued", 2), ("copied", 2),
                        ("squared", 2), ("rooted", 2)),
                "pe": (("alpha", 1), ("turned", 1), ("attn", 4), ("inter", 1)),
                "dve": (("shifted", 1), ("cummed", 1), ("laid", 2), ("masked", 4), ("added", 4), ("varied", 2)),
            }, alone=("summed", "stated", "updated", "sq_summed"))
            t0, t1, t2 = gl_t

            def act(eng, steps):
                load(eng, "gla", gl_wa[0:16, :], A["gla_wa"])
                load(eng, "gla", gl_reset, A["gl_reset"])
                load(eng, "gla", gl_mask, A["gl_mask"])
                eng.wait_ge(*e("shifted", 1))
                steps.link(eng.activation(t1, t0, ACT.Abs))
                steps.link(eng.activation(t1, t1, ACT.Exp, scale=-1.0))
                eng.activation(t2, t1, ACT.Ln, bias=ones[:, 0:1]).then_inc(e.of("logged"), 1)
                eng.wait_ge(*e("cummed", 1))
                eng.activation(t1, gl_cum, ACT.Exp, scale=1.0 / 16).then_inc(e.of("eq"), 1)
                eng.activation(gl_dn, gl_cum[:, C - 1:S:C], ACT.Exp, scale=1.0 / 16).then_inc(e.of("decays"), 1)
                eng.activation(t2, gl_cum, ACT.Exp, scale=-1.0 / 16).then_inc(e.of("ek"), 1)
                eng.wait_ge(*e("turned", 1))
                eng.copy(gl_kn.rearrange("p t c -> p (t c)"), ps[7]).then_inc(e.of("kept"), 1)
                for m in range(2):
                    eng.activation(cvt[:, m, :], zT[:, ZGR + m, :], ACT.Silu).then_inc(e.of("silued"), 1)
                eng.wait_ge(*e("summed", NCH))
                for hp in range(2):
                    eng.copy(gl_o[:, hp, :], ps[6 + hp]).then_inc(e.of("copied"), 1)
                for hp in range(2):
                    eng.wait_ge(*e("added", 2 * hp + 2))
                    eng.activation(sqr[:, hp, :], gl_o[:, hp, :], ACT.Square).then_inc(e.of("squared"), 1)
                for hp in range(2):
                    eng.wait_ge(*e("varied", hp + 1))
                    eng.activation(sqr[:, 2 + hp, :], sqr[:, 4 + hp, :], ACT.Sqrt).then_inc(e.of("rooted"), 1)

            def pe(eng, steps):
                arrived(eng, "gla")
                eng.matmul(ps[0], gl_wa[0:16, :], zT[0:16, ZGA, :], start=True, stop=True).then_inc(e.of("alpha"), 1)
                eng.wait_ge(*e("laid", 2))
                for t in range(QT):
                    last = eng.transpose(ps[7][:, t * P:(t + 1) * P], gl_k[:, t * P:(t + 1) * P], ident)
                last.then_inc(e.of("turned"), 1)
                for h in range(4):
                    for n in range(NCH):
                        par, t = n % 2, n // 2
                        r = slice(32 * h, 32 * h + 32)
                        last = eng.matmul(ps[h][64 * par:64 * par + 64, t * C:(t + 1) * C], gl_k[r, n * C:(n + 1) * C],
                                          gl_q[r, n * C:(n + 1) * C], start=True, stop=True)
                    last.then_inc(e.of("attn"), 1)
                eng.wait_ge(*e("masked", 4))
                for h in range(4):
                    for n in range(NCH):
                        par, t = n % 2, n // 2
                        r, o = slice(64 * par, 64 * par + 64), 64 * (h % 2)
                        last = eng.matmul(ps[4 + par][o:o + 64, (h // 2) * 256 + t * C:(h // 2) * 256 + (t + 1) * C],
                                          znat[r, t, 256 + C * h:256 + C * h + C], gl_at4[r, h, t, :],
                                          start=True, stop=True)
                last.then_inc(e.of("inter"), 1)
                eng.wait_ge(*e("kept", 1))
                for n in range(NCH):
                    par, t = n % 2, n // 2
                    eng.wait_ge(*e("updated", n + 1))
                    for h in range(4):
                        r, o = slice(32 * h, 32 * h + 32), 64 * (h % 2)
                        last = eng.matmul(ps[6 + h // 2][o:o + 64, n * C:(n + 1) * C], gl_st[r, :],
                                          gl_q[r, n * C:(n + 1) * C], start=True, stop=True)
                    last.then_inc(e.of("summed"), 1)
                    for h in range(4):
                        r, o = slice(64 * par, 64 * par + 64), 32 * h
                        last = eng.matmul(ps[par][o:o + 32, 0:C], gl_kn[r, t, o:o + 32],
                                          znat[r, t, 256 + C * h:256 + C * h + C], start=True, stop=True)
                    last.then_inc(e.of("stated"), 1)
                for hp in range(2):
                    eng.wait_ge(*e("squared", hp + 1))
                    eng.wait_ge(*e("updated", NCH + 1))
                    eng.matmul(ps[hp], ones64, sqr[:, hp, :], start=True, stop=True).then_inc(e.of("sq_summed"), 1)

            def dve(eng, steps):
                eng.memset(gl_st, 0.0).then_inc(e.of("updated"), 1)
                eng.wait_ge(*e("alpha", 1))
                eng.tensor_scalar(t0, ps[0], col("gla_b"), None, ALU.add).then_inc(e.of("shifted"), 1)
                eng.wait_ge(*e("shifted", 1))
                steps.link(eng.tensor_scalar(gl_q, t0, 0.0, None, ALU.min))
                eng.wait_ge(*e("logged", 1))
                steps.link(eng.tensor_tensor(gl_k, gl_q, t2, ALU.subtract))
                arrived(eng, "gla")
                eng.tensor_tensor_scan(gl_cum, gl_reset, gl_k, 0.0, ALU.mult, ALU.add).then_inc(e.of("cummed"), 1)
                eng.wait_ge(*e("cummed", 1))
                eng.wait_ge(*e("eq", 1))
                eng.scalar_tensor_tensor(gl_q, t1, 32.0 ** -0.5, zT[:, ZGQ, :], ALU.mult, ALU.mult).then_inc(e.of("laid"), 1)
                eng.wait_ge(*e("ek", 1))
                eng.tensor_tensor(gl_k, t2, zT[:, ZGK, :], ALU.mult).then_inc(e.of("laid"), 1)
                for h in range(4):
                    eng.wait_ge(*e("attn", h + 1))
                    eng.tensor_tensor(gl_at4[:, h], ps[h][:, 0:QT * C].rearrange("p (t c) -> p t c", t=QT),
                                      view(gl_mask, 0, [[0, QT], [1, C]]), ALU.mult).then_inc(e.of("masked"), 1)
                eng.wait_ge(*e("decays", 1))
                for n in range(NCH):
                    eng.wait_ge(*e("stated", n + 1))
                    eng.wait_ge(*e("summed", n + 1))
                    eng.wait_ge(*e("updated", n + 1))
                    steps.link(eng.tensor_tensor(gl_st, gl_st, ps[n % 2][:, 0:C], ALU.add))
                    eng.tensor_scalar(gl_st, gl_st, gl_dn[:, n:n + 1], None, ALU.mult).then_inc(e.of("updated"), 1)
                eng.wait_ge(*e("inter", 1))
                for hp in range(2):
                    eng.wait_ge(*e("copied", hp + 1))
                    for par in range(2):
                        o = view(gl_o[:, hp, :], par * C, [[2 * C, QT], [1, C]])
                        eng.tensor_tensor(o, o, ps[4 + par][:, hp * 256:hp * 256 + 256].rearrange(
                            "p (t c) -> p t c", t=QT), ALU.add).then_inc(e.of("added"), 1)
                for hp in range(2):
                    eng.wait_ge(*e("sq_summed", hp + 1))
                    eng.tensor_scalar(sqr[:, 4 + hp, :], ps[hp], 1.0 / 64, EPS, ALU.mult, ALU.add).then_inc(e.of("varied"), 1)
                for hp in range(2):
                    eng.wait_ge(*e("rooted", hp + 1))
                    steps.link(eng.reciprocal(sqr[:, 6 + hp, :], sqr[:, 2 + hp, :]))
                    steps.link(eng.scalar_tensor_tensor(gl_o[:, hp, :], gl_o[:, hp, :], col("gla_g", hp),
                                                        sqr[:, 6 + hp, :], ALU.mult, ALU.mult))
                    eng.wait_ge(*e("silued", hp + 1))
                    eng.tensor_tensor(mixT[:, 6 + hp, :], gl_o[:, hp, :], cvt[:, hp, :], ALU.mult)

            return dict(act=act, pe=pe, dve=dve)

        def residual(tag, rhs, ktiles=8, gate=None):
            free = sem("residual_free")
            u0, per, r = UNIT0[tag], -(-ktiles // 8), 12 * residuals[0]
            residuals[0] += 1

            def pe(eng, steps):
                def use(slot, j, i):
                    m, part = j // per, j % per
                    if part == 0:
                        eng.wait_ge(free, r + 4 * i + m + 1)
                    for k in range(8 * part, min(8 * part + 8, ktiles)):
                        last = eng.matmul(ps[m % 4], ring[:, slot, k - 8 * part, :], rhs(k), start=(k == 0),
                                          stop=(k == ktiles - 1))
                    return last
                per_unit(eng, u0, 8 * per, use, body=4 * per)

            def dve(eng, steps):
                eng.sem_inc(free, 4)
                with eng.Fori(0, 2) as i:
                    for m in range(4):
                        eng.wait_ge(units_done, u0 + per * (m + 1) + 4 * per * i)
                        x = xT[:, 4 * i + m, :]
                        if gate is None:
                            ins = eng.tensor_tensor(x, x, ps[m], ALU.add)
                        else:
                            ins = eng.scalar_tensor_tensor(x, ps[m], gate(4 * i + m), x, ALU.mult, ALU.add)
                        ins.then_inc(free, 1)

            return dict(pe=pe, dve=dve)

        @stage
        def out1():
            return residual("out1", lambda k: mixT[:, k, :])

        r2 = base.remainder()
        actT = r2.take(FT, S)
        sil = r2.take(2, S)

        @stage
        def norm_ffn():
            return norm(lambda k: xT[:, k, :], lambda k: hT[:, k, 0:S], lambda k: col("ffn_g", k))

        @stage
        def ffn1():
            free_gate, free_up, silued, used = (sem("f1_" + x) for x in ("free_gate", "free_up", "silued", "used"))
            u0 = UNIT0["ffn1"]

            def pe(eng, steps):
                def use(slot, j, i):
                    eng.wait_ge((free_gate, free_up)[j % 2], 2 * i + j // 2 + 1)
                    return product(eng, slot, lambda k: hT[:, k, 0:S], ps[j])
                per_unit(eng, u0, 2 * FT, use)

            def act(eng, steps):
                eng.sem_inc(free_gate, 2)
                with eng.Fori(0, FT // 2) as i:
                    for f in range(2):
                        eng.wait_ge(units_done, u0 + 4 * i + 2 * f + 1)
                        eng.wait_ge(used, 2 * i + f + 1)
                        eng.activation(sil[:, f, :], ps[2 * f], ACT.Silu).then_inc(silued, 1)
                        eng.wait_ge(silued, 2 * i + f + 1)
                        eng.sem_inc(free_gate, 1)

            def dve(eng, steps):
                eng.sem_inc(free_up, 2)
                eng.sem_inc(used, 2)
                with eng.Fori(0, FT // 2) as i:
                    for f in range(2):
                        eng.wait_ge(units_done, u0 + 4 * i + 2 * f + 2)
                        eng.wait_ge(silued, 2 * i + f + 1)
                        eng.tensor_tensor(actT[:, 2 * i + f, :], sil[:, f, :], ps[2 * f + 1], ALU.mult).then_inc(free_up, 1)
                        eng.wait_ge(free_up, 2 * i + f + 3)
                        eng.sem_inc(used, 1)

            return dict(pe=pe, act=act, dve=dve)

        @stage
        def down1():
            return residual("down1", lambda k: actT[:, k, :], ktiles=FT)

        r3 = base.remainder()
        pT = r3.take(2, S)
        pj = r3.take(KT, S)
        gt = r3.take(4, S)

        @stage
        def ple_project():
            free = sem("pp_free")
            u0 = UNIT0["pleproj"]

            def pe(eng, steps):
                arrived(eng, "pT")

                def use(slot, j, i):
                    for m in range(4):
                        eng.wait_ge(free, 4 * j + m + 1)
                        for k in range(2):
                            last = eng.matmul(ps[m], ring[:, slot, 2 * m + k, :], pT[:, k, :], start=(k == 0),
                                              stop=(k == 1))
                    return last
                per_unit(eng, u0, 2, use)

            def act(eng, steps):
                load(eng, "pT", pT, A["pT"])
                eng.sem_inc(free, 4)
                for j in range(2):
                    eng.wait_ge(units_done, u0 + j + 1)
                    for m in range(4):
                        eng.copy(pj[:, 4 * j + m, :], ps[m]).then_inc(free, 1)

            return dict(pe=pe, act=act)

        @stage
        def norm_ple():
            return norm(lambda k: xT[:, k, :], lambda k: hT[:, k, 0:S], lambda k: col("ple_g", k))

        @stage
        def ple_gate():
            free, sig, mixed = sem("pg_free"), sem("pg_sig"), sem("pg_mixed")
            u0 = UNIT0["ple"]

            def pe(eng, steps):
                linear_pe(eng, u0, 8, lambda k: hT[:, k, 0:S], free)

            def act(eng, steps):
                eng.sem_inc(free, 4)
                with eng.Fori(0, 2) as i:
                    for m in range(4):
                        eng.wait_ge(units_done, u0 + 4 * i + m + 1)
                        eng.wait_ge(mixed, 4 * i + m + 1)
                        eng.activation(gt[:, m, :], ps[m], ACT.Sigmoid).then_inc(sig, 1)
                        eng.wait_ge(sig, 4 * i + m + 1)
                        eng.sem_inc(free, 1)

            def dve(eng, steps):
                eng.sem_inc(mixed, 4)
                with steps.loop(2, 4) as i:
                    for m in range(4):
                        eng.wait_ge(sig, 4 * i + m + 1)
                        steps.link(eng.tensor_tensor(gt[:, m, :], gt[:, m, :], pj[:, 4 * i + m, :], ALU.mult))
                        eng.tensor_tensor(xT[:, 4 * i + m, :], xT[:, 4 * i + m, :], gt[:, m, :], ALU.add)\
                           .then_inc(mixed, 1)

            return dict(pe=pe, act=act, dve=dve)

        @stage
        def norm_final1():
            return norm(lambda k: xT[:, k, :], lambda k: xT[:, k, :], lambda k: col("fin_g", k))


        r4 = base.remainder()
        rC = r4.take(NCH, 4, C)
        kC = r4.take(12, 4, C)
        vC = r4.take(12, 4, C)
        kkC = r4.take(12, 4, C)
        yC = r4.take(NCH, 4, C)
        fT = r4.take(4, S)
        gdT = r4.take(S)
        r5 = r4.remainder()
        RAW = T2 + 3
        raw = r5.take(12, RAW)
        dft = r5.take(2, 4, S)
        r6 = r4.remainder()
        sig = [r6.take(12, 4, C) for _ in range(2)]
        kka = [r6.take(12, 4, C) for _ in range(2)]
        kd0 = r6.take(12, 4, C)
        kd = [kd0, kC]
        r7 = Region(hT.offset, hT.offset + KT * T2)
        uF = r7.take(4, S)
        mixed = r7.take(4, 2, S)
        r8 = Region(hT.offset, hT.offset + KT * T2)
        lw = r8.take(T2)
        la = r8.take(T2)
        aT = r8.take(2, T2)
        ksq = r8.take(2, T2)
        wl = r8.take(512)
        al = r8.take(512)
        ctxT = Region(r4.at, SB_COLS).take(KT, CTX)
        modrow = Region(r4.at + KT * CTX, SB_COLS).take(12, 512)
        cs = Region(r4.at + KT * CTX + 6144, SB_COLS).take(16)
        ZWD, ZAD = lw, la

        @stage
        def ada():
            cond, rows, got, turned_, modded = (sem("ada_" + x) for x in ("cond", "rows", "got", "turned", "modded"))
            u0 = UNIT0["ada"]

            def act(eng, steps):
                load(eng, "ctxT", ctxT, A["ctxT"])
                eng.activation(cs, col("c", 0, 16), ACT.Silu).then_inc(cond, 1)
                eng.sem_inc(got, 2)
                with eng.Fori(0, 6) as i:
                    for b in range(2):
                        eng.wait_ge(units_done, u0 + 8 * i + 4 * b + 4)
                        eng.copy(modrow[0:2, 2 * i + b, :], ps[b][0:2, :]).then_inc(got, 1)

            def pe(eng, steps):
                eng.wait_ge(cond, 1)

                def use(slot, j, i):
                    b, q = j // 4, j % 4
                    if q == 0:
                        eng.wait_ge(got, 2 * i + b + 1)
                    for k in range(2):
                        last = eng.matmul(ps[b][0:2, :], cs[:, 2 * q + k:16:8],
                                          ring[:, slot, 4 * k:4 * k + 4, :].rearrange("p a b -> p (a b)"),
                                          start=(q == 0 and k == 0), stop=(q == 3 and k == 1))
                    return last
                per_unit(eng, u0, 48, use, body=8)
                eng.wait_ge(got, 14)
                for t in range(48):
                    last = eng.transpose(ps[2][:, 2 * t:2 * t + 2], modrow[0:2, t // 4, P * (t % 4):P * (t % 4) + P],
                                         ident[0:2, 0:2])
                last.then_inc(turned_, 1)

            def dve(eng, steps):
                eng.wait_ge(turned_, 1)
                steps.link(eng.tensor_tensor(mod, ps[2][:, 0:96].rearrange("p (t v) -> p t v", v=2),
                                             view(col("ada_b"), 0, [[1, 48], [0, 2]]), ALU.add))
                for n, (at, v, g) in enumerate(((8, 0, "n1_g"), (8, 1, "n1_g"), (32, 0, "n2_g"))):
                    eng.scalar_tensor_tensor(gains[:, n, :], mod[:, at:at + 8, v], 1.0, col(g, 0, 8), ALU.add, ALU.mult)
                eng.tensor_scalar(omka, col("k_a", 0, 4), -1.0, 1.0, ALU.mult, ALU.add)
                arrived(eng, "ctxT")

            return dict(act=act, pe=pe, dve=dve)

        @stage
        def norm_x():
            return norm(lambda k: xT[:, k, :], lambda k: hT[:, k, CTX:T2], lambda k: gains[:, 0, k:k + 1],
                        shift=lambda k: mod[:, k, 0:1])

        @stage
        def norm_ctx():
            return norm(lambda k: ctxT[:, k, :], lambda k: hT[:, k, 0:CTX], lambda k: gains[:, 1, k:k + 1],
                        n=CTX, shift=lambda k: mod[:, k, 1:2])

        @stage
        def project2():
            free, free_ctx = sem("in2_free"), sem("in2_free_ctx")
            u0 = UNIT0["in2"]
            both = {m: True for m in range(4, 14)}
            lowT = sqr[:, 0:3, :].rearrange("p a b -> p (a b)")

            def dest(m):
                if m < 12:
                    return raw[:, m, CTX + 2:CTX + 2 + S], raw[:, m, 1:1 + CTX]
                if m < 14:
                    return lowT[:, (m - 12) * T2 + CTX:(m - 11) * T2], lowT[:, (m - 12) * T2:(m - 12) * T2 + CTX]
                return (gdT, None) if m == 14 else (fT[:, m - 15, :], None)

            def pe(eng, steps):
                def use(m):
                    def f(slot, j, i):
                        mm = m + j
                        eng.wait_ge(free, mm + 1)
                        last = product(eng, slot, lambda k: hT[:, k, CTX:T2], ps[mm % 4])
                        if mm in both:
                            eng.wait_ge(free_ctx, mm - 3)
                            last = product(eng, slot, lambda k: hT[:, k, 0:CTX], ps[4 + mm % 4][:, 0:CTX])
                        return last
                    return f
                for m in range(19):
                    per_unit(eng, u0 + m, 1, use(m))

            def act(eng, steps):
                eng.sem_inc(free, 4)
                for m in range(19):
                    eng.wait_ge(units_done, u0 + m + 1)
                    eng.copy(dest(m)[0], ps[m % 4]).then_inc(free, 1)

            def dve(eng, steps):
                eng.sem_inc(free_ctx, 4)
                for at in (0, CTX + 1, RAW - 1):
                    eng.memset(raw[:, :, at:at + 1], 0.0)
                eng.memset(raw[:, 0:4, 1:1 + CTX], 0.0)
                for m in both:
                    eng.wait_ge(units_done, u0 + m + 1)
                    eng.tensor_copy(dest(m)[1], ps[4 + m % 4][:, 0:CTX]).then_inc(free_ctx, 1)

            return dict(pe=pe, act=act, dve=dve)

        @stage
        def fourier():
            e = Events(sem, "fourier", {
                "act": (("copied", 1), ("firsts", 16), ("squared", 4), ("rooted", 1),),
                "pe": (("first", 16), ("second", 4), ("summed", 1),),
                "dve": (("varied", 1),),
            })
            dft64 = sqr[:, 3, 0:256]

            def act(eng, steps):
                load(eng, "x_out", x_dram, xT.rearrange("p a b -> p (a b)"))
                load(eng, "fourier", dft, A["dft"])
                load(eng, "fourier", dft64, A["dft64"])
                eng.copy(uF.rearrange("p a b -> p (a b)"), fT.rearrange("p a b -> p (a b)")).then_inc(e.of("copied"), 1)
                for n in range(16):
                    ct, tt = n // 4, n % 4
                    eng.wait_ge(*e("first", n + 1))
                    for q in range(2):
                        last = eng.copy(mixed[:, tt, q, ct * P:(ct + 1) * P], ps[n % 4][:, q * P:(q + 1) * P])
                    last.then_inc(e.of("firsts"), 1)
                for ct in range(4):
                    eng.wait_ge(*e("second", ct + 1))
                    eng.activation(sqr[:, 4 + ct, :], ps[4 + ct], ACT.Square).then_inc(e.of("squared"), 1)
                eng.wait_ge(*e("varied", 1))
                eng.activation(rstd2, rstd, ACT.Sqrt).then_inc(e.of("rooted"), 1)

            def pe(eng, steps):
                arrived(eng, "fourier")
                eng.wait_ge(*e("copied", 1))
                for n in range(16):
                    ct, tt = n // 4, n % 4
                    if n >= 4:
                        eng.wait_ge(*e("firsts", n - 3))
                    eng.matmul(ps[n % 4][:, 0:256], uF[:, ct, tt * P:(tt + 1) * P], dft64, start=True, stop=True)\
                       .then_inc(e.of("first"), 1)
                eng.wait_ge(*e("firsts", 16))
                for ct in range(4):
                    for tt in range(4):
                        for q in range(2):
                            last = eng.matmul(ps[4 + ct], mixed[:, tt, q, ct * P:(ct + 1) * P], dft[:, q, tt, :],
                                              start=(tt + q == 0), stop=(tt == 3 and q == 1))
                    last.then_inc(e.of("second"), 1)
                for ct in range(4):
                    eng.wait_ge(*e("squared", ct + 1))
                    last = eng.matmul(ps[0], ones, sqr[:, 4 + ct, :], start=(ct == 0), stop=(ct == 3))
                last.then_inc(e.of("summed"), 1)

            def dve(eng, steps):
                eng.wait_ge(*e("summed", 1))
                eng.tensor_scalar(rstd, ps[0], 1.0 / 512, EPS, ALU.mult, ALU.add).then_inc(e.of("varied"), 1)
                eng.wait_ge(*e("rooted", 1))
                steps.link(eng.reciprocal(rstd, rstd2))
                for ct in range(4):
                    eng.scalar_tensor_tensor(fT[:, ct, :], ps[4 + ct], col("fo_g", ct), rstd, ALU.mult, ALU.mult)

            return dict(act=act, pe=pe, dve=dve)

        def tokens(ap, hp, lo, hi):
            return ap[:, lo:hi, hp, :]

        @stage
        def shift_rkv():
            tapped = sem("sh_tapped")

            def act(eng, steps):
                load(eng, "low_rank", wl[:, :], A["w_low"])
                load(eng, "low_rank", al[:, :], A["a_low"])
                for m in range(12):
                    for dst, src, n in pieces(m):
                        eng.activation(dst, view(src, 0, [[C, n], [1, C]]), ACT.Copy, scale=col("rconv", m)).then_inc(tapped, 1)
                lowT = sqr[:, 0:3, :].rearrange("p a b -> p (a b)")
                eng.activation(lw, lowT[:, 0:T2], ACT.Tanh)
                eng.copy(la, lowT[:, T2:2 * T2])

            def pieces(m):
                q, hp = m // 4, m % 4
                dst = (rC, kC, vC)[q]
                lo = 0 if q == 0 else 4
                out_ = [(dst[:, lo:lo + NCH, hp, :], raw[:, m, CTX + 1:CTX + 1 + S], NCH)]
                if q:
                    out_.append((dst[:, 0:4, hp, :], raw[:, m, 0:CTX], 4))
                return out_

            def dve(eng, steps):
                n_ = 0
                for m in range(12):
                    for dst, src, n in pieces(m):
                        n_ += 1
                        eng.wait_ge(tapped, n_)
                        for tap in (1, 2):
                            steps.link(eng.scalar_tensor_tensor(dst, view(src, tap, [[C, n], [1, C]]),
                                                                col("rconv", 12 * tap + m), dst, ALU.mult, ALU.add))

            return dict(act=act, dve=dve)

        @stage
        def keys():
            scaled_, squared, summed, varied, rooted = (sem("kk_" + x) for x in (
                "scaled", "squared", "summed", "varied", "rooted"))

            def act(eng, steps):
                for hp in range(4):
                    eng.wait_ge(scaled_, hp + 1)
                    if hp >= 2:
                        eng.wait_ge(summed, hp - 1)
                    eng.activation(ksq[:, hp % 2, :].rearrange("p (c t) -> p c t", c=12), kkC[:, :, hp, :], ACT.Square)\
                       .then_inc(squared, 1)
                    eng.wait_ge(varied, hp + 1)
                    eng.activation(aT[:, hp % 2, :], aT[:, hp % 2, :], ACT.Sqrt).then_inc(rooted, 1)

            def pe(eng, steps):
                for hp in range(4):
                    eng.wait_ge(squared, hp + 1)
                    if hp >= 2:
                        eng.wait_ge(varied, hp - 1)
                    b = 2 * (hp % 2)
                    eng.matmul(ps[b], ones64, ksq[:, hp % 2, 0:512], start=True, stop=True)
                    eng.matmul(ps[b + 1][:, 0:256], ones64, ksq[:, hp % 2, 512:T2], start=True, stop=True).then_inc(summed, 1)

            def dve(eng, steps):
                for hp in range(4):
                    eng.tensor_scalar(kkC[:, :, hp, :], kC[:, :, hp, :], col("k_k", hp), None, ALU.mult).then_inc(scaled_, 1)
                eng.wait_ge(scaled_, 4)
                for hp in range(4):
                    b = 2 * (hp % 2)
                    eng.wait_ge(summed, hp + 1)
                    if hp >= 2:
                        steps.wait()
                    eng.tensor_scalar(aT[:, hp % 2, 0:512], ps[b], 1e-12, None, ALU.add)
                    eng.tensor_scalar(aT[:, hp % 2, 512:T2], ps[b + 1][:, 0:256], 1e-12, None, ALU.add).then_inc(varied, 1)
                    eng.wait_ge(rooted, hp + 1)
                    steps.link(eng.reciprocal(ksq[:, hp % 2, :], aT[:, hp % 2, :]))
                    steps.did(eng.tensor_tensor(kkC[:, :, hp, :], kkC[:, :, hp, :],
                                                ksq[:, hp % 2, :].rearrange("p (c t) -> p c t", c=12), ALU.mult))

            return dict(act=act, pe=pe, dve=dve)

        @stage
        def low_rank():
            made, read, rated, used = (sem("lr_" + x) for x in ("made", "read", "rated", "used"))

            def pe(eng, steps):
                arrived(eng, "low_rank")
                n = 0
                for d in range(2):
                    r = slice(64 * d, 64 * d + 64)
                    for hp in range(4):
                        for wgt, src in ((wl, lw), (al, la)):
                            b = 2 * (n % 4)
                            if n >= 4:
                                eng.wait_ge(read, n - 3)
                            w = wgt[r, hp * P:(hp + 1) * P]
                            eng.matmul(ps[b], w, src[r, 0:512], start=True, stop=True)
                            eng.matmul(ps[b + 1][:, 0:256], w, src[r, 512:T2], start=True, stop=True).then_inc(made, 1)
                            n += 1

            def act(eng, steps):
                n = 0
                for d in range(2):
                    for hp in range(4):
                        b = 2 * (n % 4)
                        eng.wait_ge(made, n + 1)
                        bias = col("w0", 4 * d + hp)
                        eng.activation(sig[d][:, 0:8, hp, :], ps[b].rearrange("p (c t) -> p c t", c=8), ACT.Sigmoid, bias=bias)
                        eng.activation(sig[d][:, 8:12, hp, :], ps[b + 1][:, 0:256].rearrange("p (c t) -> p c t", c=4),
                                       ACT.Sigmoid, bias=bias).then_inc(read, 1)
                        n += 1
                        b = 2 * (n % 4)
                        eng.wait_ge(made, n + 1)
                        k = 4 * d + hp
                        if k >= 2:
                            eng.wait_ge(used, k - 1)
                        bias = col("a0", k)
                        eng.activation(aT[:, k % 2, 0:512], ps[b], ACT.Sigmoid, bias=bias).then_inc(rated, 1)
                        eng.activation(aT[:, k % 2, 512:T2], ps[b + 1][:, 0:256], ACT.Sigmoid, bias=bias).then_inc(read, 1)
                        n += 1

            def dve(eng, steps):
                for d in range(2):
                    for hp in range(4):
                        k = 4 * d + hp
                        eng.wait_ge(read, 2 * k + 2)
                        a = aT[:, k % 2, :].rearrange("p (c t) -> p c t", c=12)
                        steps.link(eng.tensor_tensor(kka[d][:, :, hp, :], kkC[:, :, hp, :], a, ALU.mult))
                        steps.link(eng.tensor_scalar(a, a, col("k_a", hp), omka[:, hp:hp + 1], ALU.mult, ALU.add))
                        eng.tensor_tensor(kd[d][:, :, hp, :], kC[:, :, hp, :], a, ALU.mult).then_inc(used, 1)

            return dict(act=act, pe=pe, dve=dve)

        free_regions = [Region(hT.offset, hT.offset + KT * T2), Region(sqr.offset, sqr.offset + KT * S),
                        Region(xT.offset, xT.offset + KT * S),
                        Region(r6.at, SB_COLS)]

        def stage_take(*dims):
            for r in free_regions:
                if r.at + int(np.prod(dims)) <= r.end:
                    return r.take(*dims)
            raise AssertionError(dims)

        G = 4 * C
        masks = stage_take(2, 4, C)
        lev = stage_take(2, 6, C)
        eye = stage_take(C)
        reset = stage_take(2, G)
        st_ = []
        for d in range(2):
            st_.append(dict(
                cum=stage_take(4, C), prev=stage_take(4, C), e1=stage_take(4, C), e2=stage_take(4, C),
                e3=stage_take(4, C), ar=stage_take(4, 2, C), bT=stage_take(4, C), kT=stage_take(4, C),
                vT=stage_take(4, C), ab=stage_take(2, 4, C), kv=stage_take(2, 4, C), g1=stage_take(4, 2, C),
                g2=stage_take(2, 4, C), T=stage_take(4, C), Tt=stage_take(4, C), Z=stage_take(4, C),
                wtb=stage_take(2, 4, C), U=stage_take(4, C), M=stage_take(4, C)))
        DEC = math.exp(-0.5)

        def bc(ap, n=4):
            return view(ap, 0, [[0, n], [1, C]])

        @stage
        def rwkv():
            e = [{n: sem(f"rwkv_{n}{d}") for n in (
                "cum", "prev",
                "ex",
                "laid", "laid2",
                "raw",
                "masked",
                "made", "kept",
                "acted",
                "fed",
                "y", "yc", "mc",
                )} for d in range(2)]
            HB = (slice(0, 64), slice(64, 128))

            def walk(eng, steps, body, per=None):
                for n, base_, y in ((4, 0, False), (8, 4, True)):
                    if per:
                        with steps.loop(n, per(y)) as i:
                            body(i + base_, i + base_, (3 if not y else 11) - i, y)
                    else:
                        with eng.Fori(0, n) as i:
                            body(i + base_, i + base_, (3 if not y else 11) - i, y)

            def pe(eng, steps):
                def each(fn):
                    for hp in range(4):
                        for b in range(2):
                            last = fn(hp, HB[b])
                    return last

                def body(it, c0, c1, y):
                    for d in range(2):
                        s, q, B = st_[d], e[d], ps[4 * d:4 * d + 4]
                        eng.wait_ge(q["laid"], it + 1)
                        eng.wait_ge(q["laid2"], it + 2)
                        eng.wait_ge(q["mc"], it + 1)
                        if y:
                            eng.wait_ge(q["yc"], it - 4)
                        eng.wait_ge(q["acted"], 3 * it)
                        passed(eng, "pe")
                        each(lambda hp, r: eng.matmul(B[0][r, hp * C:(hp + 1) * C], s["ar"][r, hp, 0, :], ident[r, r], start=True, stop=True))
                        each(lambda hp, r: eng.matmul(B[0][r, G + hp * C:G + (hp + 1) * C], s["bT"][r, hp, :], ident[r, r], start=True, stop=True))
                        each(lambda hp, r: eng.matmul(B[1][r, hp * C:(hp + 1) * C], s["kT"][r, hp, :], ident[r, r], start=True, stop=True))
                        each(lambda hp, r: eng.matmul(B[1][r, G + hp * C:G + (hp + 1) * C], s["vT"][r, hp, :], ident[r, r], start=True, stop=True)
                             ).then_inc(q["raw"], 1)
                        n = 2 if y else 1
                        each(lambda hp, r: eng.matmul(B[2][r, hp * 2 * C:hp * 2 * C + n * C], s["bT"][r, hp, :],
                                                      s["ar"][r, hp, 0:n, :].rearrange("p a t -> p (a t)"), start=True, stop=True))
                        last = each(lambda hp, r: eng.matmul(B[3][r, hp * C:(hp + 1) * C], s["ar"][r, hp, 0, :],
                                                             s["kT"][r, hp, :], start=True, stop=True))
                        if y:
                            last = each(lambda hp, r: eng.matmul(B[3][r, G + hp * C:G + (hp + 1) * C], s["kT"][r, hp, :],
                                                                 s["ar"][r, hp, 1, :], start=True, stop=True))
                        last.then_inc(q["raw"], 1)
                    for lv in range(5):
                        for d in range(2):
                            s, q, B = st_[d], e[d], ps[4 * d:4 * d + 4]
                            if lv == 0:
                                eng.wait_ge(q["acted"], 3 * it + 1)
                                eng.wait_ge(q["masked"], 2 * it + 1)
                            else:
                                eng.wait_ge(q["kept"], 10 * it + 2 * lv)
                            passed(eng, "pe")
                            each(lambda hp, r: eng.matmul(B[0][r, hp * C:(hp + 1) * C], s["g1"][r, hp, 0, :], s["T"][r, hp, :],
                                                          start=True, stop=True)).then_inc(q["made"], 1)
                        for d in range(2):
                            s, q, B = st_[d], e[d], ps[4 * d:4 * d + 4]
                            eng.wait_ge(q["kept"], 10 * it + 2 * lv + 1)
                            passed(eng, "pe")
                            a, b_ = (s["Tt"], s["Z"]) if lv < 4 else (s["Z"], s["Tt"])
                            each(lambda hp, r: eng.matmul(B[1][r, hp * C:(hp + 1) * C], a[r, hp, :], b_[r, hp, :],
                                                          start=True, stop=True)).then_inc(q["made"], 1)
                    for d in range(2):
                        s, q, B = st_[d], e[d], ps[4 * d:4 * d + 4]
                        eng.wait_ge(q["kept"], 10 * it + 10)
                        eng.wait_ge(q["masked"], 2 * it + 2)
                        passed(eng, "pe")
                        each(lambda hp, r: eng.matmul(B[2][r, hp * C:(hp + 1) * C], s["ab"][r, 0, hp, :], s["Tt"][r, hp, :],
                                                      start=True, stop=True))
                        each(lambda hp, r: eng.matmul(B[2][r, G + hp * C:G + (hp + 1) * C], s["g2"][r, 0, hp, :],
                                                      s["Tt"][r, hp, :], start=True, stop=True)).then_inc(q["fed"], 1)
                    for d in range(2):
                        s, q, B = st_[d], e[d], ps[4 * d:4 * d + 4]
                        eng.wait_ge(q["acted"], 3 * it + 2)
                        passed(eng, "pe")

                        def u(hp, r):
                            eng.matmul(B[3][r, hp * C:(hp + 1) * C], s["wtb"][r, 0, hp, :], s["M"][r, hp, :], start=True,
                                       stop=False)
                            return eng.matmul(B[3][r, hp * C:(hp + 1) * C], s["wtb"][r, 1, hp, :], s["kv"][r, 1, hp, :],
                                              start=False, stop=True)
                        each(u).then_inc(q["fed"], 1)
                    for d in range(2):
                        s, q, B = st_[d], e[d], ps[4 * d:4 * d + 4]
                        eng.wait_ge(q["acted"], 3 * it + 3)
                        passed(eng, "pe")
                        if y:
                            def yy(hp, r):
                                dst = B[0][r, hp * C:(hp + 1) * C]
                                eng.matmul(dst, s["M"][r, hp, :], s["ar"][r, hp, 1, :], start=True, stop=False)
                                eng.matmul(dst, s["U"][r, hp, :], s["g1"][r, hp, 1, :], start=False, stop=False)
                                return eng.matmul(dst, s["kv"][r, 1, hp, :], s["g2"][r, 1, hp, :], start=False, stop=True)
                            each(yy).then_inc(q["y"], 1)

                        def mm(hp, r):
                            dst = B[1][r, hp * C:(hp + 1) * C]
                            eng.matmul(dst, s["ab"][r, 1, hp, :], s["U"][r, hp, :], start=True, stop=False)
                            return eng.matmul(dst, s["kv"][r, 0, hp, :], s["kv"][r, 1, hp, :], start=False, stop=True)
                        each(mm).then_inc(q["fed"], 1)
                for q in e:
                    eng.sem_inc(q["fed"], 1)
                walk(eng, steps, body)

            def flat(ap):
                return ap.rearrange("p h t -> p (h t)")

            def dve(eng, steps):
                arrived(eng, "rwkv")
                eng.memset(yC, 0.0)
                arrived(eng, "x_out")
                for d in range(2):
                    eng.memset(st_[d]["M"], 0.0).then_inc(e[d]["mc"], 1)

                def body(it, c0, c1, y):
                    for d, c in enumerate((c0, c1)):
                        s, q = st_[d], e[d]
                        eng.wait_ge(q["ex"], it + 1)
                        passed(eng, "dve")
                        eng.tensor_tensor_scan(flat(s["cum"]), reset[:, 0, :], flat(sig[d][:, c]), 0.0,
                                               ALU.mult, ALU.add).then_inc(q["cum"], 1)
                        eng.wait_ge(q["cum"], it + 1)
                        passed(eng, "dve")
                        if d:
                            steps.link(eng.tensor_tensor(s["prev"], view(s["cum"][:, 0, C - 1:C], 0, [[C, 4], [0, C]]), s["cum"],
                                                         ALU.subtract))
                            eng.tensor_tensor(s["cum"], s["prev"], sig[d][:, c], ALU.add).then_inc(q["prev"], 1)
                        else:
                            eng.tensor_tensor(s["prev"], s["cum"], sig[d][:, c], ALU.subtract).then_inc(q["prev"], 1)
                    for d, c in enumerate((c0, c1)):
                        s, q = st_[d], e[d]
                        eng.wait_ge(q["ex"], it + 2)
                        eng.wait_ge(q["fed"], 3 * it + 1)
                        passed(eng, "dve")
                        last = eng.tensor_tensor(s["bT"], kka[d][:, c], s["e2"], ALU.mult)
                        if y:
                            last = eng.tensor_tensor(s["ar"][:, :, 1, :], rC[:, c - 4], s["e3"], ALU.mult)
                        last.then_inc(q["laid"], 1)
                    for d in range(2):
                        s, q, B = st_[d], e[d], ps[4 * d:4 * d + 4]
                        eng.wait_ge(q["raw"], 2 * it + 2)
                        n = 2 if y else 1
                        mk = masks[:, d]
                        steps.did(eng.tensor_tensor(s["g1"][:, :, 0:n, :], B[2].rearrange("p (h n t) -> p h n t", h=4, n=2)[:, :, 0:n, :],
                                                    view(mk[:, 0:2, :], 0, [[0, 4], [C, n], [1, C]]), ALU.mult))
                        steps.wait()
                        steps.link(eng.tensor_tensor(s["Z"], s["g1"][:, :, 0, :], bc(lev[:, d, 0, :]), ALU.mult))
                        steps.link(eng.tensor_tensor(s["Tt"], s["Z"], bc(eye), ALU.add))
                        eng.transpose(flat(s["T"]), flat(s["Tt"])).then_inc(q["masked"], 1)
                        last = eng.tensor_tensor(s["g2"][:, 0], B[3][:, 0:G].rearrange("p (h t) -> p h t", h=4),
                                                 bc(mk[:, 2, :]), ALU.mult)
                        if y:
                            last = eng.tensor_tensor(s["g2"][:, 1], B[3][:, G:2 * G].rearrange("p (h t) -> p h t", h=4),
                                                     bc(mk[:, 1, :]), ALU.mult)
                        last.then_inc(q["masked"], 1)
                    for lv in range(5):
                        for d in range(2):
                            s, q, B = st_[d], e[d], ps[4 * d:4 * d + 4]
                            eng.wait_ge(q["made"], 10 * it + 2 * lv + 1)
                            eng.tensor_tensor(s["Z"], B[0][:, 0:G].rearrange("p (h t) -> p h t", h=4),
                                              bc(lev[:, d, 1 + lv, :]), ALU.mult).then_inc(q["kept"], 1)
                        for d in range(2):
                            s, q, B = st_[d], e[d], ps[4 * d:4 * d + 4]
                            eng.wait_ge(q["made"], 10 * it + 2 * lv + 2)
                            x = B[1][:, 0:G].rearrange("p (h t) -> p h t", h=4)
                            if lv < 4:
                                steps.link(eng.tensor_tensor(s["T"], s["T"], x, ALU.subtract))
                                if lv < 4:
                                    eng.transpose(flat(s["Tt"]), flat(s["T"])).then_inc(q["kept"], 1)
                            else:
                                eng.tensor_tensor(s["Tt"], s["Tt"], x, ALU.subtract).then_inc(q["kept"], 1)
                    for d, c in enumerate((c0, c1)):
                        s, q, B = st_[d], e[d], ps[4 * d:4 * d + 4]
                        if y:
                            eng.wait_ge(q["y"], it - 3)
                            passed(eng, "dve")
                            yy = yC[:, c - 4]
                            eng.tensor_tensor(yy, yy, B[0][:, 0:G].rearrange("p (h t) -> p h t", h=4), ALU.add).then_inc(q["yc"], 1)
                        eng.wait_ge(q["fed"], 3 * it + 4)
                        steps.link(eng.tensor_tensor(s["M"], s["M"], B[1][:, 0:G].rearrange("p (h t) -> p h t", h=4), ALU.add))
                        at = 0 if d else C - 1
                        eng.tensor_tensor(s["M"], s["M"], view(s["e3"][:, 0, at:at + 1], 0, [[C, 4], [0, C]]),
                                          ALU.mult).then_inc(q["mc"], 1)
                walk(eng, steps, body, per=lambda y: 17)

            def act(eng, steps):
                def body(it, c0, c1, y):
                    for d in range(2):
                        s, q = st_[d], e[d]
                        eng.wait_ge(q["prev"], it + 1)
                        eng.wait_ge(q["laid2"], it + 1)
                        eng.wait_ge(q["mc"], it + 1)
                        eng.activation(flat(s["e1"]), flat(s["prev"]), ACT.Exp, scale=-DEC)
                        eng.activation(flat(s["e2"]), flat(s["cum"]), ACT.Exp, scale=DEC)
                        eng.activation(flat(s["e3"]), flat(s["cum"]), ACT.Exp, scale=-DEC).then_inc(q["ex"], 1)
                    for d in range(2):
                        s, q, B = st_[d], e[d], ps[4 * d:4 * d + 4]
                        eng.wait_ge(q["raw"], 2 * it + 1)
                        eng.copy(s["ab"].rearrange("p a h t -> p (a h t)"), B[0])
                        eng.copy(s["kv"].rearrange("p a h t -> p (a h t)"), B[1]).then_inc(q["acted"], 1)
                    for d in range(2):
                        s, q, B = st_[d], e[d], ps[4 * d:4 * d + 4]
                        eng.wait_ge(q["fed"], 3 * it + 2)
                        eng.copy(s["wtb"].rearrange("p a h t -> p (a h t)"), B[2]).then_inc(q["acted"], 1)
                    for d in range(2):
                        s, q, B = st_[d], e[d], ps[4 * d:4 * d + 4]
                        eng.wait_ge(q["fed"], 3 * it + 3)
                        eng.activation(flat(s["U"]), B[3][:, 0:G], ACT.Copy, scale=-1.0).then_inc(q["acted"], 1)
                arrived(eng, "x_out")
                load(eng, "rwkv", masks, A["masks"])
                load(eng, "rwkv", lev, A["lev"])
                load(eng, "rwkv", eye, A["eye"])
                load(eng, "rwkv", reset, A["reset"])
                for q in e:
                    eng.sem_inc(q["ex"], 1)
                walk(eng, steps, body)

            def pool(eng, steps):
                def body(it, c0, c1, y):
                    for d, c in enumerate((c0, c1)):
                        s, q = st_[d], e[d]
                        eng.wait_ge(q["fed"], 3 * it + 1)
                        passed(eng, "pool")
                        eng.tensor_copy(s["vT"], vC[:, c])
                        eng.wait_ge(q["ex"], it + 2)
                        passed(eng, "pool")
                        eng.tensor_tensor(s["ar"][:, :, 0, :], kkC[:, c], s["e1"], ALU.mult)
                        eng.tensor_tensor(s["kT"], kd[d][:, c], s["e2"], ALU.mult).then_inc(q["laid2"], 1)
                for q in e:
                    eng.sem_inc(q["laid2"], 1)
                walk(eng, steps, body)

            return dict(pe=pe, dve=dve, act=act, pool=pool)

        r9 = Region(hT.offset, hT.offset + KT * T2)
        rwT = r9.take(4, S)
        gcen = r9.take(4, S)
        g2w = r9.take(512)
        gsig = r9.take(S)
        r10 = Region(sqr.offset, sqr.offset + KT * S)
        gsq = r10.take(4, S)
        gvar = r10.take(2, S)
        groot = r10.take(2, S)

        @stage
        def rwkv_out():
            e = Events(sem, "rwout", {
                "act": (("gate", 1), ("squared", 4), ("rooted", 4)),
                "pe": (("mean", 4), ("summed", 4), ("bonus", 4), ("gated", 4)),
                "dve": (("centred", 4), ("keyed", 4)),
            }, alone=("varied", "normed"))

            def chunked(ap):
                return ap.rearrange("p (c t) -> p c t", c=NCH)

            def act(eng, steps):
                load(eng, "x_back", xT.rearrange("p a b -> p (a b)"), x_dram)
                load(eng, "g2w", g2w, A["g2w"])
                eng.activation(gsig, gdT, ACT.Sigmoid).then_inc(e.of("gate"), 1)
                for hp in range(4):
                    eng.wait_ge(*e("centred", hp + 1))
                    eng.activation(gsq[:, hp, :], gcen[:, hp, :], ACT.Square).then_inc(e.of("squared"), 1)
                for hp in range(4):
                    eng.wait_ge(*e("varied", hp + 1))
                    eng.activation(groot[:, hp % 2, :], gvar[:, hp % 2, :], ACT.Sqrt).then_inc(e.of("rooted"), 1)
                    eng.wait_ge(*e("normed", hp + 1))

            def pe(eng, steps):
                for hp in range(4):
                    eng.matmul(chunked(ps[hp]), ones64, yC[:, :, hp, :], start=True, stop=True).then_inc(e.of("mean"), 1)
                for hp in range(4):
                    eng.wait_ge(*e("squared", hp + 1))
                    eng.matmul(ps[4 + hp], ones64, gsq[:, hp, :], start=True, stop=True).then_inc(e.of("summed"), 1)
                for hp in range(4):
                    eng.wait_ge(*e("keyed", hp + 1))
                    eng.wait_ge(*e("centred", hp + 1))
                    eng.matmul(chunked(ps[hp]), ones64, kka[0][:, 0:NCH, hp, :], start=True, stop=True)\
                       .then_inc(e.of("bonus"), 1)
                arrived(eng, "g2w")
                eng.wait_ge(*e("gate", 1))
                for hp in range(4):
                    eng.wait_ge(*e("varied", hp + 1))
                    eng.matmul(ps[4 + hp], g2w[:, hp * P:(hp + 1) * P], gsig, start=True, stop=True).then_inc(e.of("gated"), 1)

            def dve(eng, steps):
                for hp in range(4):
                    eng.wait_ge(*e("mean", hp + 1))
                    eng.scalar_tensor_tensor(chunked(gcen[:, hp, :]), chunked(ps[hp]), -1.0 / 64, yC[:, :, hp, :],
                                             ALU.mult, ALU.add).then_inc(e.of("centred"), 1)
                for hp in range(4):
                    t = kka[0][:, 0:NCH, hp, :]
                    steps.link(eng.tensor_tensor(t, kd[0][:, 4:12, hp, :], kd[1][:, 4:12, hp, :], ALU.add))
                    eng.scalar_tensor_tensor(t, t, col("r_k", hp), rC[:, :, hp, :], ALU.mult, ALU.mult)\
                       .then_inc(e.of("keyed"), 1)
                eng.wait_ge(*e("centred", 4))
                for hp in range(4):
                    g = gcen[:, hp, :]
                    eng.wait_ge(*e("summed", hp + 1))
                    if hp >= 2:
                        eng.wait_ge(*e("rooted", hp - 1))
                    eng.tensor_scalar(gvar[:, hp % 2, :], ps[4 + hp], 1.0 / 64, 64e-5, ALU.mult, ALU.add).then_inc(e.of("varied"), 1)
                    eng.wait_ge(*e("rooted", hp + 1))
                    steps.link(eng.reciprocal(gvar[:, hp % 2, :], groot[:, hp % 2, :]))
                    steps.link(eng.scalar_tensor_tensor(g, g, col("gn_g", hp), gvar[:, hp % 2, :], ALU.mult, ALU.mult))
                    eng.wait_ge(*e("bonus", hp + 1))
                    steps.link(eng.tensor_tensor(chunked(rwT[:, hp, :]), chunked(ps[hp]), vC[:, 4:12, hp, :], ALU.mult))
                    steps.link(eng.scalar_tensor_tensor(rwT[:, hp, :], g, col("gn_b", hp), rwT[:, hp, :], ALU.add, ALU.add))
                    eng.sem_inc(e.of("normed"), 1)
                arrived(eng, "x_back")
                for hp in range(4):
                    eng.wait_ge(*e("gated", hp + 1))
                    eng.tensor_tensor(rwT[:, hp, :], rwT[:, hp, :], ps[4 + hp], ALU.mult)

            return dict(act=act, pe=pe, dve=dve)

        @stage
        def out2():
            return residual("out2", lambda k: fT[:, k, :] if k < 4 else rwT[:, k - 4, :], gate=lambda m: mod[:, 16 + m, 0:1])

        @stage
        def norm_ffn2():
            return norm(lambda k: xT[:, k, :], lambda k: hT[:, k, 0:S], lambda k: gains[:, 2, k:k + 1],
                        shift=lambda k: mod[:, 24 + k, 0:1])

        r11 = base.remainder()
        act2T = r11.take(FT, S)
        pad = r11.take(4, 10, 66)
        cacc = r11.take(4, 8, 64)
        csil = r11.take(2, S)
        fcw = cols[:, COL0["fc_w"]:COL0["fc_w"] + 396].rearrange("p (k t) -> p k t", k=9)
        fcb = cols[:, COL0["fc_b"]:COL0["fc_b"] + 44]

        @stage
        def ffn2():
            free, padded, convolved, silued, conv_used, used = (sem("f2_" + x) for x in (
                "free", "padded", "convolved", "silued", "conv_used", "used"))
            u0 = UNIT0["ffn2"]
            NI = FT // 2

            def pe(eng, steps):
                linear_pe(eng, u0, 2 * FT, lambda k: hT[:, k, 0:S], free)

            def act(eng, steps):
                def grids(i, f):
                    for j in (2 * f, 2 * f + 1):
                        eng.wait_ge(units_done, u0 + 4 * i + j + 1)
                        eng.wait_ge(conv_used, 4 * i + j + 1)
                        eng.copy(pad[:, j, 1:9, 1:65], ps[j].rearrange("p (y x) -> p y x", y=8)).then_inc(padded, 1)
                        eng.wait_ge(padded, 4 * i + j + 1)
                        eng.sem_inc(free, 1)

                def silu(i, f):
                    eng.wait_ge(convolved, 4 * i + 2 * f + 1)
                    eng.wait_ge(used, 2 * i + f + 1)
                    eng.activation(csil[:, f, :], cacc[:, 2 * f].rearrange("p y x -> p (y x)"), ACT.Silu,
                                   bias=fcb[:, bass.ds(2 * i + f, 1)]).then_inc(silued, 1)

                eng.sem_inc(free, 4)
                grids(0, 0)
                with eng.Fori(0, NI - 1) as i:
                    for f in range(2):
                        grids(i + f, 1 - f)
                        silu(i, f)
                grids(NI - 1, 1)
                silu(NI - 1, 0)
                silu(NI - 1, 1)

            def dve(eng, steps):
                def taps(i, f):
                    for j in (2 * f, 2 * f + 1):
                        eng.wait_ge(padded, 4 * i + j + 1)
                    for tap in range(9):
                        for j in (2 * f, 2 * f + 1):
                            w = fcw[:, tap, bass.ds(2 * i + f + FT * (j % 2), 1)]
                            src = pad[:, j, tap // 3:tap // 3 + 8, tap % 3:tap % 3 + 64]
                            if tap == 0:
                                steps.did(eng.tensor_scalar(cacc[:, j], src, w, None, ALU.mult))
                            else:
                                steps.did_but(1, lambda: eng.scalar_tensor_tensor(cacc[:, j], src, w, cacc[:, j],
                                                                                  ALU.mult, ALU.add))
                    steps.wait()
                    eng.sem_inc(conv_used, 2)
                    eng.sem_inc(convolved, 2)

                def gated(i, f):
                    eng.wait_ge(silued, 2 * i + f + 1)
                    passed(eng, "dve")
                    eng.scalar_tensor_tensor(act2T[:, bass.ds(2 * i + f, 1), :].rearrange("p a t -> p (a t)"),
                                             cacc[:, 2 * f + 1].rearrange("p y x -> p (y x)"),
                                             fcb[:, bass.ds(FT + 2 * i + f, 1)], csil[:, f, :], ALU.add, ALU.mult)\
                       .then_inc(used_dve, 1)
                    eng.wait_ge(used_dve, 2 * i + f + 1)
                    eng.sem_inc(used, 1)

                steps.link(eng.memset(pad, 0.0))
                eng.sem_inc(conv_used, 4)
                eng.sem_inc(used, 2)
                taps(0, 0)
                with steps.loop(NI - 1, 36) as i:
                    for f in range(2):
                        taps(i + f, 1 - f)
                        gated(i, f)
                taps(NI - 1, 1)
                gated(NI - 1, 0)
                gated(NI - 1, 1)

            used_dve = sem("f2_act")
            return dict(pe=pe, act=act, dve=dve)

        @stage
        def down2():
            return residual("down2", lambda k: act2T[:, k, :], ktiles=FT, gate=lambda m: mod[:, 40 + m, 0:1])

        @stage
        def norm_final2():
            return norm(lambda k: xT[:, k, :], lambda k: xT[:, k, :], lambda k: col("fin2_g", k))

        named = dict(locals())
        @block.tensor
        def _(eng):
            run(eng, "pe", Steps(eng, sem("pe_steps")))

        @block.vector
        def _(eng):
            run(eng, "dve", Steps(eng, sem("dve_steps")))

        @block.scalar
        def _(eng):
            run(eng, "act", Steps(eng, sem("act_steps")))

        @block.gpsimd
        def _(eng):
            run(eng, "pool", Steps(eng, sem("pool_steps")))

        @block.sync
        def _(eng):
            for j in range(4):
                eng.dma_start(ring[:, j], units[j]).then_inc(landed[j], 16)
            with eng.Fori(1, nunits // 4) as i:
                for j in range(4):
                    eng.wait_ge(units_done, 4 * i + (j - 3))
                    eng.dma_start(ring[:, j], units[4 * i + j]).then_inc(landed[j], 16)
            eng.wait_ge(stage_done, 4 * len(stages))
            for n, (name, dst) in enumerate(dump or []):
                eng.dma_start(dst, named[name]).then_inc(sem("dumped"), 16)
            if out is not None:
                eng.dma_start(out, xT).then_inc(sem("stored"), 16)
                eng.wait_ge(sem("stored"), 16)
            if dump:
                arrived(eng, *loaded)
                eng.wait_ge(sem("dumped"), 16 * len(dump))



def _tiles(w):
    k, m = w.shape
    kp, mp = -(-k // D) * D, -(-m // P) * P
    full = np.zeros((kp, mp), np.float32)
    full[:k, :m] = w
    return full.reshape(kp // D, 8, P, mp // P, P).transpose(3, 0, 2, 1, 4).reshape(-1, P, 8, P)


def _columns(v):
    return np.ascontiguousarray(v.reshape(-1, P).T)


def t5_bucket(n):
    large = 16 + (np.log(np.maximum(n, 1) / np.float32(16)) / math.log(8) * 16).astype(np.int32)
    return np.where(n < 16, n, np.minimum(large, 31))


def layout(x):
    g = {k: np.asarray(v, np.float32) for k, v in x.items()}
    A = {}
    w = g["w_in"][0]
    cut = np.cumsum([0, 512, 128, 128, 128, 128, 128, 128, 24, 512, 128, 128, 256, 16, 256])
    nq, kc, vc, ks, vs, kw, vw, ng, cu, gq, gk, gv, ga, gr = (w[:, a:b] for a, b in zip(cut[:-1], cut[1:]))
    heads = [h for j in range(NPAIR) for h in (j, NPAIR + j)]
    nq = np.concatenate([nq[:, 64 * h:64 * h + 64] for h in heads], axis=1)
    ga = np.concatenate([ga, np.zeros((D, P - 16), np.float32)], axis=1)
    units = [_tiles(np.concatenate([ks, kw, kc, vc, gq, gk, ga, nq, cu, gr], axis=1))]
    wo = g["w_out"][0]
    wo = np.concatenate([wo[64 * h:64 * h + 64] for h in heads] + [wo[512:]], axis=0)
    units.append(_tiles(wo))

    def pairs(a, b):
        return np.stack([_tiles(a), _tiles(b)], axis=1).reshape(-1, P, 8, P)

    units.append(pairs(g["ffn_w_gate"][0], g["ffn_w_up"][0]))
    units.append(_tiles(g["ffn_w_down"][0]))
    pp = g["ple_w_proj"][0].reshape(2, P, 2, 4, P).transpose(2, 1, 3, 0, 4).reshape(2, P, 8, P)
    units.append(pp)
    units.append(_tiles(g["ple_w_gate"][0]))
    units.append(g["ada_w_2"][0].reshape(4, 2, P, 12, 512).transpose(3, 0, 2, 1, 4).reshape(48, P, 8, P))
    w2 = g["w_in_2"][0]
    units.append(_tiles(np.concatenate([w2[:, 512:], w2[:, :512]], axis=1)))
    units.append(_tiles(g["w_out_2"][0]))
    units.append(pairs(g["ffn_w_up_2"][0][:, :2816], g["ffn_w_up_2"][0][:, 2816:]))
    units.append(_tiles(g["ffn_w_down_2"][0]))
    units = np.concatenate(units)
    A["units"] = np.concatenate([units, np.zeros((NUNITS_PAD - len(units), P, 8, P), np.float32)])
    assert len(units) == NUNITS

    A["wn"] = np.concatenate([vs, vw, gv, ng], axis=1).reshape(8, P, 536).transpose(1, 0, 2)
    A["xT"] = g["x"][0].T.reshape(8, P, S).transpose(1, 0, 2)
    ident = np.eye(P, dtype=np.float32)
    two = np.kron(np.eye(2), np.ones((64, 64))).astype(np.float32)
    A["consts"] = np.concatenate([ident, np.ones((P, P), np.float32), two], axis=1)
    d = 511 - np.arange(640)
    A["onehot"] = (t5_bucket(np.maximum(d, 0))[None, :] == np.arange(32)[:, None]).astype(np.float32)
    A["negmask"] = np.tile(np.where(d < 0, NEG, 0.0).astype(np.float32), (8, 1))
    A["rel_bias"] = g["rel_bias"]
    A["cw1"] = np.stack([g["cmp_w1_" + n][0].reshape(16, P, 256).transpose(1, 0, 2) for n in "kv"])
    A["cw2"] = np.stack([g["cmp_w2_" + n][0].reshape(2, P, 64).transpose(1, 0, 2) for n in "kv"])
    A["gla_wa"] = g["gla_w_alpha"][0]
    A["gl_reset"] = np.tile((np.arange(S) % C != 0).astype(np.float32), (P, 1))
    tri = (np.arange(C)[:, None] <= np.arange(C)[None, :]).astype(np.float32)
    A["gl_mask"] = np.tile(tri, (2, 1))
    A["ctxT"] = g["ctx_2"][0].T.reshape(8, P, CTX).transpose(1, 0, 2)
    A["w_low"] = g["decay_w2_2"][0].reshape(P, 512)
    A["a_low"] = g["iclr_a2_2"][0].reshape(P, 512)
    A["g2w"] = g["gate_g2_2"][0]
    ang = 2 * np.pi * np.outer(np.arange(S), np.arange(S)) % (2 * np.pi * S) / S
    A["dft"] = (np.stack([np.cos(ang), -np.sin(ang)]) / math.sqrt(S)).reshape(2, 4, P, S).transpose(2, 0, 1, 3)
    ang = 2 * np.pi * np.outer(np.arange(C), np.arange(C)) / C
    A["dft64"] = np.concatenate([np.kron(np.eye(2), f(ang) / 8) for f in (np.cos, np.sin)], axis=1)
    s, t = np.arange(C)[:, None], np.arange(C)[None, :]
    before, upto = s < t, s <= t
    fwd = np.stack([before, upto, before.T, before.T])
    rev = np.stack([before.T, upto.T, before, before])
    A["masks"] = np.concatenate([np.stack([fwd, rev]).transpose(2, 0, 1, 3)] * 2, axis=0)
    lv = [-1.0 * (before & (s // 2 == t // 2))]
    for b in (2, 4, 8, 16, 32):
        lv.append(1.0 * (before & (s // (2 * b) == t // (2 * b)) & (s // b != t // b)).T)
    lv = np.stack(lv)
    lv2 = lv.transpose(0, 2, 1)
    A["lev"] = np.concatenate([np.stack([lv, lv2]).transpose(2, 0, 1, 3)] * 2, axis=0)
    A["eye"] = np.tile(np.eye(C), (2, 1))
    A["reset"] = np.tile((np.arange(4 * C) % C != 0), (P, 2, 1))
    A["pT"] = g["p"][0, 0].T.reshape(2, P, S).transpose(1, 0, 2)
    c = {"mix_g": g["mix_norm_g"], "ffn_g": g["ffn_norm_g"], "ple_g": g["ple_norm_g"], "fin_g": g["final_norm_g"],
         "b1k": g["cmp_b1_k"], "b1v": g["cmp_b1_v"], "conv_b": g["conv_b"], "ln_g": g["conv_ln_g"],
         "ln_b": g["conv_ln_b"], "gla_b": g["gla_b_alpha"], "gla_g": g["gla_norm_g"],
         "conv_w": g["conv_w"][0], "posk": g["cmp_pos_k"][0], "posv": g["cmp_pos_v"][0],
         "n1_g": g["norm1_g_2"], "n2_g": g["norm2_g_2"], "fin2_g": g["final_g_2"], "ada_b": g["ada_b_2"],
         "c": np.concatenate([g["c_2"], g["c_ctx_2"][None]]), "rconv": g["rwkv_conv_w_2"][0],
         "w0": g["decay_w0_2"][0], "a0": g["iclr_a0_2"][0], "k_k": g["k_k_2"], "k_a": g["k_a_2"],
         "r_k": g["r_k_2"].reshape(1, 512), "gn_g": g["gn_g_2"], "gn_b": g["gn_b_2"],
         "fc_w": g["ffn_conv_w_2"][0].reshape(9, -1), "fc_b": g["ffn_conv_b_2"],
         "fo_g": g["fourier_g_2"]}
    A["cols"] = np.concatenate([_columns(c[name]) for name, _ in COLS], axis=1)
    return {k: np.ascontiguousarray(v, dtype=np.float32) for k, v in A.items()}



def kernel(**inputs):
    import concourse.bacc as bacc
    from concourse.bass_utils import run_bass_kernel_spmd

    nc = bacc.Bacc("TRN2", target_bir_lowering=False, num_devices=1)
    arrays = {f"in_{k}": v for k, v in layout(inputs).items()}
    A = {k[3:]: nc.dram_tensor(k, v.shape, F32, kind="ExternalInput").ap() for k, v in arrays.items()}
    out = nc.dram_tensor("out_0", (P, KT, S), F32, kind="ExternalOutput").ap()
    build(nc, A, out)
    r = run_bass_kernel_spmd(nc, [arrays], core_ids=[0])
    return np.ascontiguousarray(r.results[0]["out_0"].transpose(2, 1, 0).reshape(1, S, D))
```

```python
import math
from contextlib import ExitStack, contextmanager

import numpy as np

import concourse.bass as bass
from concourse import mybir

F32 = mybir.dt.float32
ALU = mybir.AluOpType
ACT = mybir.ActivationFunctionType
AX = mybir.AxisListType

P = 128
D = 1024
KT = D // P
S = 512
CTX = 256
T2 = CTX + S
EPS = 1e-6
NEG = -1e30
NPAIR = 4
QT = S // P
NCMP = S // 16 - 1
CONV_W = 31
FT = 2816 // P
C = 64
NCH = S // C
TOEP = 639

STREAM = [("in1", 17), ("ada", 48), ("out1", 8), ("ffn1", 2 * FT), ("pleproj", 2), ("down1", 24), ("ple", 8),
          ("in2", 19), ("out2", 8), ("ffn2", 2 * FT), ("down2", 24)]
UNIT0, NUNITS = {}, 0
for _n, _c in STREAM:
    UNIT0[_n] = NUNITS
    NUNITS += _c
NUNITS_PAD = -(-NUNITS // 4) * 4

COLS = [("mix_g", 8), ("ffn_g", 8), ("ple_g", 8), ("fin_g", 8), ("b1k", 2), ("b1v", 2),
        ("posk", 16), ("posv", 16), ("conv_b", 2), ("ln_g", 2), ("ln_b", 2), ("conv_w", 2 * CONV_W),
        ("gla_b", 1), ("gla_g", 2), ("n1_g", 8), ("n2_g", 8), ("fin2_g", 8), ("ada_b", 48),
        ("c", 16), ("rconv", 36), ("w0", 8), ("a0", 8), ("k_k", 4), ("k_a", 4), ("r_k", 4),
        ("gn_g", 4), ("gn_b", 4), ("fc_w", 44 * 9), ("fc_b", 44), ("fo_g", 4)]
COL0, NCOLS = {}, 0
for _n, _c in COLS:
    COL0[_n] = NCOLS
    NCOLS += _c


LOADS = {"start": 6, "compress": 4, "gla": 3, "fourier": 2, "low_rank": 2, "rwkv": 4}


class Steps:

    def __init__(self, eng, sem):
        self.eng, self.sem, self.total, self.index, self.per = eng, sem, 0, None, 0

    def did(self, ins):
        ins.then_inc(self.sem, 1)
        self.total += 1

    def wait(self, engine=None):
        value = self.total if self.index is None else self.index * self.per + self.total
        (engine or self.eng).wait_ge(self.sem, value)

    def did_but(self, n, make):
        value = self.total - n
        self.eng.wait_ge(self.sem, value if self.index is None else self.index * self.per + value)
        self.did(make())

    def link(self, ins):
        self.did(ins)
        self.wait()

    @contextmanager
    def loop(self, n, per):
        with self.eng.Fori(0, n) as i:
            start, self.index, self.per = self.total, i, per
            yield i
            assert self.total - start == per, (self.total - start, per)
        self.index, self.total = None, start + n * per


class Events:

    def __init__(self, sem, tag, orders, alone=()):
        self.sem_of, self.first, self.given = {}, {}, {}
        for engine, order in orders.items():
            n = 0
            for name, count in order:
                self.sem_of[name], self.first[name] = sem(f"{tag}_{engine}"), n
                self.given[name] = [engine, 0, count]
                n += count
        for name in alone:
            self.sem_of[name], self.first[name] = sem(f"{tag}_{name}"), 0
        self.totals = {engine: 0 for engine in orders}

    def of(self, name):
        if name in self.given:
            g = self.given[name]
            assert self.totals[g[0]] == self.first[name] + g[1] and g[1] < g[2], name
            self.totals[g[0]] += 1
            g[1] += 1
        return self.sem_of[name]

    def __call__(self, name, k):
        return self.sem_of[name], self.first[name] + k


def view(ap, offset, dims):
    return bass.AP(ap.tensor, ap.offset + offset, [list(ap.ap[0])] + [list(d) for d in dims])


def build(nc, A, out, upto=99, dump=None, nunits=NUNITS_PAD):
    with ExitStack() as ctx:
        sem_of = {}

        def sem(name):
            if name not in sem_of:
                sem_of[name] = ctx.enter_context(nc.semaphore(name))
            return sem_of[name]

        SB_COLS = 53000
        mem = ctx.enter_context(nc.sbuf_tensor("mem", [P, SB_COLS], F32))
        psum = ctx.enter_context(nc.psum_tensor("psum", [P, 8, 512], F32))
        ps = [psum[:, b, :] for b in range(8)]
        bias_dram = nc.dram_tensor("bias_scratch", [8, TOEP + 1], F32, kind="Internal").ap()
        x_dram = nc.dram_tensor("x_scratch", [P, KT * S], F32, kind="Internal").ap()
        bias_tiles = nc.dram_tensor("bias_tiles", [8, P, S], F32, kind="Internal").ap()

        class Region:
            def __init__(self, start, end):
                self.at, self.end = start, end

            def take(self, *dims):
                n = int(np.prod(dims))
                assert self.at + n <= self.end, (self.at, n, self.end)
                ap = mem[:, self.at:self.at + n]
                self.at += n
                if len(dims) == 1:
                    return ap
                names = "abcd"[:len(dims)]
                return ap.rearrange(f"p ({' '.join(names)}) -> p {' '.join(names)}",
                                    **dict(zip(names, dims)))

            def remainder(self):
                return Region(self.at, self.end)

        base = Region(0, SB_COLS)
        ring = base.take(4, 8, P)
        ident = base.take(P)
        ones = base.take(P)
        ones64 = base.take(P)
        cols = base.take(NCOLS)
        xT = base.take(KT, S)
        hT = base.take(KT, T2)
        sqr = base.take(KT, S)
        mod = base.take(48, 2)
        gains = base.take(3, KT)
        omka = base.take(4)
        rstd = base.take(512)
        rstd2 = base.take(512)

        def col(name, i=0, n=1):
            return cols[:, COL0[name] + i:COL0[name] + i + n]

        r1 = base.remainder()
        assert base.at < 21600, base.at
        zT = r1.take(17, S)
        ZCU, ZKS, ZKW, ZKC, ZVC, ZGQ, ZGK, ZGA, ZQ, ZGR = 0, 4, 5, 6, 7, 8, 9, 10, 11, 15
        znat = r1.take(QT, 512)
        gates = r1.take(QT, 8, 3)
        mixT = r1.take(KT, S)
        mixT_nsa, mixT_conv, mixT_gla = mixT[:, 0:4], mixT[:, 4:6], mixT[:, 6:8]
        kcmpT = r1.take(32)
        vcmp = r1.take(P)
        wn = r1.take(8, 536)
        r_cmp = r1.remainder()
        cw1 = [r_cmp.take(16, 256), r_cmp.take(16, 256)]
        cw2 = [r_cmp.take(2, 64), r_cmp.take(2, 64)]
        swapped = r_cmp.take(2, S)
        blocks = [r_cmp.take(16, 2, NCMP), r_cmp.take(16, 2, NCMP)]
        hid = [r_cmp.take(2, 2 * NCMP), r_cmp.take(2, 2 * NCMP)]
        r_bias = Region(mixT.offset, mixT.offset + KT * S)
        onehot = r_bias.take(640)
        negmask = r_bias.take(640)
        relb = r_bias.take(8)
        bvec = r_bias.take(640)
        assert r_cmp.at <= SB_COLS
        r_att = Region(wn.offset, SB_COLS)
        qs = r_att.take(S)
        bias = r_att.take(2, S)
        sc = [[r_att.take(64), r_att.take(512), r_att.take(512)] for _ in range(3)]
        pt = [[r_att.take(P), r_att.take(512), r_att.take(512)] for _ in range(2)]
        stat = [r_att.take(16) for _ in range(3)]
        r_cv = Region(sqr.offset, sqr.offset + KT * S)
        cvt = r_cv.take(2, S)
        cva = r_cv.take(2, S)
        cvx = r_cv.remainder().take(2, S)
        cvh = r_cv.take(2, 544)
        r_gl = Region(wn.offset, SB_COLS)
        gl_silu = r_gl.take(2, S)
        gl_wa = r_gl.take(P)
        gl_t = [r_gl.take(S) for _ in range(3)]
        gl_reset = r_gl.take(S)
        gl_cum = r_gl.take(S)
        gl_q = r_gl.take(S)
        gl_k = r_gl.take(S)
        gl_dn = r_gl.take(NCH)
        gl_kn = r_gl.take(QT, P)
        gl_mask = r_gl.take(C)
        gl_at4 = r_gl.take(4, QT, C)
        gl_st = r_gl.take(C)
        gl_o = r_gl.take(2, S)
        r_ada = Region(SB_COLS - KT * CTX - 2 * CTX - 12 * 512 - 16, SB_COLS)
        assert r_gl.at <= r_ada.at
        modrow = r_ada.take(12, 512)
        sqc = modrow[:, 0:4, :].rearrange("p a b -> p (a b)").rearrange("p (k t) -> p k t", k=KT)
        cs = r_ada.take(16)
        ctxT = r_ada.take(KT, CTX)
        rstdc = r_ada.take(CTX)
        rstdc2 = r_ada.take(CTX)

        units = A["units"]
        units_done = sem("units_done")
        landed = [sem(f"landed{j}") for j in range(4)]
        stage_done = sem("stage_done")
        loaded = {}

        block = ctx.enter_context(nc.Block())

        stages = []

        built = []

        def stage(f):
            if len(built) < upto:
                built.append(f)
                stages.append([f()])
            return f

        def joined(f):
            if len(built) < upto:
                built.append(f)
                stages[-1].append(f())
            return f

        def run(eng, key, steps):
            for n, parts in enumerate(stages):
                if n:
                    eng.wait_ge(stage_done, 4 * n)
                for part in parts:
                    if key in part:
                        part[key](eng, steps)
                eng.drain().then_inc(stage_done, 1)

        def passed(eng, name):
            eng.sem_inc(sem("passed_" + name), 1)

        def load(eng, name, dst, src):
            eng.dma_start(dst, src).then_inc(sem("ld_" + name), 16)
            loaded[name] = True

        def arrived(eng, *names):
            for name in names:
                eng.wait_ge(sem("ld_" + name), 16 * LOADS.get(name, 1))

        def per_unit(pe, u0, count, use, body=4):
            def one(j, i):
                slot = (u0 + j) % 4
                pe.wait_ge(landed[slot], 16 * ((u0 + j) // 4 + 1 + i * (body // 4)))
                use(slot, j, i).then_inc(units_done, 1)
            looped = 0
            if count // body > 1:
                looped = count // body * body
                with pe.Fori(0, count // body) as i:
                    for j in range(body):
                        one(j, i)
            for j in range(looped, count):
                one(j, 0)

        def product(pe, slot, rhs, dst, ready=None):
            for k in range(8):
                if ready:
                    ready(pe, k)
                last = pe.matmul(dst, ring[:, slot, k, :], rhs(k), start=(k == 0), stop=(k == 7))
            return last

        def linear_pe(pe, u0, count, rhs, bank_free, banks=4, ready=None):
            def use(slot, j, i):
                pe.wait_ge(bank_free, 4 * i + j + 1)
                return product(pe, slot, rhs, ps[j % banks], ready)
            per_unit(pe, u0, count, use)

        norms, residuals = [0, 0, None, 0], [0]

        norm_sems = [sem("norm_" + x) for x in ("squared", "added", "summed", "varied", "rooted", "scaled", "shifted")]

        def norm(src, dst, g, n=S, shift=None, source=None, pooled=True, before_sum=None):
            squared, added, summed, varied, rooted, scaled, shifted = norm_sems
            r, shifts = norms[0], norms[1]
            norms[0] += 1
            norms[1] += KT * (shift is not None)
            pooled = pooled and source is not None
            sums = norms[3] = norms[3] + pooled

            def act(eng, steps):
                if r:
                    eng.wait_ge(summed, r)
                for k in range(KT):
                    if source:
                        source(eng, k)
                    eng.activation(sqr[:, k, 0:n], src(k), ACT.Square).then_inc(squared, 1)
                eng.wait_ge(varied, r + 1)
                eng.activation(rstd2[:, 0:n], rstd[:, 0:n], ACT.Sqrt).then_inc(rooted, 1)
                if shift is not None:
                    for k in range(KT):
                        eng.wait_ge(scaled, KT * r + k + 1)
                        eng.activation(dst(k), dst(k), ACT.Identity, bias=shift(k)).then_inc(shifted, 1)

            def pool(eng, steps):
                for k in range(1, KT - 1):
                    eng.wait_ge(squared, KT * r + k + 1)
                    steps.link(eng.tensor_tensor(sqr[:, 0, 0:n], sqr[:, 0, 0:n], sqr[:, k, 0:n], ALU.add))
                eng.sem_inc(added, 1)

            def pe(eng, steps):
                if before_sum:
                    before_sum(eng)
                if pooled:
                    eng.wait_ge(added, sums)
                    eng.matmul(ps[7][:, 0:n], ones, sqr[:, 0, 0:n], start=True, stop=False)
                    eng.wait_ge(squared, KT * r + KT)
                    last = eng.matmul(ps[7][:, 0:n], ones, sqr[:, KT - 1, 0:n], start=False, stop=True)
                else:
                    for k in range(KT):
                        eng.wait_ge(squared, KT * r + k + 1)
                        last = eng.matmul(ps[7][:, 0:n], ones, sqr[:, k, 0:n], start=(k == 0), stop=(k == KT - 1))
                last.then_inc(summed, 1)

            def dve(eng, steps):
                eng.wait_ge(summed, r + 1)
                eng.tensor_scalar(rstd[:, 0:n], ps[7][:, 0:n], 1.0 / D, EPS, ALU.mult,
                                  ALU.add).then_inc(varied, 1)
                eng.wait_ge(rooted, r + 1)
                steps.link(eng.reciprocal(rstd[:, 0:n], rstd2[:, 0:n]))
                for k in range(KT):
                    eng.scalar_tensor_tensor(dst(k), src(k), g(k), rstd[:, 0:n], ALU.mult,
                                             ALU.mult).then_inc(scaled, 1)

            norms[2] = (scaled, KT * r) if shift is None else (shifted, shifts)
            return dict(act=act, pe=pe, dve=dve, **(dict(pool=pool) if pooled else {}))

        def normed():
            s, n = norms[2]

            def ready(eng, k):
                eng.wait_ge(s, n + k + 1)
            return ready

        @stage
        def start():
            biased, bias_put = sem("biased"), sem("bias_put")

            def act(eng, steps):
                load(eng, "start", mem[:, ident.offset:ident.offset + 3 * P], A["consts"])
                load(eng, "start", xT, A["xT"])
                load(eng, "start", cols, A["cols"])
                load(eng, "start", onehot[0:32, :], A["onehot"])
                load(eng, "start", relb[0:32, :], A["rel_bias"])
                load(eng, "start", negmask[0:8, :], A["negmask"])
                load(eng, "wn", wn, A["wn"])
                for n in range(2):
                    load(eng, "compress", cw1[n], A["cw1"][n])
                    load(eng, "compress", cw2[n], A["cw2"][n])
                eng.wait_ge(bias_put, 1)
                load(eng, "bias_dram", bias_dram, bvec[0:8, :])
                arrived(eng, "bias_dram")
                load(eng, "bias_tiles", bias_tiles,
                     bass.AP(bias_dram.tensor, bias_dram.offset + 127, [[TOEP + 1, 8], [-1, P], [1, S]]))

            def pe(eng, steps):
                arrived(eng, "start")
                for n in range(2):
                    last = eng.matmul(ps[1 + n][0:8, 0:320], relb[0:32, :], onehot[0:32, 320 * n:320 * n + 320],
                                      start=True, stop=True)
                last.then_inc(biased, 1)

            def dve(eng, steps):
                arrived(eng, "start")
                eng.wait_ge(biased, 1)
                for n in range(2):
                    steps.did(eng.tensor_tensor(bvec[0:8, 320 * n:320 * n + 320], ps[1 + n][0:8, 0:320],
                                                negmask[0:8, 320 * n:320 * n + 320], ALU.add))
                steps.wait()
                eng.sem_inc(bias_put, 1)
                arrived(eng, "start")

            return dict(act=act, pe=pe, dve=dve)

        @stage
        def norm1():
            return norm(lambda k: xT[:, k, :], lambda k: hT[:, k, 0:S], lambda k: col("mix_g", k))

        cv = Events(sem, "conv", {
            "act": (("gated", 2), ("squared", 2), ("rooted", 1),),
            "pe": (("meaned", 1), ("summed", 1),),
            "dve": (("convolved", 2), ("centred", 2), ("varied", 1), ("scaled", 2),),
        })

        def conv_gate(eng):
            for m in range(2):
                eng.activation(cvt[:, m, :], zT[:, ZCU + 2 + m, :], ACT.Sigmoid).then_inc(cv.of("gated"), 1)

        def conv_square(eng):
            for m in range(2):
                eng.wait_ge(*cv("centred", m + 1))
                eng.activation(cvt[:, m, :], cvx[:, m, :], ACT.Square).then_inc(cv.of("squared"), 1)

        def conv_swish(eng):
            eng.wait_ge(*cv("varied", 1))
            eng.activation(rstd2, rstd, ACT.Sqrt).then_inc(cv.of("rooted"), 1)
            for m in range(2):
                eng.wait_ge(*cv("scaled", m + 1))
                eng.activation(mixT[:, 4 + m, :], cvx[:, m, :], ACT.Silu, bias=col("ln_b", m))

        def conv_sum(eng, b, src, ready, done):
            for m in range(2):
                eng.wait_ge(*cv(ready, m + 1))
                last = eng.matmul(ps[b], ones, src[:, m, :], start=(m == 0), stop=(m == 1))
            last.then_inc(cv.of(done), 1)

        def conv_taps(eng, steps):
            for m in range(2):
                eng.memset(cvh[:, m, 0:CONV_W - 1], 0.0)
                eng.wait_ge(*cv("gated", m + 1))
                steps.did(eng.tensor_tensor(cvh[:, m, CONV_W - 1:CONV_W - 1 + S], zT[:, ZCU + m, :], cvt[:, m, :],
                                            ALU.mult))
            steps.wait()
            for k in range(CONV_W):
                for m in range(2):
                    w = col("conv_w", 2 * k + m)
                    if k == 0:
                        steps.did(eng.tensor_scalar(cva[:, m, :], cvh[:, m, 0:S], w, col("conv_b", m), ALU.mult, ALU.add))
                        continue
                    tap = lambda: eng.scalar_tensor_tensor(cva[:, m, :], cvh[:, m, k:k + S], w, cva[:, m, :],
                                                           ALU.mult, ALU.add)
                    if k < CONV_W - 1:
                        steps.did_but(1, tap)
                    else:
                        if m == 0:
                            steps.wait()
                        tap().then_inc(cv.of("convolved"), 1)
            eng.wait_ge(*cv("convolved", 2))
            eng.wait_ge(*cv("meaned", 1))
            for m in range(2):
                eng.scalar_tensor_tensor(cvx[:, m, :], ps[1], -1.0 / 256, cva[:, m, :], ALU.mult,
                                         ALU.add).then_inc(cv.of("centred"), 1)

        def conv_scale(eng, steps):
            eng.wait_ge(*cv("summed", 1))
            eng.tensor_scalar(rstd, ps[2], 1.0 / 256, EPS, ALU.mult, ALU.add).then_inc(cv.of("varied"), 1)
            eng.wait_ge(*cv("rooted", 1))
            eng.wait_ge(*cv("centred", 2))
            steps.link(eng.reciprocal(rstd, rstd2))
            for m in range(2):
                eng.scalar_tensor_tensor(cvx[:, m, :], cvx[:, m, :], col("ln_g", m), rstd, ALU.mult,
                                         ALU.mult).then_inc(cv.of("scaled"), 1)

        @joined
        def project1():
            free, nat = sem("in1_free"), sem("in1_nat")
            nat_copied, gates_read = sem("in1_nat_copied"), sem("in1_gates_read")
            u0 = UNIT0["in1"]
            ready = normed()

            def pe(eng, steps):
                linear_pe(eng, u0, 17, lambda k: hT[:, k, 0:S], free, ready=ready)
                eng.wait_ge(free, 20)
                conv_sum(eng, 1, cva, "convolved", "meaned")
                arrived(eng, "wn")
                for t in range(QT):
                    if t >= 2:
                        eng.wait_ge(nat_copied, t - 1)
                        eng.wait_ge(gates_read, t - 1)
                    for k in range(8):
                        eng.matmul(ps[4 + 2 * (t % 2)], hT[:, k, t * P:(t + 1) * P], wn[:, k, 0:512],
                                   start=(k == 0), stop=(k == 7))
                    for k in range(8):
                        last = eng.matmul(ps[5 + 2 * (t % 2)][:, 0:24], hT[:, k, t * P:(t + 1) * P],
                                          wn[:, k, 512:536], start=(k == 0), stop=(k == 7))
                    last.then_inc(nat, 1)
                conv_sum(eng, 2, cvt, "squared", "summed")

            def act(eng, steps):
                def tile(i, j):
                    eng.wait_ge(units_done, u0 + 1 + j + 4 * i)
                    eng.copy(zT[:, 4 * i + j, :], ps[j]).then_inc(free, 1)

                eng.sem_inc(free, 4)
                for j in range(4):
                    tile(0, j)
                eng.wait_ge(free, 8)
                conv_gate(eng)
                with eng.Fori(1, 4) as i:
                    for j in range(4):
                        tile(i, j)
                eng.wait_ge(units_done, u0 + 17)
                eng.copy(zT[:, 16, :], ps[0])
                conv_square(eng)
                for t in range(QT):
                    eng.wait_ge(nat, t + 1)
                    eng.activation(gates[:, t].rearrange("p h b -> p (h b)"), ps[5 + 2 * (t % 2)][:, 0:24],
                                   ACT.Sigmoid).then_inc(gates_read, 1)
                conv_swish(eng)

            def dve(eng, steps):
                conv_taps(eng, steps)
                for t in range(QT):
                    eng.wait_ge(nat, t + 1)
                    eng.tensor_copy(znat[:, t, :], ps[4 + 2 * (t % 2)]).then_inc(nat_copied, 1)
                conv_scale(eng, steps)

            return dict(pe=pe, act=act, dve=dve)

        @stage
        def compress():
            swap, laid, hidden, acted, small = (sem("cmp_" + x) for x in ("swap", "laid", "hidden", "acted", "small"))

            def act(eng, steps):
                for n, z in enumerate((ZKC, ZVC)):
                    eng.dma_start(swapped[0:64, n, :], zT[64:128, z, :]).then_inc(swap, 16)
                    eng.dma_start(swapped[64:128, n, :], zT[0:64, z, :]).then_inc(swap, 16)
                for n in range(2):
                    eng.wait_ge(hidden, n + 1)
                    for m in range(2):
                        eng.activation(hid[n][:, m, :], ps[2 * n + m][:, 0:2 * NCMP], ACT.Silu,
                                       bias=col("b1" + "kv"[n], m)).then_inc(acted, 1)

            def dve(eng, steps):
                eng.wait_ge(swap, 64)
                for n, z in enumerate((ZKC, ZVC)):
                    pos = "pos" + "kv"[n]
                    for par in range(2):
                        lo = 64 * par
                        for g in range(2):
                            src = zT[lo:lo + 64, z, :] if par == g else swapped[lo:lo + 64, n, :]
                            eng.tensor_tensor(blocks[n][lo:lo + 64, :, g, :], view(src, par, [[2, 16], [16, NCMP]]),
                                              view(col(pos)[lo:lo + 64], 0, [[1, 16], [0, NCMP]]),
                                              ALU.add).then_inc(laid, 1)
                eng.wait_ge(small, 1)
                eng.tensor_copy(kcmpT[:, 0:NCMP], ps[4][:, 0:NCMP])
                eng.tensor_copy(vcmp[0:NCMP, :], ps[5][0:NCMP, 0:P])

            def pe(eng, steps):
                arrived(eng, "compress")
                for n in range(2):
                    eng.wait_ge(laid, 4 * n + 4)
                    for m in range(2):
                        for jj in range(16):
                            last = eng.matmul(ps[2 * n + m][:, 0:2 * NCMP], cw1[n][:, jj, m * P:(m + 1) * P],
                                              blocks[n][:, jj].rearrange("p g n -> p (g n)"),
                                              start=(jj == 0), stop=(jj == 15))
                    last.then_inc(hidden, 1)
                eng.wait_ge(acted, 4)
                for g in range(2):
                    for m in range(2):
                        eng.matmul(ps[4][64 * g:64 * g + 64, 0:NCMP], cw2[0][:, m, :],
                                   hid[0][:, m, g * NCMP:(g + 1) * NCMP], start=(m == 0), stop=(m == 1))
                for g in range(2):
                    for m in range(2):
                        last = eng.matmul(ps[5][0:NCMP, 64 * g:64 * g + 64], hid[1][:, m, g * NCMP:(g + 1) * NCMP],
                                          cw2[1][:, m, :], start=(m == 0), stop=(m == 1))
                last.then_inc(small, 1)

            return dict(act=act, dve=dve, pe=pe)

        @stage
        def attention():
            qs_ready, bias_in, scored, read_s, neg, exped, coef, scaled, scaled_sel, turned, kept, kept_sel, summed, y_free = (
                sem("at_" + x) for x in ("qs", "bias", "scored", "read", "neg", "exped", "coef",
                                         "scaled", "scaled_sel", "turned", "kept", "kept_sel", "summed", "yfree"))
            order = [(g, i) for i in range(QT) for g in range(2)]
            NU = len(order)

            def nkeys(i):
                return [8 * i + 7, (i + 1) * P, (i + 1) * P]

            def score_bank(u, b):
                par = u % 2
                return ps[4][:, 64 * par:64 * par + 32] if b == 0 else ps[2 * par + b - 1]

            def pe(eng, steps):
                keys = [kcmpT, zT[:, ZKS, :], zT[:, ZKW, :]]

                def scores(u, j):
                    g, i = order[u]
                    eng.wait_ge(read_s, NU * j + u + 1)
                    eng.wait_ge(kept, NU * j + max(u - 2, 0) + 1)
                    eng.wait_ge(scored, NU * j + u + 1)
                    for b in range(3):
                        n = nkeys(i)[b]
                        last = eng.matmul(score_bank(u, b)[:, 0:n], qs[64 * g:64 * g + 64, i * P:(i + 1) * P],
                                          keys[b][64 * g:64 * g + 64, 0:n], start=True, stop=True)
                    last.then_inc(scored, 1)

                def turn(u, j):
                    g, i = order[u]
                    for s in (scaled, scaled_sel):
                        eng.wait_ge(s, NU * j + u + 1)
                    for s in (kept, kept_sel):
                        eng.wait_ge(s, NU * j + u + 1)
                    eng.wait_ge(read_s, NU * j + min(u + 3, NU) + 1)
                    eng.transpose(ps[4][0:nkeys(i)[0], P:2 * P], sc[u % 3][0][:, 0:nkeys(i)[0]], ident)
                    for b in (1, 2):
                        for kb in range(i + 1):
                            last = eng.transpose(ps[4 + b][:, kb * P:(kb + 1) * P],
                                                 sc[u % 3][b][:, kb * P:(kb + 1) * P], ident)
                    last.then_inc(turned, 1)

                def weigh(u, j):
                    g, i = order[u]
                    for s in (kept, kept_sel):
                        eng.wait_ge(s, NU * j + u + 2)
                    if u == 0:
                        eng.wait_ge(y_free, j + 1)
                    dst = ps[7][64 * g:64 * g + 64, i * P:(i + 1) * P]
                    n = nkeys(i)[0]
                    eng.matmul(dst, vcmp[0:n, 64 * g:64 * g + 64], pt[u % 2][0][0:n, :], start=True, stop=False)
                    for b in (1, 2):
                        for kb in range(i + 1):
                            last = eng.matmul(dst, znat[:, kb, P * (b - 1) + 64 * g:P * (b - 1) + 64 * g + 64],
                                              pt[u % 2][b][:, kb * P:(kb + 1) * P], start=False,
                                              stop=(b == 2 and kb == i))
                    last.then_inc(summed, 1)

                for s in (scored, turned, summed):
                    eng.sem_inc(s, 1)
                with eng.Fori(0, NPAIR) as j:
                    eng.wait_ge(qs_ready, j + 1)
                    for u in range(NU + 3):
                        if u < NU:
                            scores(u, j)
                        if u >= 3:
                            weigh(u - 3, j)
                        if 2 <= u < NU + 2:
                            turn(u - 2, j)

            def dve(eng, steps):
                def maxima(u, j):
                    g, i = order[u]
                    st = stat[u % 3]
                    eng.wait_ge(scored, NU * j + u + 2)
                    eng.wait_ge(turned, NU * j + max(u - 2, 0) + 1)
                    passed(eng, "dve")
                    for b in range(3):
                        n = nkeys(i)[b]
                        at = 415 - 128 * i
                        bb = bias[:, g, at:at + 16 * (n - 1) + 1:16] if b == 0 else bias[:, g, 128 * (3 - i):512]
                        last = eng.tensor_tensor_reduce(sc[u % 3][b][:, 0:n], score_bank(u, b)[:, 0:n], bb, 1.0,
                                                        -1e20, ALU.add, ALU.max, st[:, b:b + 1])
                    last.then_inc(read_s, 1)
                    eng.wait_ge(read_s, NU * j + u + 2)
                    eng.tensor_scalar(st[:, 3:6], st[:, 0:3], -1.0, None, ALU.mult).then_inc(neg, 1)

                def weights(u, j):
                    g, i = order[u]
                    st, n = stat[u % 3], nkeys(i)
                    eng.wait_ge(exped, NU * j + u + 1)
                    steps.link(eng.tensor_scalar(st[:, 9:12], st[:, 6:9], 1e-30, None, ALU.max))
                    steps.link(eng.reciprocal(st[:, 12:15], st[:, 9:12]))
                    eng.tensor_tensor(st[:, 9:12], st[:, 12:15], gates[:, i, 4 * g + j, :], ALU.mult).then_inc(coef, 1)
                    eng.wait_ge(coef, NU * j + u + 1)
                    eng.tensor_scalar(sc[u % 3][0][:, 0:n[0]], sc[u % 3][0][:, 0:n[0]], st[:, 9:10], None, ALU.mult)
                    eng.tensor_scalar(sc[u % 3][2][:, 0:n[2]], sc[u % 3][2][:, 0:n[2]], st[:, 11:12], None,
                                      ALU.mult).then_inc(scaled, 1)

                def keep(u, j):
                    n = nkeys(order[u][1])
                    eng.wait_ge(turned, NU * j + u + 2)
                    eng.wait_ge(summed, NU * j + max(u - 1, 0) + 1)
                    eng.tensor_copy(pt[u % 2][0][0:n[0], :], ps[4][0:n[0], P:2 * P])
                    eng.tensor_copy(pt[u % 2][2][:, 0:n[2]], ps[6][:, 0:n[2]]).then_inc(kept, 1)

                for s in (read_s, kept):
                    eng.sem_inc(s, 1)
                with steps.loop(NPAIR, 2 * NU) as j:
                    eng.wait_ge(bias_in, 32 * j + 32)
                    for u in range(NU + 3):
                        if u >= 3:
                            keep(u - 3, j)
                        if u < NU:
                            maxima(u, j)
                        if 1 <= u <= NU:
                            weights(u - 1, j)

            def pool(eng, steps):
                with eng.Fori(0, NPAIR) as j:
                    for u in range(NU):
                        n = nkeys(order[u][1])[1]
                        eng.wait_ge(coef, NU * j + u + 1)
                        passed(eng, "pool")
                        eng.tensor_scalar(sc[u % 3][1][:, 0:n], sc[u % 3][1][:, 0:n], stat[u % 3][:, 10:11], None,
                                          ALU.mult).then_inc(scaled_sel, 1)

            def act(eng, steps):
                arrived(eng, "bias_tiles")
                for s in (kept_sel, y_free):
                    eng.sem_inc(s, 1)
                with eng.Fori(0, NPAIR) as j:
                    eng.wait_ge(read_s, NU * j + 1)
                    eng.wait_ge(scored, NU * j + 1)
                    for g in range(2):
                        eng.dma_start(bias[:, g, :], bias_tiles[4 * g + j]).then_inc(bias_in, 16)
                    eng.activation(qs[:, :], zT[:, ZQ + j, :], ACT.Copy, scale=0.125).then_inc(qs_ready, 1)
                    for u in range(NU + 3):
                        if u >= 3:
                            n = nkeys(order[u - 3][1])[1]
                            eng.wait_ge(turned, NU * j + u - 1)
                            eng.wait_ge(summed, NU * j + max(u - 4, 0) + 1)
                            eng.copy(pt[(u - 3) % 2][1][:, 0:n], ps[5][:, 0:n]).then_inc(kept_sel, 1)
                        if u < NU:
                            g, i = order[u]
                            st = stat[u % 3]
                            eng.wait_ge(neg, NU * j + u + 1)
                            for b in range(3):
                                n = nkeys(i)[b]
                                last = eng.activation(sc[u % 3][b][:, 0:n], sc[u % 3][b][:, 0:n], ACT.Exp,
                                                      bias=st[:, 3 + b:4 + b], accum_out=st[:, 6 + b:7 + b])
                            last.then_inc(exped, 1)
                    eng.wait_ge(summed, NU * j + NU + 1)
                    eng.copy(mixT[:, j, :], ps[7]).then_inc(y_free, 1)

            return dict(pe=pe, dve=dve, act=act, pool=pool)


        cond, got, turned_, ctx_squared, ctx_summed, ctx_varied, ctx_rooted = (sem("ada_" + x) for x in (
            "cond", "got", "turned", "ctx_squared", "ctx_summed", "ctx_varied", "ctx_rooted"))
        ADA = UNIT0["ada"]

        def ada_start(eng):
            load(eng, "ctxT", ctxT, A["ctxT"])
            eng.activation(cs, col("c", 0, 16), ACT.Silu).then_inc(cond, 1)
            eng.sem_inc(got, 2)

        def ctx_squares(eng):
            arrived(eng, "ctxT")
            for k in range(KT):
                eng.activation(sqc[:, k, :], ctxT[:, k, :], ACT.Square).then_inc(ctx_squared, 1)

        def ctx_sum(eng):
            for k in range(KT):
                eng.wait_ge(ctx_squared, k + 1)
                last = eng.matmul(ps[1][:, 0:CTX], ones, sqc[:, k, :], start=(k == 0), stop=(k == KT - 1))
            last.then_inc(ctx_summed, 1)

        def ada_units(eng, n, count, body=100):
            def use(slot, j, i):
                b, q = (n + j) // 4, (n + j) % 4
                if q == 0:
                    eng.wait_ge(got, 2 * i + b + 1)
                for k in range(2):
                    last = eng.matmul(ps[2 + b % 2][0:2, :], cs[:, 2 * q + k:16:8],
                                      ring[:, slot, 4 * k:4 * k + 4, :].rearrange("p a b -> p (a b)"),
                                      start=(q == 0 and k == 0), stop=(q == 3 and k == 1))
                return last
            per_unit(eng, ADA + n, count, use, body)

        def ada_turn(eng):
            eng.wait_ge(got, 14)
            for t in range(48):
                last = eng.transpose(ps[2][:, 2 * t:2 * t + 2], modrow[0:2, t // 4, P * (t % 4):P * (t % 4) + P],
                                     ident[0:2, 0:2])
            last.then_inc(turned_, 1)

        def ada_row(eng, b, i=0):
            eng.wait_ge(units_done, ADA + 4 * b + 4 + 8 * i)
            eng.copy(modrow[0:2, 2 * i + b, :], ps[2 + b % 2][0:2, :]).then_inc(got, 1)

        def ctx_root(eng, steps):
            eng.wait_ge(ctx_summed, 1)
            eng.tensor_scalar(rstdc2, ps[1][:, 0:CTX], 1.0 / D, EPS, ALU.mult, ALU.add).then_inc(ctx_varied, 1)

        def ada_columns(eng, steps):
            eng.wait_ge(ctx_rooted, 1)
            eng.reciprocal(rstdc, rstdc2)
            eng.wait_ge(turned_, 1)
            steps.link(eng.tensor_tensor(mod, ps[2][:, 0:96].rearrange("p (t v) -> p t v", v=2),
                                         view(col("ada_b"), 0, [[1, 48], [0, 2]]), ALU.add))
            for n, (at, v, g) in enumerate(((8, 0, "n1_g"), (8, 1, "n1_g"), (32, 0, "n2_g"))):
                eng.scalar_tensor_tensor(gains[:, n, :], mod[:, at:at + 8, v], 1.0, col(g, 0, 8), ALU.add, ALU.mult)
            eng.tensor_scalar(omka, col("k_a", 0, 4), -1.0, 1.0, ALU.mult, ALU.add)

        @stage
        def gla():
            e = Events(sem, "gla", {
                "act": (("logged", 1), ("eq", 1), ("decays", 1), ("ek", 1), ("kept", 1), ("silued", 2), ("copied", 2),
                        ("squared", 2), ("rooted", 2)),
                "pe": (("alpha", 1), ("turned", 1), ("attn", 4), ("inter", 1)),
                "dve": (("shifted", 1), ("cummed", 1), ("laid", 2), ("masked", 4), ("added", 4), ("varied", 2)),
            }, alone=("summed", "stated", "updated", "sq_summed"))
            t0, t1, t2 = gl_t

            def act(eng, steps):
                load(eng, "gla", gl_wa[0:16, :], A["gla_wa"])
                load(eng, "gla", gl_reset, A["gl_reset"])
                load(eng, "gla", gl_mask, A["gl_mask"])
                ada_start(eng)
                eng.wait_ge(*e("shifted", 1))
                steps.link(eng.activation(t1, t0, ACT.Abs))
                steps.link(eng.activation(t1, t1, ACT.Exp, scale=-1.0))
                eng.activation(t2, t1, ACT.Ln, bias=ones[:, 0:1]).then_inc(e.of("logged"), 1)
                ctx_squares(eng)
                eng.wait_ge(*e("cummed", 1))
                eng.activation(t1, gl_cum, ACT.Exp, scale=1.0 / 16).then_inc(e.of("eq"), 1)
                eng.activation(gl_dn, gl_cum[:, C - 1:S:C], ACT.Exp, scale=1.0 / 16).then_inc(e.of("decays"), 1)
                eng.activation(t2, gl_cum, ACT.Exp, scale=-1.0 / 16).then_inc(e.of("ek"), 1)
                eng.wait_ge(ctx_varied, 1)
                eng.activation(rstdc2, rstdc2, ACT.Sqrt).then_inc(ctx_rooted, 1)
                ada_row(eng, 0)
                eng.wait_ge(*e("turned", 1))
                eng.copy(gl_kn.rearrange("p t c -> p (t c)"), ps[7]).then_inc(e.of("kept"), 1)
                for m in range(2):
                    eng.activation(gl_silu[:, m, :], zT[:, ZGR + m, :], ACT.Silu).then_inc(e.of("silued"), 1)
                ada_row(eng, 1)
                ada_row(eng, 2)
                eng.wait_ge(*e("summed", NCH))
                for hp in range(2):
                    eng.copy(gl_o[:, hp, :], ps[6 + hp]).then_inc(e.of("copied"), 1)
                for hp in range(2):
                    eng.wait_ge(*e("added", 2 * hp + 2))
                    eng.activation(sqr[:, hp, :], gl_o[:, hp, :], ACT.Square).then_inc(e.of("squared"), 1)
                ada_row(eng, 3)
                for hp in range(2):
                    eng.wait_ge(*e("varied", hp + 1))
                    eng.activation(sqr[:, 2 + hp, :], sqr[:, 4 + hp, :], ACT.Sqrt).then_inc(e.of("rooted"), 1)
                with eng.Fori(0, 4) as i:
                    ada_row(eng, 4, i)
                    ada_row(eng, 5, i)

            def pe(eng, steps):
                arrived(eng, "gla")
                eng.matmul(ps[0], gl_wa[0:16, :], zT[0:16, ZGA, :], start=True, stop=True).then_inc(e.of("alpha"), 1)
                eng.wait_ge(cond, 1)
                ada_units(eng, 0, 4)
                ctx_sum(eng)
                eng.wait_ge(*e("laid", 2))
                for t in range(QT):
                    last = eng.transpose(ps[7][:, t * P:(t + 1) * P], gl_k[:, t * P:(t + 1) * P], ident)
                last.then_inc(e.of("turned"), 1)
                eng.wait_ge(got, 3)
                eng.wait_ge(ctx_rooted, 1)
                for h in range(4):
                    for n in range(NCH):
                        par, t = n % 2, n // 2
                        r = slice(32 * h, 32 * h + 32)
                        last = eng.matmul(ps[h][64 * par:64 * par + 64, t * C:(t + 1) * C], gl_k[r, n * C:(n + 1) * C],
                                          gl_q[r, n * C:(n + 1) * C], start=True, stop=True)
                    last.then_inc(e.of("attn"), 1)
                eng.wait_ge(*e("masked", 4))
                for h in range(4):
                    for n in range(NCH):
                        par, t = n % 2, n // 2
                        r, o = slice(64 * par, 64 * par + 64), 64 * (h % 2)
                        last = eng.matmul(ps[4 + par][o:o + 64, (h // 2) * 256 + t * C:(h // 2) * 256 + (t + 1) * C],
                                          znat[r, t, 256 + C * h:256 + C * h + C], gl_at4[r, h, t, :],
                                          start=True, stop=True)
                last.then_inc(e.of("inter"), 1)
                eng.wait_ge(*e("kept", 1))
                for n in range(NCH):
                    par, t = n % 2, n // 2
                    eng.wait_ge(*e("updated", n + 1))
                    for h in range(4):
                        r, o = slice(32 * h, 32 * h + 32), 64 * (h % 2)
                        last = eng.matmul(ps[6 + h // 2][o:o + 64, n * C:(n + 1) * C], gl_st[r, :],
                                          gl_q[r, n * C:(n + 1) * C], start=True, stop=True)
                    last.then_inc(e.of("summed"), 1)
                    ada_units(eng, 4 + n, 1)
                    for h in range(4):
                        r, o = slice(64 * par, 64 * par + 64), 32 * h
                        last = eng.matmul(ps[par][o:o + 32, 0:C], gl_kn[r, t, o:o + 32],
                                          znat[r, t, 256 + C * h:256 + C * h + C], start=True, stop=True)
                    last.then_inc(e.of("stated"), 1)
                ada_units(eng, 12, 4)
                for hp in range(2):
                    eng.wait_ge(*e("squared", hp + 1))
                    eng.wait_ge(*e("updated", NCH + 1))
                    eng.matmul(ps[hp], ones64, sqr[:, hp, :], start=True, stop=True).then_inc(e.of("sq_summed"), 1)
                ada_units(eng, 16, 32, body=8)
                ada_turn(eng)

            def dve(eng, steps):
                eng.memset(gl_st, 0.0).then_inc(e.of("updated"), 1)
                eng.wait_ge(*e("alpha", 1))
                eng.tensor_scalar(t0, ps[0], col("gla_b"), None, ALU.add).then_inc(e.of("shifted"), 1)
                eng.wait_ge(*e("shifted", 1))
                steps.link(eng.tensor_scalar(gl_q, t0, 0.0, None, ALU.min))
                eng.wait_ge(*e("logged", 1))
                steps.link(eng.tensor_tensor(gl_k, gl_q, t2, ALU.subtract))
                arrived(eng, "gla")
                eng.tensor_tensor_scan(gl_cum, gl_reset, gl_k, 0.0, ALU.mult, ALU.add).then_inc(e.of("cummed"), 1)
                eng.wait_ge(*e("cummed", 1))
                ctx_root(eng, steps)
                eng.wait_ge(*e("eq", 1))
                eng.scalar_tensor_tensor(gl_q, t1, 32.0 ** -0.5, zT[:, ZGQ, :], ALU.mult, ALU.mult).then_inc(e.of("laid"), 1)
                eng.wait_ge(*e("ek", 1))
                eng.tensor_tensor(gl_k, t2, zT[:, ZGK, :], ALU.mult).then_inc(e.of("laid"), 1)
                for h in range(4):
                    eng.wait_ge(*e("attn", h + 1))
                    eng.tensor_tensor(gl_at4[:, h], ps[h][:, 0:QT * C].rearrange("p (t c) -> p t c", t=QT),
                                      view(gl_mask, 0, [[0, QT], [1, C]]), ALU.mult).then_inc(e.of("masked"), 1)
                eng.wait_ge(*e("decays", 1))
                for n in range(NCH):
                    eng.wait_ge(*e("stated", n + 1))
                    eng.wait_ge(*e("summed", n + 1))
                    eng.wait_ge(*e("updated", n + 1))
                    steps.link(eng.tensor_tensor(gl_st, gl_st, ps[n % 2][:, 0:C], ALU.add))
                    eng.tensor_scalar(gl_st, gl_st, gl_dn[:, n:n + 1], None, ALU.mult).then_inc(e.of("updated"), 1)
                eng.wait_ge(*e("inter", 1))
                for hp in range(2):
                    eng.wait_ge(*e("copied", hp + 1))
                    for par in range(2):
                        o = view(gl_o[:, hp, :], par * C, [[2 * C, QT], [1, C]])
                        eng.tensor_tensor(o, o, ps[4 + par][:, hp * 256:hp * 256 + 256].rearrange(
                            "p (t c) -> p t c", t=QT), ALU.add).then_inc(e.of("added"), 1)
                for hp in range(2):
                    eng.wait_ge(*e("sq_summed", hp + 1))
                    eng.tensor_scalar(sqr[:, 4 + hp, :], ps[hp], 1.0 / 64, EPS, ALU.mult, ALU.add).then_inc(e.of("varied"), 1)
                for hp in range(2):
                    eng.wait_ge(*e("rooted", hp + 1))
                    steps.link(eng.reciprocal(sqr[:, 6 + hp, :], sqr[:, 2 + hp, :]))
                    steps.link(eng.scalar_tensor_tensor(gl_o[:, hp, :], gl_o[:, hp, :], col("gla_g", hp),
                                                        sqr[:, 6 + hp, :], ALU.mult, ALU.mult))
                    eng.wait_ge(*e("silued", hp + 1))
                    eng.tensor_tensor(mixT[:, 6 + hp, :], gl_o[:, hp, :], gl_silu[:, hp, :], ALU.mult)
                ada_columns(eng, steps)

            return dict(act=act, pe=pe, dve=dve)

        def residual(tag, rhs, ktiles=8, gate=None, ready=None):
            free = sem("residual_free")
            u0, per, r = UNIT0[tag], -(-ktiles // 8), 12 * residuals[0]
            residuals[0] += 1

            def pe(eng, steps):
                def use(slot, j, i):
                    m, part = j // per, j % per
                    if part == 0:
                        eng.wait_ge(free, r + 4 * i + m + 1)
                    for k in range(8 * part, min(8 * part + 8, ktiles)):
                        if ready:
                            ready(eng, k)
                        last = eng.matmul(ps[m % 4], ring[:, slot, k - 8 * part, :], rhs(k), start=(k == 0),
                                          stop=(k == ktiles - 1))
                    return last
                per_unit(eng, u0, 8 * per, use, body=4 * per)

            def dve(eng, steps):
                eng.sem_inc(free, 4)
                with eng.Fori(0, 2) as i:
                    for m in range(4):
                        eng.wait_ge(units_done, u0 + per * (m + 1) + 4 * per * i)
                        x = xT[:, 4 * i + m, :]
                        if gate is None:
                            ins = eng.tensor_tensor(x, x, ps[m], ALU.add)
                        else:
                            ins = eng.scalar_tensor_tensor(x, ps[m], gate(4 * i + m), x, ALU.mult, ALU.add)
                        ins.then_inc(free, 1)

            return dict(pe=pe, dve=dve)

        def added():
            s, n = sem("residual_free"), 12 * (residuals[0] - 1) + 4

            def source(eng, k):
                eng.wait_ge(s, n + k + 1)
            return source

        @stage
        def out1():
            return residual("out1", lambda k: mixT[:, k, :])

        r2 = base.remainder()
        actT = r2.take(FT, S)
        sil = r2.take(2, S)

        @joined
        def norm_ffn():
            return norm(lambda k: xT[:, k, :], lambda k: hT[:, k, 0:S], lambda k: col("ffn_g", k), source=added())

        @joined
        def ffn1():
            free_gate, free_up, silued, used = (sem("f1_" + x) for x in ("free_gate", "free_up", "silued", "used"))
            u0 = UNIT0["ffn1"]
            ready = normed()

            def pe(eng, steps):
                def use(slot, j, i):
                    eng.wait_ge((free_gate, free_up)[j % 2], 2 * i + j // 2 + 1)
                    return product(eng, slot, lambda k: hT[:, k, 0:S], ps[j], ready)
                per_unit(eng, u0, 2 * FT, use)

            def act(eng, steps):
                eng.sem_inc(free_gate, 2)
                with eng.Fori(0, FT // 2) as i:
                    for f in range(2):
                        eng.wait_ge(units_done, u0 + 4 * i + 2 * f + 1)
                        eng.wait_ge(used, 2 * i + f + 1)
                        eng.activation(sil[:, f, :], ps[2 * f], ACT.Silu).then_inc(silued, 1)
                        eng.wait_ge(silued, 2 * i + f + 1)
                        eng.sem_inc(free_gate, 1)

            def dve(eng, steps):
                eng.sem_inc(free_up, 2)
                eng.sem_inc(used, 2)
                with eng.Fori(0, FT // 2) as i:
                    for f in range(2):
                        eng.wait_ge(units_done, u0 + 4 * i + 2 * f + 2)
                        eng.wait_ge(silued, 2 * i + f + 1)
                        eng.tensor_tensor(actT[:, 2 * i + f, :], sil[:, f, :], ps[2 * f + 1], ALU.mult).then_inc(free_up, 1)
                        eng.wait_ge(free_up, 2 * i + f + 3)
                        eng.sem_inc(used, 1)

            return dict(pe=pe, act=act, dve=dve)

        r3 = r2.remainder()
        pT = r3.take(2, S)
        pj = r3.take(KT, S)
        gt = r3.take(4, S)

        @joined
        def ple_project():
            free = sem("pp_free")
            u0 = UNIT0["pleproj"]

            def pe(eng, steps):
                arrived(eng, "pT")

                def use(slot, j, i):
                    for m in range(4):
                        eng.wait_ge(free, 4 * j + m + 1)
                        for k in range(2):
                            last = eng.matmul(ps[4 + m], ring[:, slot, 2 * m + k, :], pT[:, k, :], start=(k == 0),
                                              stop=(k == 1))
                    return last
                per_unit(eng, u0, 2, use)

            def act(eng, steps):
                load(eng, "pT", pT, A["pT"])
                eng.sem_inc(free, 4)
                for j in range(2):
                    eng.wait_ge(units_done, u0 + j + 1)
                    for m in range(4):
                        eng.copy(pj[:, 4 * j + m, :], ps[4 + m]).then_inc(free, 1)

            return dict(pe=pe, act=act)

        @joined
        def down1():
            used = sem("f1_used")

            def ready(eng, k):
                if k == 0:
                    eng.wait_ge(used, 2 + FT)
            return residual("down1", lambda k: actT[:, k, :], ktiles=FT, ready=ready)

        @joined
        def norm_ple():
            return norm(lambda k: xT[:, k, :], lambda k: hT[:, k, 0:S], lambda k: col("ple_g", k), source=added(),
                        before_sum=lambda eng: eng.wait_ge(sem("pp_free"), 12))

        @joined
        def ple_gate():
            free, sig, mixed = sem("pg_free"), sem("pg_sig"), sem("pg_mixed")
            u0 = UNIT0["ple"]
            ready = normed()

            def pe(eng, steps):
                linear_pe(eng, u0, 8, lambda k: hT[:, k, 0:S], free, ready=ready)

            def act(eng, steps):
                eng.sem_inc(free, 4)
                with eng.Fori(0, 2) as i:
                    for m in range(4):
                        eng.wait_ge(units_done, u0 + 4 * i + m + 1)
                        eng.wait_ge(mixed, 4 * i + m + 1)
                        eng.activation(gt[:, m, :], ps[m], ACT.Sigmoid).then_inc(sig, 1)
                        eng.wait_ge(sig, 4 * i + m + 1)
                        eng.sem_inc(free, 1)

            def dve(eng, steps):
                eng.sem_inc(mixed, 4)
                with steps.loop(2, 4) as i:
                    for m in range(4):
                        eng.wait_ge(sig, 4 * i + m + 1)
                        steps.link(eng.tensor_tensor(gt[:, m, :], gt[:, m, :], pj[:, 4 * i + m, :], ALU.mult))
                        eng.tensor_tensor(xT[:, 4 * i + m, :], xT[:, 4 * i + m, :], gt[:, m, :], ALU.add)\
                           .then_inc(mixed, 1)

            return dict(pe=pe, act=act, dve=dve)

        @joined
        def norm_final1():
            return norm(lambda k: xT[:, k, :], lambda k: xT[:, k, :], lambda k: col("fin_g", k),
                        source=lambda eng, k: eng.wait_ge(sem("pg_mixed"), 4 + k + 1))


        r4 = base.remainder()
        rC = r4.take(NCH, 4, C)
        kC = r4.take(12, 4, C)
        vC = r4.take(12, 4, C)
        kkC = r4.take(12, 4, C)
        yC = r4.take(NCH, 4, C)
        fT = r4.take(4, S)
        gdT = r4.take(S)
        r5 = r4.remainder()
        RAW = T2 + 3
        raw = r5.take(12, RAW)
        dft = r5.take(2, 4, S)
        r6 = r4.remainder()
        sig = [r6.take(12, 4, C) for _ in range(2)]
        kka = [r6.take(12, 4, C) for _ in range(2)]
        kd0 = r6.take(12, 4, C)
        kd = [kd0, kC]
        r7 = Region(hT.offset, hT.offset + KT * T2)
        lw = r7.take(T2)
        la = r7.take(T2)
        aT = r7.take(2, T2)
        mixed = Region(r7.end - 4096, r7.end).take(4, 2, S)
        lowT = sqr[:, 0:3, :].rearrange("p a b -> p (a b)")
        dft64 = sqr[:, 3, 0:256]
        r8 = Region(yC.offset, yC.offset + NCH * 4 * C)
        wl = r8.take(512)
        al = r8.take(512)
        r9 = Region(raw.offset, raw.offset + 4 * RAW)
        kroot = r9.take(2, T2)
        ksq = r9.take(2, T2)
        krec = Region(raw.offset + 4 * RAW, raw.offset + 6 * RAW).take(2, T2)

        @joined
        def norm_x():
            s, n = norms[2]
            return norm(lambda k: xT[:, k, :], lambda k: hT[:, k, CTX:T2], lambda k: gains[:, 0, k:k + 1],
                        shift=lambda k: mod[:, k, 0:1], source=lambda eng, k: eng.wait_ge(s, n + k + 1), pooled=False)

        ctx_scaled, ctx_shifted = sem("ctx_scaled"), sem("ctx_shifted")

        @joined
        def norm_ctx():
            def dve(eng, steps):
                for k in range(KT):
                    eng.scalar_tensor_tensor(hT[:, k, 0:CTX], ctxT[:, k, :], gains[:, 1, k:k + 1], rstdc, ALU.mult,
                                             ALU.mult).then_inc(ctx_scaled, 1)

            def act(eng, steps):
                for k in range(KT):
                    eng.wait_ge(ctx_scaled, k + 1)
                    eng.activation(hT[:, k, 0:CTX], hT[:, k, 0:CTX], ACT.Identity, bias=mod[:, k, 1:2]).then_inc(ctx_shifted, 1)

            return dict(dve=dve, act=act)

        low_rank_waits = []

        @joined
        def project2():
            free, free_ctx, tapped = sem("in2_free"), sem("in2_free_ctx"), sem("in2_tapped")
            scaled_, squared, summed, varied, rooted = (sem("kk_" + x) for x in (
                "scaled", "squared", "summed", "varied", "rooted"))
            u0 = UNIT0["in2"]
            ready = normed()
            both = range(4, 14)

            def dest(m):
                if m < 12:
                    return raw[:, m, CTX + 2:CTX + 2 + S], raw[:, m, 1:1 + CTX]
                if m < 14:
                    return lowT[:, (m - 12) * T2 + CTX:(m - 11) * T2], lowT[:, (m - 12) * T2:(m - 12) * T2 + CTX]
                return (gdT, None) if m == 14 else (fT[:, m - 15, :], None)

            def pieces(m):
                q, hp = m // 4, m % 4
                dst = (rC, kC, vC)[q]
                lo = 0 if q == 0 else 4
                out_ = [(dst[:, lo:lo + NCH, hp, :], raw[:, m, CTX + 1:CTX + 1 + S], NCH)]
                if q:
                    out_.append((dst[:, 0:4, hp, :], raw[:, m, 0:CTX], 4))
                return out_

            def pe(eng, steps):
                def use(m):
                    def f(slot, j, i):
                        eng.wait_ge(free, m + 1)
                        last = product(eng, slot, lambda k: hT[:, k, CTX:T2], ps[m % 4], ready)
                        if m in both:
                            eng.wait_ge(free_ctx, m - 3)
                            last = product(eng, slot, lambda k: hT[:, k, 0:CTX], ps[4 + m % 4][:, 0:CTX],
                                           lambda eng, k: eng.wait_ge(ctx_shifted, k + 1))
                        return last
                    return f

                def key_sums(hp):
                    eng.wait_ge(squared, hp + 1)
                    if hp >= 2:
                        eng.wait_ge(varied, hp - 1)
                    b = 4 + 2 * (hp % 2)
                    eng.matmul(ps[b], ones64, ksq[:, hp % 2, 0:512], start=True, stop=True)
                    eng.matmul(ps[b + 1][:, 0:256], ones64, ksq[:, hp % 2, 512:T2], start=True, stop=True).then_inc(summed, 1)

                for m in range(19):
                    per_unit(eng, u0 + m, 1, use(m))
                    if m in (15, 17):
                        eng.wait_ge(free_ctx, 14)
                        for hp in (m - 15, m - 14):
                            key_sums(hp)

            def act(eng, steps):
                taps = [0]

                def first_taps(m):
                    eng.wait_ge(free, m + 5)
                    eng.wait_ge(free_ctx, max(m - 3, 0) + 4)
                    for dst, src, n in pieces(m):
                        eng.activation(dst, view(src, 0, [[C, n], [1, C]]), ACT.Copy, scale=col("rconv", m)).then_inc(tapped, 1)

                def key_squares(hp):
                    eng.wait_ge(scaled_, hp + 1)
                    if hp >= 2:
                        eng.wait_ge(summed, hp - 1)
                        eng.wait_ge(varied, hp + 1 - 2)
                    eng.activation(ksq[:, hp % 2, :].rearrange("p (c t) -> p c t", c=12), kkC[:, :, hp, :], ACT.Square)\
                       .then_inc(squared, 1)

                def key_roots(hp):
                    eng.wait_ge(varied, hp + 1)
                    eng.activation(kroot[:, hp % 2, :], kroot[:, hp % 2, :], ACT.Sqrt).then_inc(rooted, 1)

                eng.wait_ge(ctx_shifted, 8)
                load(eng, "x_out", x_dram, xT.rearrange("p a b -> p (a b)"))
                load(eng, "fourier", dft, A["dft"])
                load(eng, "fourier", dft64, A["dft64"])
                load(eng, "low_rank", wl[:, :], A["w_low"])
                load(eng, "low_rank", al[:, :], A["a_low"])
                eng.sem_inc(free, 4)
                for m in range(19):
                    eng.wait_ge(units_done, u0 + m + 1)
                    eng.copy(dest(m)[0], ps[m % 4]).then_inc(free, 1)
                    if 1 <= m <= 12:
                        first_taps(m - 1)
                    if m == 14:
                        key_squares(0)
                        key_squares(1)
                    if m == 16:
                        key_roots(0)
                        key_roots(1)
                        key_squares(2)
                        key_squares(3)
                key_roots(2)
                key_roots(3)

            def dve(eng, steps):
                for at in (0, CTX + 1, RAW - 1):
                    steps.did(eng.memset(raw[:, :, at:at + 1], 0.0))
                steps.wait()
                eng.sem_inc(free_ctx, 4)
                n_ = 0
                for m in range(14):
                    if m in both:
                        eng.wait_ge(units_done, u0 + m + 1)
                        eng.tensor_copy(dest(m)[1], ps[4 + m % 4][:, 0:CTX]).then_inc(free_ctx, 1)
                    for dst, src, n in pieces(m - 1) if 1 <= m <= 12 else ():
                        n_ += 1
                        eng.wait_ge(tapped, n_)
                        for tap in (1, 2):
                            steps.link(eng.scalar_tensor_tensor(dst, view(src, tap, [[C, n], [1, C]]),
                                                                col("rconv", 12 * tap + m - 1), dst, ALU.mult, ALU.add))
                for hp in range(4):
                    eng.tensor_scalar(kkC[:, :, hp, :], kC[:, :, hp, :], col("k_k", hp), None, ALU.mult).then_inc(scaled_, 1)
                eng.wait_ge(scaled_, 4)
                for hp0 in (0, 2):
                    for hp in (hp0, hp0 + 1):
                        b = 4 + 2 * (hp % 2)
                        eng.wait_ge(summed, hp + 1)
                        if hp >= 2:
                            steps.wait()
                        eng.tensor_scalar(kroot[:, hp % 2, 0:512], ps[b], 1e-12, None, ALU.add)
                        eng.tensor_scalar(kroot[:, hp % 2, 512:T2], ps[b + 1][:, 0:256], 1e-12, None, ALU.add).then_inc(varied, 1)
                    for hp in (hp0, hp0 + 1):
                        eng.wait_ge(rooted, hp + 1)
                        steps.link(eng.reciprocal(krec[:, hp % 2, :], kroot[:, hp % 2, :]))
                        steps.did(eng.tensor_tensor(kkC[:, :, hp, :], kkC[:, :, hp, :],
                                                    krec[:, hp % 2, :].rearrange("p (c t) -> p c t", c=12), ALU.mult))
                steps.wait()

            return dict(pe=pe, act=act, dve=dve)

        @joined
        def fourier():
            e = Events(sem, "fourier", {
                "act": (("firsts", 16), ("squared", 4), ("rooted", 1),),
                "pe": (("first", 16), ("second", 4), ("summed", 1),),
                "dve": (("varied", 1), ("out", 4)),
            })
            projected = sem("in2_free")

            def act(eng, steps):
                eng.wait_ge(*e("first", 1))
                eng.activation(lw, lowT[:, 0:T2], ACT.Tanh)
                eng.copy(la, lowT[:, T2:2 * T2]).then_inc(sem("low_moved"), 1)
                for n in range(16):
                    ct, tt = n // 4, n % 4
                    eng.wait_ge(*e("first", n + 1))
                    for q in range(2):
                        last = eng.copy(mixed[:, tt, q, ct * P:(ct + 1) * P], ps[n % 4][:, q * P:(q + 1) * P])
                    last.then_inc(e.of("firsts"), 1)
                for ct in range(4):
                    eng.wait_ge(*e("second", ct + 1))
                    eng.activation(sqr[:, 4 + ct, :], ps[4 + ct], ACT.Square).then_inc(e.of("squared"), 1)
                eng.wait_ge(*e("varied", 1))
                eng.activation(rstd2, rstd, ACT.Sqrt).then_inc(e.of("rooted"), 1)

            def pe(eng, steps):
                arrived(eng, "fourier")
                eng.wait_ge(projected, 23)
                for n in range(16):
                    ct, tt = n // 4, n % 4
                    if n >= 4:
                        eng.wait_ge(*e("firsts", n - 3))
                    eng.matmul(ps[n % 4][:, 0:256], fT[:, ct, tt * P:(tt + 1) * P], dft64, start=True, stop=True)\
                       .then_inc(e.of("first"), 1)
                eng.wait_ge(*e("firsts", 16))
                eng.wait_ge(sem("kk_varied"), 4)
                for ct in range(4):
                    for tt in range(4):
                        for q in range(2):
                            last = eng.matmul(ps[4 + ct], mixed[:, tt, q, ct * P:(ct + 1) * P], dft[:, q, tt, :],
                                              start=(tt + q == 0), stop=(tt == 3 and q == 1))
                    last.then_inc(e.of("second"), 1)
                for ct in range(4):
                    eng.wait_ge(*e("squared", ct + 1))
                    last = eng.matmul(ps[0], ones, sqr[:, 4 + ct, :], start=(ct == 0), stop=(ct == 3))
                last.then_inc(e.of("summed"), 1)

            def dve(eng, steps):
                eng.wait_ge(*e("summed", 1))
                eng.tensor_scalar(rstd, ps[0], 1.0 / 512, EPS, ALU.mult, ALU.add).then_inc(e.of("varied"), 1)
                eng.wait_ge(*e("rooted", 1))
                steps.link(eng.reciprocal(rstd, rstd2))
                for ct in range(4):
                    eng.scalar_tensor_tensor(fT[:, ct, :], ps[4 + ct], col("fo_g", ct), rstd, ALU.mult, ALU.mult)\
                       .then_inc(e.of("out"), 1)

            low_rank_waits.append((e("varied", 1), e("out", 4)))
            return dict(act=act, pe=pe, dve=dve)

        @joined
        def low_rank():
            made, read, rated, used = (sem("lr_" + x) for x in ("made", "read", "rated", "used"))

            def pe(eng, steps):
                arrived(eng, "low_rank")
                eng.wait_ge(sem("low_moved"), 1)
                varied, written = low_rank_waits[0]
                eng.wait_ge(*varied)
                n = 0
                for d in range(2):
                    r = slice(64 * d, 64 * d + 64)
                    for hp in range(4):
                        for wgt, src in ((wl, lw), (al, la)):
                            b = 2 * (n % 4)
                            if n >= 4:
                                eng.wait_ge(read, n - 3)
                            elif n == 2:
                                eng.wait_ge(*written)
                            w = wgt[r, hp * P:(hp + 1) * P]
                            eng.matmul(ps[b], w, src[r, 0:512], start=True, stop=True)
                            eng.matmul(ps[b + 1][:, 0:256], w, src[r, 512:T2], start=True, stop=True).then_inc(made, 1)
                            n += 1

            def act(eng, steps):
                n = 0
                for d in range(2):
                    for hp in range(4):
                        b = 2 * (n % 4)
                        eng.wait_ge(made, n + 1)
                        bias = col("w0", 4 * d + hp)
                        eng.activation(sig[d][:, 0:8, hp, :], ps[b].rearrange("p (c t) -> p c t", c=8), ACT.Sigmoid, bias=bias)
                        eng.activation(sig[d][:, 8:12, hp, :], ps[b + 1][:, 0:256].rearrange("p (c t) -> p c t", c=4),
                                       ACT.Sigmoid, bias=bias).then_inc(read, 1)
                        n += 1
                        b = 2 * (n % 4)
                        eng.wait_ge(made, n + 1)
                        k = 4 * d + hp
                        if k >= 2:
                            eng.wait_ge(used, k - 1)
                        bias = col("a0", k)
                        eng.activation(aT[:, k % 2, 0:512], ps[b], ACT.Sigmoid, bias=bias).then_inc(rated, 1)
                        eng.activation(aT[:, k % 2, 512:T2], ps[b + 1][:, 0:256], ACT.Sigmoid, bias=bias).then_inc(read, 1)
                        n += 1

            def dve(eng, steps):
                for d in range(2):
                    for hp in range(4):
                        k = 4 * d + hp
                        eng.wait_ge(read, 2 * k + 2)
                        a = aT[:, k % 2, :].rearrange("p (c t) -> p c t", c=12)
                        steps.link(eng.tensor_tensor(kka[d][:, :, hp, :], kkC[:, :, hp, :], a, ALU.mult))
                        steps.link(eng.tensor_scalar(a, a, col("k_a", hp), omka[:, hp:hp + 1], ALU.mult, ALU.add))
                        eng.tensor_tensor(kd[d][:, :, hp, :], kC[:, :, hp, :], a, ALU.mult).then_inc(used, 1)

            return dict(act=act, pe=pe, dve=dve)

        free_regions = [Region(hT.offset, hT.offset + KT * T2), Region(sqr.offset, sqr.offset + KT * S),
                        Region(xT.offset, xT.offset + KT * S),
                        Region(r6.at, SB_COLS)]

        def stage_take(*dims):
            for r in free_regions:
                if r.at + int(np.prod(dims)) <= r.end:
                    return r.take(*dims)
            raise AssertionError(dims)

        G = 4 * C
        masks = stage_take(2, 4, C)
        lev = stage_take(2, 6, C)
        eye = stage_take(C)
        reset = stage_take(2, G)
        st_ = []
        for d in range(2):
            st_.append(dict(
                cum=stage_take(4, C), prev=stage_take(4, C), e1=stage_take(4, C), e2=stage_take(4, C),
                e3=stage_take(4, C), ar=stage_take(4, 2, C), bT=stage_take(4, C), kT=stage_take(4, C),
                vT=stage_take(4, C), ab=stage_take(2, 4, C), kv=stage_take(2, 4, C), g1=stage_take(4, 2, C),
                g2=stage_take(2, 4, C), T=stage_take(4, C), Tt=stage_take(4, C), Z=stage_take(4, C),
                wtb=stage_take(2, 4, C), U=stage_take(4, C), M=stage_take(4, C)))
        DEC = math.exp(-0.5)

        def bc(ap, n=4):
            return view(ap, 0, [[0, n], [1, C]])

        @stage
        def rwkv():
            e = [{n: sem(f"rwkv_{n}{d}") for n in (
                "cum", "prev",
                "ex",
                "laid", "laid2",
                "raw",
                "masked",
                "made", "kept",
                "acted",
                "fed",
                "y", "yc", "mc",
                )} for d in range(2)]
            HB = (slice(0, 64), slice(64, 128))

            def walk(eng, steps, body, per=None):
                for n, base_, y in ((4, 0, False), (8, 4, True)):
                    if per:
                        with steps.loop(n, per(y)) as i:
                            body(i + base_, i + base_, (3 if not y else 11) - i, y)
                    else:
                        with eng.Fori(0, n) as i:
                            body(i + base_, i + base_, (3 if not y else 11) - i, y)

            def pe(eng, steps):
                def each(fn):
                    for hp in range(4):
                        for b in range(2):
                            last = fn(hp, HB[b])
                    return last

                def body(it, c0, c1, y):
                    for d in range(2):
                        s, q, B = st_[d], e[d], ps[4 * d:4 * d + 4]
                        eng.wait_ge(q["laid"], it + 1)
                        eng.wait_ge(q["laid2"], it + 2)
                        eng.wait_ge(q["mc"], it + 1)
                        if y:
                            eng.wait_ge(q["yc"], it - 4)
                        eng.wait_ge(q["acted"], 3 * it)
                        passed(eng, "pe")
                        each(lambda hp, r: eng.matmul(B[0][r, hp * C:(hp + 1) * C], s["ar"][r, hp, 0, :], ident[r, r], start=True, stop=True))
                        each(lambda hp, r: eng.matmul(B[0][r, G + hp * C:G + (hp + 1) * C], s["bT"][r, hp, :], ident[r, r], start=True, stop=True))
                        each(lambda hp, r: eng.matmul(B[1][r, hp * C:(hp + 1) * C], s["kT"][r, hp, :], ident[r, r], start=True, stop=True))
                        each(lambda hp, r: eng.matmul(B[1][r, G + hp * C:G + (hp + 1) * C], s["vT"][r, hp, :], ident[r, r], start=True, stop=True)
                             ).then_inc(q["raw"], 1)
                        n = 2 if y else 1
                        each(lambda hp, r: eng.matmul(B[2][r, hp * 2 * C:hp * 2 * C + n * C], s["bT"][r, hp, :],
                                                      s["ar"][r, hp, 0:n, :].rearrange("p a t -> p (a t)"), start=True, stop=True))
                        last = each(lambda hp, r: eng.matmul(B[3][r, hp * C:(hp + 1) * C], s["ar"][r, hp, 0, :],
                                                             s["kT"][r, hp, :], start=True, stop=True))
                        if y:
                            last = each(lambda hp, r: eng.matmul(B[3][r, G + hp * C:G + (hp + 1) * C], s["kT"][r, hp, :],
                                                                 s["ar"][r, hp, 1, :], start=True, stop=True))
                        last.then_inc(q["raw"], 1)
                    for lv in range(5):
                        for d in range(2):
                            s, q, B = st_[d], e[d], ps[4 * d:4 * d + 4]
                            if lv == 0:
                                eng.wait_ge(q["acted"], 3 * it + 1)
                                eng.wait_ge(q["masked"], 2 * it + 1)
                            else:
                                eng.wait_ge(q["kept"], 10 * it + 2 * lv)
                            passed(eng, "pe")
                            each(lambda hp, r: eng.matmul(B[0][r, hp * C:(hp + 1) * C], s["g1"][r, hp, 0, :], s["T"][r, hp, :],
                                                          start=True, stop=True)).then_inc(q["made"], 1)
                        for d in range(2):
                            s, q, B = st_[d], e[d], ps[4 * d:4 * d + 4]
                            eng.wait_ge(q["kept"], 10 * it + 2 * lv + 1)
                            passed(eng, "pe")
                            a, b_ = (s["Tt"], s["Z"]) if lv < 4 else (s["Z"], s["Tt"])
                            each(lambda hp, r: eng.matmul(B[1][r, hp * C:(hp + 1) * C], a[r, hp, :], b_[r, hp, :],
                                                          start=True, stop=True)).then_inc(q["made"], 1)
                    for d in range(2):
                        s, q, B = st_[d], e[d], ps[4 * d:4 * d + 4]
                        eng.wait_ge(q["kept"], 10 * it + 10)
                        eng.wait_ge(q["masked"], 2 * it + 2)
                        passed(eng, "pe")
                        each(lambda hp, r: eng.matmul(B[2][r, hp * C:(hp + 1) * C], s["ab"][r, 0, hp, :], s["Tt"][r, hp, :],
                                                      start=True, stop=True))
                        each(lambda hp, r: eng.matmul(B[2][r, G + hp * C:G + (hp + 1) * C], s["g2"][r, 0, hp, :],
                                                      s["Tt"][r, hp, :], start=True, stop=True)).then_inc(q["fed"], 1)
                    for d in range(2):
                        s, q, B = st_[d], e[d], ps[4 * d:4 * d + 4]
                        eng.wait_ge(q["acted"], 3 * it + 2)
                        passed(eng, "pe")

                        def u(hp, r):
                            eng.matmul(B[3][r, hp * C:(hp + 1) * C], s["wtb"][r, 0, hp, :], s["M"][r, hp, :], start=True,
                                       stop=False)
                            return eng.matmul(B[3][r, hp * C:(hp + 1) * C], s["wtb"][r, 1, hp, :], s["kv"][r, 1, hp, :],
                                              start=False, stop=True)
                        each(u).then_inc(q["fed"], 1)
                    for d in range(2):
                        s, q, B = st_[d], e[d], ps[4 * d:4 * d + 4]
                        eng.wait_ge(q["acted"], 3 * it + 3)
                        passed(eng, "pe")
                        if y:
                            def yy(hp, r):
                                dst = B[0][r, hp * C:(hp + 1) * C]
                                eng.matmul(dst, s["M"][r, hp, :], s["ar"][r, hp, 1, :], start=True, stop=False)
                                eng.matmul(dst, s["U"][r, hp, :], s["g1"][r, hp, 1, :], start=False, stop=False)
                                return eng.matmul(dst, s["kv"][r, 1, hp, :], s["g2"][r, 1, hp, :], start=False, stop=True)
                            each(yy).then_inc(q["y"], 1)

                        def mm(hp, r):
                            dst = B[1][r, hp * C:(hp + 1) * C]
                            eng.matmul(dst, s["ab"][r, 1, hp, :], s["U"][r, hp, :], start=True, stop=False)
                            return eng.matmul(dst, s["kv"][r, 0, hp, :], s["kv"][r, 1, hp, :], start=False, stop=True)
                        each(mm).then_inc(q["fed"], 1)
                for q in e:
                    eng.sem_inc(q["fed"], 1)
                walk(eng, steps, body)

            def flat(ap):
                return ap.rearrange("p h t -> p (h t)")

            def dve(eng, steps):
                arrived(eng, "rwkv")
                eng.memset(yC, 0.0)
                arrived(eng, "x_out")
                for d in range(2):
                    eng.memset(st_[d]["M"], 0.0).then_inc(e[d]["mc"], 1)

                def body(it, c0, c1, y):
                    for d, c in enumerate((c0, c1)):
                        s, q = st_[d], e[d]
                        eng.wait_ge(q["ex"], it + 1)
                        passed(eng, "dve")
                        eng.tensor_tensor_scan(flat(s["cum"]), reset[:, 0, :], flat(sig[d][:, c]), 0.0,
                                               ALU.mult, ALU.add).then_inc(q["cum"], 1)
                        eng.wait_ge(q["cum"], it + 1)
                        passed(eng, "dve")
                        if d:
                            steps.link(eng.tensor_tensor(s["prev"], view(s["cum"][:, 0, C - 1:C], 0, [[C, 4], [0, C]]), s["cum"],
                                                         ALU.subtract))
                            eng.tensor_tensor(s["cum"], s["prev"], sig[d][:, c], ALU.add).then_inc(q["prev"], 1)
                        else:
                            eng.tensor_tensor(s["prev"], s["cum"], sig[d][:, c], ALU.subtract).then_inc(q["prev"], 1)
                    for d, c in enumerate((c0, c1)):
                        s, q = st_[d], e[d]
                        eng.wait_ge(q["ex"], it + 2)
                        eng.wait_ge(q["fed"], 3 * it + 1)
                        passed(eng, "dve")
                        last = eng.tensor_tensor(s["bT"], kka[d][:, c], s["e2"], ALU.mult)
                        if y:
                            last = eng.tensor_tensor(s["ar"][:, :, 1, :], rC[:, c - 4], s["e3"], ALU.mult)
                        last.then_inc(q["laid"], 1)
                    for d in range(2):
                        s, q, B = st_[d], e[d], ps[4 * d:4 * d + 4]
                        eng.wait_ge(q["raw"], 2 * it + 2)
                        n = 2 if y else 1
                        mk = masks[:, d]
                        steps.did(eng.tensor_tensor(s["g1"][:, :, 0:n, :], B[2].rearrange("p (h n t) -> p h n t", h=4, n=2)[:, :, 0:n, :],
                                                    view(mk[:, 0:2, :], 0, [[0, 4], [C, n], [1, C]]), ALU.mult))
                        steps.wait()
                        steps.link(eng.tensor_tensor(s["Z"], s["g1"][:, :, 0, :], bc(lev[:, d, 0, :]), ALU.mult))
                        steps.link(eng.tensor_tensor(s["Tt"], s["Z"], bc(eye), ALU.add))
                        eng.transpose(flat(s["T"]), flat(s["Tt"])).then_inc(q["masked"], 1)
                        last = eng.tensor_tensor(s["g2"][:, 0], B[3][:, 0:G].rearrange("p (h t) -> p h t", h=4),
                                                 bc(mk[:, 2, :]), ALU.mult)
                        if y:
                            last = eng.tensor_tensor(s["g2"][:, 1], B[3][:, G:2 * G].rearrange("p (h t) -> p h t", h=4),
                                                     bc(mk[:, 1, :]), ALU.mult)
                        last.then_inc(q["masked"], 1)
                    for lv in range(5):
                        for d in range(2):
                            s, q, B = st_[d], e[d], ps[4 * d:4 * d + 4]
                            eng.wait_ge(q["made"], 10 * it + 2 * lv + 1)
                            eng.tensor_tensor(s["Z"], B[0][:, 0:G].rearrange("p (h t) -> p h t", h=4),
                                              bc(lev[:, d, 1 + lv, :]), ALU.mult).then_inc(q["kept"], 1)
                        for d in range(2):
                            s, q, B = st_[d], e[d], ps[4 * d:4 * d + 4]
                            eng.wait_ge(q["made"], 10 * it + 2 * lv + 2)
                            x = B[1][:, 0:G].rearrange("p (h t) -> p h t", h=4)
                            if lv < 4:
                                steps.link(eng.tensor_tensor(s["T"], s["T"], x, ALU.subtract))
                                if lv < 4:
                                    eng.transpose(flat(s["Tt"]), flat(s["T"])).then_inc(q["kept"], 1)
                            else:
                                eng.tensor_tensor(s["Tt"], s["Tt"], x, ALU.subtract).then_inc(q["kept"], 1)
                    for d, c in enumerate((c0, c1)):
                        s, q, B = st_[d], e[d], ps[4 * d:4 * d + 4]
                        if y:
                            eng.wait_ge(q["y"], it - 3)
                            passed(eng, "dve")
                            yy = yC[:, c - 4]
                            eng.tensor_tensor(yy, yy, B[0][:, 0:G].rearrange("p (h t) -> p h t", h=4), ALU.add).then_inc(q["yc"], 1)
                        eng.wait_ge(q["fed"], 3 * it + 4)
                        steps.link(eng.tensor_tensor(s["M"], s["M"], B[1][:, 0:G].rearrange("p (h t) -> p h t", h=4), ALU.add))
                        at = 0 if d else C - 1
                        eng.tensor_tensor(s["M"], s["M"], view(s["e3"][:, 0, at:at + 1], 0, [[C, 4], [0, C]]),
                                          ALU.mult).then_inc(q["mc"], 1)
                walk(eng, steps, body, per=lambda y: 17)

            def act(eng, steps):
                def body(it, c0, c1, y):
                    for d in range(2):
                        s, q = st_[d], e[d]
                        eng.wait_ge(q["prev"], it + 1)
                        eng.wait_ge(q["laid2"], it + 1)
                        eng.wait_ge(q["mc"], it + 1)
                        eng.activation(flat(s["e1"]), flat(s["prev"]), ACT.Exp, scale=-DEC)
                        eng.activation(flat(s["e2"]), flat(s["cum"]), ACT.Exp, scale=DEC)
                        eng.activation(flat(s["e3"]), flat(s["cum"]), ACT.Exp, scale=-DEC).then_inc(q["ex"], 1)
                    for d in range(2):
                        s, q, B = st_[d], e[d], ps[4 * d:4 * d + 4]
                        eng.wait_ge(q["raw"], 2 * it + 1)
                        eng.copy(s["ab"].rearrange("p a h t -> p (a h t)"), B[0])
                        eng.copy(s["kv"].rearrange("p a h t -> p (a h t)"), B[1]).then_inc(q["acted"], 1)
                    for d in range(2):
                        s, q, B = st_[d], e[d], ps[4 * d:4 * d + 4]
                        eng.wait_ge(q["fed"], 3 * it + 2)
                        eng.copy(s["wtb"].rearrange("p a h t -> p (a h t)"), B[2]).then_inc(q["acted"], 1)
                    for d in range(2):
                        s, q, B = st_[d], e[d], ps[4 * d:4 * d + 4]
                        eng.wait_ge(q["fed"], 3 * it + 3)
                        eng.activation(flat(s["U"]), B[3][:, 0:G], ACT.Copy, scale=-1.0).then_inc(q["acted"], 1)
                arrived(eng, "x_out")
                load(eng, "rwkv", masks, A["masks"])
                load(eng, "rwkv", lev, A["lev"])
                load(eng, "rwkv", eye, A["eye"])
                load(eng, "rwkv", reset, A["reset"])
                for q in e:
                    eng.sem_inc(q["ex"], 1)
                walk(eng, steps, body)

            def pool(eng, steps):
                def body(it, c0, c1, y):
                    for d, c in enumerate((c0, c1)):
                        s, q = st_[d], e[d]
                        eng.wait_ge(q["fed"], 3 * it + 1)
                        passed(eng, "pool")
                        eng.tensor_copy(s["vT"], vC[:, c])
                        eng.wait_ge(q["ex"], it + 2)
                        passed(eng, "pool")
                        eng.tensor_tensor(s["ar"][:, :, 0, :], kkC[:, c], s["e1"], ALU.mult)
                        eng.tensor_tensor(s["kT"], kd[d][:, c], s["e2"], ALU.mult).then_inc(q["laid2"], 1)
                for q in e:
                    eng.sem_inc(q["laid2"], 1)
                walk(eng, steps, body)

            return dict(pe=pe, dve=dve, act=act, pool=pool)

        r9 = Region(hT.offset, hT.offset + KT * T2)
        rwT = r9.take(4, S)
        gcen = r9.take(4, S)
        g2w = r9.take(512)
        gsig = r9.take(S)
        r10 = Region(sqr.offset, sqr.offset + KT * S)
        gsq = r10.take(4, S)
        gvar = r10.take(2, S)
        groot = r10.take(2, S)

        @stage
        def rwkv_out():
            e = Events(sem, "rwout", {
                "act": (("gate", 1), ("squared", 4), ("rooted", 4)),
                "pe": (("mean", 4), ("summed", 4), ("bonus", 4), ("gated", 4)),
                "dve": (("centred", 4), ("keyed", 4)),
            }, alone=("varied", "normed"))

            def chunked(ap):
                return ap.rearrange("p (c t) -> p c t", c=NCH)

            def act(eng, steps):
                load(eng, "x_back", xT.rearrange("p a b -> p (a b)"), x_dram)
                load(eng, "g2w", g2w, A["g2w"])
                eng.activation(gsig, gdT, ACT.Sigmoid).then_inc(e.of("gate"), 1)
                for hp in range(4):
                    eng.wait_ge(*e("centred", hp + 1))
                    eng.activation(gsq[:, hp, :], gcen[:, hp, :], ACT.Square).then_inc(e.of("squared"), 1)
                for hp in range(4):
                    eng.wait_ge(*e("varied", hp + 1))
                    eng.activation(groot[:, hp % 2, :], gvar[:, hp % 2, :], ACT.Sqrt).then_inc(e.of("rooted"), 1)
                    eng.wait_ge(*e("normed", hp + 1))

            def pe(eng, steps):
                for hp in range(4):
                    eng.matmul(chunked(ps[hp]), ones64, yC[:, :, hp, :], start=True, stop=True).then_inc(e.of("mean"), 1)
                for hp in range(4):
                    eng.wait_ge(*e("squared", hp + 1))
                    eng.matmul(ps[4 + hp], ones64, gsq[:, hp, :], start=True, stop=True).then_inc(e.of("summed"), 1)
                for hp in range(4):
                    eng.wait_ge(*e("keyed", hp + 1))
                    eng.wait_ge(*e("centred", hp + 1))
                    eng.matmul(chunked(ps[hp]), ones64, kka[0][:, 0:NCH, hp, :], start=True, stop=True)\
                       .then_inc(e.of("bonus"), 1)
                arrived(eng, "g2w")
                eng.wait_ge(*e("gate", 1))
                for hp in range(4):
                    eng.wait_ge(*e("varied", hp + 1))
                    eng.matmul(ps[4 + hp], g2w[:, hp * P:(hp + 1) * P], gsig, start=True, stop=True).then_inc(e.of("gated"), 1)

            def dve(eng, steps):
                for hp in range(4):
                    eng.wait_ge(*e("mean", hp + 1))
                    eng.scalar_tensor_tensor(chunked(gcen[:, hp, :]), chunked(ps[hp]), -1.0 / 64, yC[:, :, hp, :],
                                             ALU.mult, ALU.add).then_inc(e.of("centred"), 1)
                for hp in range(4):
                    t = kka[0][:, 0:NCH, hp, :]
                    steps.link(eng.tensor_tensor(t, kd[0][:, 4:12, hp, :], kd[1][:, 4:12, hp, :], ALU.add))
                    eng.scalar_tensor_tensor(t, t, col("r_k", hp), rC[:, :, hp, :], ALU.mult, ALU.mult)\
                       .then_inc(e.of("keyed"), 1)
                eng.wait_ge(*e("centred", 4))
                for hp in range(4):
                    g = gcen[:, hp, :]
                    eng.wait_ge(*e("summed", hp + 1))
                    if hp >= 2:
                        eng.wait_ge(*e("rooted", hp - 1))
                    eng.tensor_scalar(gvar[:, hp % 2, :], ps[4 + hp], 1.0 / 64, 64e-5, ALU.mult, ALU.add).then_inc(e.of("varied"), 1)
                    eng.wait_ge(*e("rooted", hp + 1))
                    steps.link(eng.reciprocal(gvar[:, hp % 2, :], groot[:, hp % 2, :]))
                    steps.link(eng.scalar_tensor_tensor(g, g, col("gn_g", hp), gvar[:, hp % 2, :], ALU.mult, ALU.mult))
                    eng.wait_ge(*e("bonus", hp + 1))
                    steps.link(eng.tensor_tensor(chunked(rwT[:, hp, :]), chunked(ps[hp]), vC[:, 4:12, hp, :], ALU.mult))
                    steps.link(eng.scalar_tensor_tensor(rwT[:, hp, :], g, col("gn_b", hp), rwT[:, hp, :], ALU.add, ALU.add))
                    eng.sem_inc(e.of("normed"), 1)
                arrived(eng, "x_back")
                for hp in range(4):
                    eng.wait_ge(*e("gated", hp + 1))
                    eng.tensor_tensor(rwT[:, hp, :], rwT[:, hp, :], ps[4 + hp], ALU.mult)

            return dict(act=act, pe=pe, dve=dve)

        @stage
        def out2():
            return residual("out2", lambda k: fT[:, k, :] if k < 4 else rwT[:, k - 4, :], gate=lambda m: mod[:, 16 + m, 0:1])

        @joined
        def norm_ffn2():
            return norm(lambda k: xT[:, k, :], lambda k: hT[:, k, 0:S], lambda k: gains[:, 2, k:k + 1], source=added(),
                        shift=lambda k: mod[:, 24 + k, 0:1])

        r11 = base.remainder()
        act2T = r11.take(FT, S)
        pad = r11.take(4, 10, 66)
        cacc = r11.take(4, 8, 64)
        csil = r11.take(2, S)
        fcw = cols[:, COL0["fc_w"]:COL0["fc_w"] + 396].rearrange("p (k t) -> p k t", k=9)
        fcb = cols[:, COL0["fc_b"]:COL0["fc_b"] + 44]

        @joined
        def ffn2():
            free, padded, convolved, silued, conv_used, used = (sem("f2_" + x) for x in (
                "free", "padded", "convolved", "silued", "conv_used", "used"))
            u0 = UNIT0["ffn2"]
            NI = FT // 2
            ready = normed()

            def pe(eng, steps):
                linear_pe(eng, u0, 2 * FT, lambda k: hT[:, k, 0:S], free, ready=ready)

            def act(eng, steps):
                def grids(i, f):
                    for j in (2 * f, 2 * f + 1):
                        eng.wait_ge(units_done, u0 + 4 * i + j + 1)
                        eng.wait_ge(conv_used, 4 * i + j + 1)
                        eng.copy(pad[:, j, 1:9, 1:65], ps[j].rearrange("p (y x) -> p y x", y=8)).then_inc(padded, 1)
                        eng.wait_ge(padded, 4 * i + j + 1)
                        eng.sem_inc(free, 1)

                def silu(i, f):
                    eng.wait_ge(convolved, 4 * i + 2 * f + 1)
                    eng.wait_ge(used, 2 * i + f + 1)
                    eng.activation(csil[:, f, :], cacc[:, 2 * f].rearrange("p y x -> p (y x)"), ACT.Silu,
                                   bias=fcb[:, bass.ds(2 * i + f, 1)]).then_inc(silued, 1)

                eng.sem_inc(free, 4)
                grids(0, 0)
                with eng.Fori(0, NI - 1) as i:
                    for f in range(2):
                        grids(i + f, 1 - f)
                        silu(i, f)
                grids(NI - 1, 1)
                silu(NI - 1, 0)
                silu(NI - 1, 1)

            def dve(eng, steps):
                def taps(i, f):
                    for j in (2 * f, 2 * f + 1):
                        eng.wait_ge(padded, 4 * i + j + 1)
                    for tap in range(9):
                        for j in (2 * f, 2 * f + 1):
                            w = fcw[:, tap, bass.ds(2 * i + f + FT * (j % 2), 1)]
                            src = pad[:, j, tap // 3:tap // 3 + 8, tap % 3:tap % 3 + 64]
                            if tap == 0:
                                steps.did(eng.tensor_scalar(cacc[:, j], src, w, None, ALU.mult))
                            else:
                                steps.did_but(1, lambda: eng.scalar_tensor_tensor(cacc[:, j], src, w, cacc[:, j],
                                                                                  ALU.mult, ALU.add))
                    steps.wait()
                    eng.sem_inc(conv_used, 2)
                    eng.sem_inc(convolved, 2)

                def gated(i, f):
                    eng.wait_ge(silued, 2 * i + f + 1)
                    passed(eng, "dve")
                    eng.scalar_tensor_tensor(act2T[:, bass.ds(2 * i + f, 1), :].rearrange("p a t -> p (a t)"),
                                             cacc[:, 2 * f + 1].rearrange("p y x -> p (y x)"),
                                             fcb[:, bass.ds(FT + 2 * i + f, 1)], csil[:, f, :], ALU.add, ALU.mult)\
                       .then_inc(used_dve, 1)
                    eng.wait_ge(used_dve, 2 * i + f + 1)
                    eng.sem_inc(used, 1)

                steps.link(eng.memset(pad, 0.0))
                eng.sem_inc(conv_used, 4)
                eng.sem_inc(used, 2)
                taps(0, 0)
                with steps.loop(NI - 1, 36) as i:
                    for f in range(2):
                        taps(i + f, 1 - f)
                        gated(i, f)
                taps(NI - 1, 1)
                gated(NI - 1, 0)
                gated(NI - 1, 1)

            used_dve = sem("f2_act")
            return dict(pe=pe, act=act, dve=dve)

        @joined
        def down2():
            used = sem("f2_used")

            def ready(eng, k):
                eng.wait_ge(used, 2 + min(k + 1, FT))
            return residual("down2", lambda k: act2T[:, k, :], ktiles=FT, gate=lambda m: mod[:, 40 + m, 0:1], ready=ready)

        @joined
        def norm_final2():
            return norm(lambda k: xT[:, k, :], lambda k: xT[:, k, :], lambda k: col("fin2_g", k), source=added())

        named = dict(locals())
        @block.tensor
        def _(eng):
            run(eng, "pe", Steps(eng, sem("pe_steps")))

        @block.vector
        def _(eng):
            run(eng, "dve", Steps(eng, sem("dve_steps")))

        @block.scalar
        def _(eng):
            run(eng, "act", Steps(eng, sem("act_steps")))

        @block.gpsimd
        def _(eng):
            run(eng, "pool", Steps(eng, sem("pool_steps")))

        @block.sync
        def _(eng):
            for j in range(4):
                eng.dma_start(ring[:, j], units[j]).then_inc(landed[j], 16)
            with eng.Fori(1, nunits // 4) as i:
                for j in range(4):
                    eng.wait_ge(units_done, 4 * i + (j - 3))
                    eng.dma_start(ring[:, j], units[4 * i + j]).then_inc(landed[j], 16)
            eng.wait_ge(stage_done, 4 * len(stages))
            for n, (name, dst) in enumerate(dump or []):
                eng.dma_start(dst, named[name]).then_inc(sem("dumped"), 16)
            if out is not None:
                eng.dma_start(out, xT).then_inc(sem("stored"), 16)
                eng.wait_ge(sem("stored"), 16)
            if dump:
                arrived(eng, *loaded)
                eng.wait_ge(sem("dumped"), 16 * len(dump))



def _tiles(w):
    k, m = w.shape
    kp, mp = -(-k // D) * D, -(-m // P) * P
    full = np.zeros((kp, mp), np.float32)
    full[:k, :m] = w
    return full.reshape(kp // D, 8, P, mp // P, P).transpose(3, 0, 2, 1, 4).reshape(-1, P, 8, P)


def _columns(v):
    return np.ascontiguousarray(v.reshape(-1, P).T)


def t5_bucket(n):
    large = 16 + (np.log(np.maximum(n, 1) / np.float32(16)) / math.log(8) * 16).astype(np.int32)
    return np.where(n < 16, n, np.minimum(large, 31))


def layout(x):
    g = {k: np.asarray(v, np.float32) for k, v in x.items()}
    A = {}
    w = g["w_in"][0]
    cut = np.cumsum([0, 512, 128, 128, 128, 128, 128, 128, 24, 512, 128, 128, 256, 16, 256])
    nq, kc, vc, ks, vs, kw, vw, ng, cu, gq, gk, gv, ga, gr = (w[:, a:b] for a, b in zip(cut[:-1], cut[1:]))
    heads = [h for j in range(NPAIR) for h in (j, NPAIR + j)]
    nq = np.concatenate([nq[:, 64 * h:64 * h + 64] for h in heads], axis=1)
    ga = np.concatenate([ga, np.zeros((D, P - 16), np.float32)], axis=1)
    units = {}
    units["in1"] = _tiles(np.concatenate([cu, ks, kw, kc, vc, gq, gk, ga, nq, gr], axis=1))
    wo = g["w_out"][0]
    wo = np.concatenate([wo[64 * h:64 * h + 64] for h in heads] + [wo[512:]], axis=0)
    units["out1"] = _tiles(wo)

    def pairs(a, b):
        return np.stack([_tiles(a), _tiles(b)], axis=1).reshape(-1, P, 8, P)

    units["ffn1"] = pairs(g["ffn_w_gate"][0], g["ffn_w_up"][0])
    units["down1"] = _tiles(g["ffn_w_down"][0])
    pp = g["ple_w_proj"][0].reshape(2, P, 2, 4, P).transpose(2, 1, 3, 0, 4).reshape(2, P, 8, P)
    units["pleproj"] = pp
    units["ple"] = _tiles(g["ple_w_gate"][0])
    units["ada"] = g["ada_w_2"][0].reshape(4, 2, P, 12, 512).transpose(3, 0, 2, 1, 4).reshape(48, P, 8, P)
    w2 = g["w_in_2"][0]
    units["in2"] = _tiles(np.concatenate([w2[:, 512:], w2[:, :512]], axis=1))
    units["out2"] = _tiles(g["w_out_2"][0])
    units["ffn2"] = pairs(g["ffn_w_up_2"][0][:, :2816], g["ffn_w_up_2"][0][:, 2816:])
    units["down2"] = _tiles(g["ffn_w_down_2"][0])
    units = np.concatenate([units[name] for name, _ in STREAM])
    A["units"] = np.concatenate([units, np.zeros((NUNITS_PAD - len(units), P, 8, P), np.float32)])
    assert len(units) == NUNITS

    A["wn"] = np.concatenate([vs, vw, gv, ng], axis=1).reshape(8, P, 536).transpose(1, 0, 2)
    A["xT"] = g["x"][0].T.reshape(8, P, S).transpose(1, 0, 2)
    ident = np.eye(P, dtype=np.float32)
    two = np.kron(np.eye(2), np.ones((64, 64))).astype(np.float32)
    A["consts"] = np.concatenate([ident, np.ones((P, P), np.float32), two], axis=1)
    d = 511 - np.arange(640)
    A["onehot"] = (t5_bucket(np.maximum(d, 0))[None, :] == np.arange(32)[:, None]).astype(np.float32)
    A["negmask"] = np.tile(np.where(d < 0, NEG, 0.0).astype(np.float32), (8, 1))
    A["rel_bias"] = g["rel_bias"]
    A["cw1"] = np.stack([g["cmp_w1_" + n][0].reshape(16, P, 256).transpose(1, 0, 2) for n in "kv"])
    A["cw2"] = np.stack([g["cmp_w2_" + n][0].reshape(2, P, 64).transpose(1, 0, 2) for n in "kv"])
    A["gla_wa"] = g["gla_w_alpha"][0]
    A["gl_reset"] = np.tile((np.arange(S) % C != 0).astype(np.float32), (P, 1))
    tri = (np.arange(C)[:, None] <= np.arange(C)[None, :]).astype(np.float32)
    A["gl_mask"] = np.tile(tri, (2, 1))
    A["ctxT"] = g["ctx_2"][0].T.reshape(8, P, CTX).transpose(1, 0, 2)
    A["w_low"] = g["decay_w2_2"][0].reshape(P, 512)
    A["a_low"] = g["iclr_a2_2"][0].reshape(P, 512)
    A["g2w"] = g["gate_g2_2"][0]
    ang = 2 * np.pi * np.outer(np.arange(S), np.arange(S)) % (2 * np.pi * S) / S
    A["dft"] = (np.stack([np.cos(ang), -np.sin(ang)]) / math.sqrt(S)).reshape(2, 4, P, S).transpose(2, 0, 1, 3)
    ang = 2 * np.pi * np.outer(np.arange(C), np.arange(C)) / C
    A["dft64"] = np.concatenate([np.kron(np.eye(2), f(ang) / 8) for f in (np.cos, np.sin)], axis=1)
    s, t = np.arange(C)[:, None], np.arange(C)[None, :]
    before, upto = s < t, s <= t
    fwd = np.stack([before, upto, before.T, before.T])
    rev = np.stack([before.T, upto.T, before, before])
    A["masks"] = np.concatenate([np.stack([fwd, rev]).transpose(2, 0, 1, 3)] * 2, axis=0)
    lv = [-1.0 * (before & (s // 2 == t // 2))]
    for b in (2, 4, 8, 16, 32):
        lv.append(1.0 * (before & (s // (2 * b) == t // (2 * b)) & (s // b != t // b)).T)
    lv = np.stack(lv)
    lv2 = lv.transpose(0, 2, 1)
    A["lev"] = np.concatenate([np.stack([lv, lv2]).transpose(2, 0, 1, 3)] * 2, axis=0)
    A["eye"] = np.tile(np.eye(C), (2, 1))
    A["reset"] = np.tile((np.arange(4 * C) % C != 0), (P, 2, 1))
    A["pT"] = g["p"][0, 0].T.reshape(2, P, S).transpose(1, 0, 2)
    c = {"mix_g": g["mix_norm_g"], "ffn_g": g["ffn_norm_g"], "ple_g": g["ple_norm_g"], "fin_g": g["final_norm_g"],
         "b1k": g["cmp_b1_k"], "b1v": g["cmp_b1_v"], "conv_b": g["conv_b"], "ln_g": g["conv_ln_g"],
         "ln_b": g["conv_ln_b"], "gla_b": g["gla_b_alpha"], "gla_g": g["gla_norm_g"],
         "conv_w": g["conv_w"][0], "posk": g["cmp_pos_k"][0], "posv": g["cmp_pos_v"][0],
         "n1_g": g["norm1_g_2"], "n2_g": g["norm2_g_2"], "fin2_g": g["final_g_2"], "ada_b": g["ada_b_2"],
         "c": np.concatenate([g["c_2"], g["c_ctx_2"][None]]), "rconv": g["rwkv_conv_w_2"][0],
         "w0": g["decay_w0_2"][0], "a0": g["iclr_a0_2"][0], "k_k": g["k_k_2"], "k_a": g["k_a_2"],
         "r_k": g["r_k_2"].reshape(1, 512), "gn_g": g["gn_g_2"], "gn_b": g["gn_b_2"],
         "fc_w": g["ffn_conv_w_2"][0].reshape(9, -1), "fc_b": g["ffn_conv_b_2"],
         "fo_g": g["fourier_g_2"]}
    A["cols"] = np.concatenate([_columns(c[name]) for name, _ in COLS], axis=1)
    return {k: np.ascontiguousarray(v, dtype=np.float32) for k, v in A.items()}



def kernel(**inputs):
    import concourse.bacc as bacc
    from concourse.bass_utils import run_bass_kernel_spmd

    nc = bacc.Bacc("TRN2", target_bir_lowering=False, num_devices=1)
    arrays = {f"in_{k}": v for k, v in layout(inputs).items()}
    A = {k[3:]: nc.dram_tensor(k, v.shape, F32, kind="ExternalInput").ap() for k, v in arrays.items()}
    out = nc.dram_tensor("out_0", (P, KT, S), F32, kind="ExternalOutput").ap()
    build(nc, A, out)
    r = run_bass_kernel_spmd(nc, [arrays], core_ids=[0])
    return np.ascontiguousarray(r.results[0]["out_0"].transpose(2, 1, 0).reshape(1, S, D))
```

```python
import math
from contextlib import ExitStack, contextmanager

import numpy as np

import concourse.bass as bass
from concourse import mybir

F32 = mybir.dt.float32
ALU = mybir.AluOpType
ACT = mybir.ActivationFunctionType
AX = mybir.AxisListType

P = 128
D = 1024
KT = D // P
S = 512
CTX = 256
T2 = CTX + S
EPS = 1e-6
NEG = -1e30
NPAIR = 4
QT = S // P
NCMP = S // 16 - 1
CONV_W = 31
FT = 2816 // P
C = 64
NCH = S // C
TOEP = 639

STREAM = [("in1", 17), ("ada", 24), ("out1", 8), ("ada6", 4), ("ffn1", 2 * FT), ("pleproj", 2), ("down1", 24),
          ("ada7", 4), ("ple", 8), ("ada8", 4), ("ada9", 4), ("ada10", 4), ("ada11", 4), ("in2", 19), ("out2", 8), ("ffn2", 2 * FT), ("down2", 24)]
UNIT0, NUNITS = {}, 0
for _n, _c in STREAM:
    UNIT0[_n] = NUNITS
    NUNITS += _c
NUNITS_PAD = -(-NUNITS // 4) * 4

COLS = [("mix_g", 8), ("ffn_g", 8), ("ple_g", 8), ("fin_g", 8), ("b1k", 2), ("b1v", 2),
        ("posk", 16), ("posv", 16), ("conv_b", 2), ("ln_g", 2), ("ln_b", 2), ("conv_w", 2 * CONV_W),
        ("gla_b", 1), ("gla_g", 2), ("n1_g", 8), ("n2_g", 8), ("fin2_g", 8), ("ada_b", 48),
        ("c", 16), ("rconv", 36), ("w0", 8), ("a0", 8), ("k_k", 4), ("k_a", 4), ("r_k", 4),
        ("gn_g", 4), ("gn_b", 4), ("fc_w", 44 * 9), ("fc_b", 44), ("fo_g", 4)]
COL0, NCOLS = {}, 0
for _n, _c in COLS:
    COL0[_n] = NCOLS
    NCOLS += _c


LOADS = {"start": 6, "compress": 4, "gla": 3, "fourier": 2, "low_rank": 2, "rwkv": 4}


class Steps:

    def __init__(self, eng, sem):
        self.eng, self.sem, self.total, self.index, self.per = eng, sem, 0, None, 0

    def did(self, ins):
        ins.then_inc(self.sem, 1)
        self.total += 1

    def wait(self, engine=None):
        value = self.total if self.index is None else self.index * self.per + self.total
        (engine or self.eng).wait_ge(self.sem, value)

    def did_but(self, n, make):
        value = self.total - n
        self.eng.wait_ge(self.sem, value if self.index is None else self.index * self.per + value)
        self.did(make())

    def link(self, ins):
        self.did(ins)
        self.wait()

    @contextmanager
    def loop(self, n, per):
        with self.eng.Fori(0, n) as i:
            start, self.index, self.per = self.total, i, per
            yield i
            assert self.total - start == per, (self.total - start, per)
        self.index, self.total = None, start + n * per


class Events:

    def __init__(self, sem, tag, orders, alone=()):
        self.sem_of, self.first, self.given = {}, {}, {}
        for engine, order in orders.items():
            n = 0
            for name, count in order:
                self.sem_of[name], self.first[name] = sem(f"{tag}_{engine}"), n
                self.given[name] = [engine, 0, count]
                n += count
        for name in alone:
            self.sem_of[name], self.first[name] = sem(f"{tag}_{name}"), 0
        self.totals = {engine: 0 for engine in orders}

    def of(self, name):
        if name in self.given:
            g = self.given[name]
            assert self.totals[g[0]] == self.first[name] + g[1] and g[1] < g[2], name
            self.totals[g[0]] += 1
            g[1] += 1
        return self.sem_of[name]

    def __call__(self, name, k):
        return self.sem_of[name], self.first[name] + k


def view(ap, offset, dims):
    return bass.AP(ap.tensor, ap.offset + offset, [list(ap.ap[0])] + [list(d) for d in dims])


def build(nc, A, out, upto=99, dump=None, nunits=NUNITS_PAD):
    with ExitStack() as ctx:
        sem_of = {}

        def sem(name):
            if name not in sem_of:
                sem_of[name] = ctx.enter_context(nc.semaphore(name))
            return sem_of[name]

        SB_COLS = 53000
        mem = ctx.enter_context(nc.sbuf_tensor("mem", [P, SB_COLS], F32))
        psum = ctx.enter_context(nc.psum_tensor("psum", [P, 8, 512], F32))
        ps = [psum[:, b, :] for b in range(8)]
        bias_dram = nc.dram_tensor("bias_scratch", [8, TOEP + 1], F32, kind="Internal").ap()
        x_dram = nc.dram_tensor("x_scratch", [P, KT * S], F32, kind="Internal").ap()
        bias_tiles = nc.dram_tensor("bias_tiles", [8, P, S], F32, kind="Internal").ap()

        class Region:
            def __init__(self, start, end):
                self.at, self.end = start, end

            def take(self, *dims):
                n = int(np.prod(dims))
                assert self.at + n <= self.end, (self.at, n, self.end)
                ap = mem[:, self.at:self.at + n]
                self.at += n
                if len(dims) == 1:
                    return ap
                names = "abcd"[:len(dims)]
                return ap.rearrange(f"p ({' '.join(names)}) -> p {' '.join(names)}",
                                    **dict(zip(names, dims)))

            def remainder(self):
                return Region(self.at, self.end)

        base = Region(0, SB_COLS)
        ring = base.take(4, 8, P)
        ident = base.take(P)
        ones = base.take(P)
        ones64 = base.take(P)
        cols = base.take(NCOLS)
        xT = base.take(KT, S)
        hT = base.take(KT, T2)
        sqr = base.take(KT, S)
        mod = base.take(48, 2)
        gains = base.take(3, KT)
        omka = base.take(4)
        rstd = base.take(512)
        rstd2 = base.take(512)
        eps = base.take(1)
        eps_rw = base.take(1)

        def col(name, i=0, n=1):
            return cols[:, COL0[name] + i:COL0[name] + i + n]

        r1 = base.remainder()
        assert base.at < 21600, base.at
        zT = r1.take(17, S)
        ZCU, ZKS, ZKW, ZKC, ZVC, ZGQ, ZGK, ZGA, ZQ, ZGR = 0, 4, 5, 6, 7, 8, 9, 10, 11, 15
        znat = r1.take(QT, 512)
        gates = r1.take(QT, 8, 3)
        mixT = r1.take(KT, S)
        mixT_nsa, mixT_conv, mixT_gla = mixT[:, 0:4], mixT[:, 4:6], mixT[:, 6:8]
        kcmpT = r1.take(32)
        vcmp = r1.take(P)
        wn = r1.take(8, 536)
        r_cmp = r1.remainder()
        cw1 = [r_cmp.take(16, 256), r_cmp.take(16, 256)]
        cw2 = [r_cmp.take(2, 64), r_cmp.take(2, 64)]
        swapped = r_cmp.take(2, S)
        blocks = [r_cmp.take(16, 2, NCMP), r_cmp.take(16, 2, NCMP)]
        hid = [r_cmp.take(2, 2 * NCMP), r_cmp.take(2, 2 * NCMP)]
        r_bias = Region(mixT.offset, mixT.offset + KT * S)
        onehot = r_bias.take(640)
        negmask = r_bias.take(640)
        relb = r_bias.take(8)
        bvec = r_bias.take(640)
        assert r_cmp.at <= SB_COLS
        r_att = Region(wn.offset, SB_COLS)
        qs = r_att.take(S)
        bias = r_att.take(2, S)
        sc = [[r_att.take(64), r_att.take(512), r_att.take(512)] for _ in range(3)]
        pt = [[r_att.take(P), r_att.take(512), r_att.take(512)] for _ in range(2)]
        stat = [r_att.take(16) for _ in range(3)]
        r_cv = Region(sqr.offset, sqr.offset + KT * S)
        cvt = r_cv.take(2, S)
        cva = r_cv.take(2, S)
        cvx = r_cv.remainder().take(2, S)
        cvh = r_cv.take(2, 544)
        r_gl = Region(wn.offset, SB_COLS)
        gl_silu = r_gl.take(2, S)
        gl_wa = r_gl.take(P)
        gl_t = [r_gl.take(S) for _ in range(3)]
        gl_reset = r_gl.take(S)
        gl_cum = r_gl.take(S)
        gl_q = r_gl.take(S)
        gl_k = r_gl.take(S)
        gl_dn = r_gl.take(NCH)
        gl_kn = r_gl.take(QT, P)
        gl_mask = r_gl.take(C)
        gl_at4 = r_gl.take(4, QT, C)
        gl_st = r_gl.take(C)
        gl_o = r_gl.take(2, S)
        r_ada = Region(SB_COLS - KT * CTX - 2 * CTX - 12 * 512 - 16, SB_COLS)
        assert r_gl.at <= r_ada.at
        modrow = r_ada.take(12, 512)
        sqc = modrow[:, 0:4, :].rearrange("p a b -> p (a b)").rearrange("p (k t) -> p k t", k=KT)
        cs = r_ada.take(16)
        ctxT = r_ada.take(KT, CTX)
        rstdc = r_ada.take(CTX)
        rstdc2 = r_ada.take(CTX)

        units = A["units"]
        units_done = sem("units_done")
        landed = [sem(f"landed{j}") for j in range(4)]
        stage_done = sem("stage_done")
        loaded = {}

        block = ctx.enter_context(nc.Block())

        stages = []

        built = []

        def stage(f):
            if len(built) < upto:
                built.append(f)
                stages.append([f()])
            return f

        def joined(f):
            if len(built) < upto:
                built.append(f)
                stages[-1].append(f())
            return f

        def run(eng, key, steps):
            for n, parts in enumerate(stages):
                if n:
                    eng.wait_ge(stage_done, 4 * n)
                for part in parts:
                    if key in part:
                        part[key](eng, steps)
                eng.drain().then_inc(stage_done, 1)

        def passed(eng, name):
            eng.sem_inc(sem("passed_" + name), 1)

        def load(eng, name, dst, src):
            eng.dma_start(dst, src).then_inc(sem("ld_" + name), 16)
            loaded[name] = True

        def arrived(eng, *names):
            for name in names:
                eng.wait_ge(sem("ld_" + name), 16 * LOADS.get(name, 1))

        def per_unit(pe, u0, count, use, body=4):
            def one(j, i):
                slot = (u0 + j) % 4
                pe.wait_ge(landed[slot], 16 * ((u0 + j) // 4 + 1 + i * (body // 4)))
                use(slot, j, i).then_inc(units_done, 1)
            looped = 0
            if count // body > 1:
                looped = count // body * body
                with pe.Fori(0, count // body) as i:
                    for j in range(body):
                        one(j, i)
            for j in range(looped, count):
                one(j, 0)

        def product(pe, slot, rhs, dst, ready=None):
            for k in range(8):
                if ready:
                    ready(pe, k)
                last = pe.matmul(dst, ring[:, slot, k, :], rhs(k), start=(k == 0), stop=(k == 7))
            return last

        def linear_pe(pe, u0, count, rhs, bank_free, banks=4, ready=None):
            def use(slot, j, i):
                pe.wait_ge(bank_free, 4 * i + j + 1)
                return product(pe, slot, rhs, ps[j % banks], ready)
            per_unit(pe, u0, count, use)

        norms, residuals = [0, 0, None, 0], [0]

        norm_sems = [sem("norm_" + x) for x in ("squared", "added", "summed", "rooted", "scaled", "shifted")]

        def norm(src, dst, g, n=S, shift=None, source=None, pooled=True, before_sum=None, after_sum=None,
                 rows=None, late_rows=None, columns=None):
            squared, added, summed, rooted, scaled, shifted = norm_sems
            r, shifts = norms[0], norms[1]
            norms[0] += 1
            norms[1] += KT * (shift is not None)
            pooled = pooled and source is not None
            sums = norms[3] = norms[3] + pooled

            def act(eng, steps):
                if r:
                    eng.wait_ge(summed, r)
                else:
                    eng.wait_ge(sem("eps_set"), 1)
                for k in range(KT):
                    if source:
                        source(eng, k)
                    eng.activation(sqr[:, k, 0:n], src(k), ACT.Square).then_inc(squared, 1)
                if rows:
                    rows(eng)
                eng.wait_ge(summed, r + 1)
                eng.activation(rstd2[:, 0:n], ps[7][:, 0:n], ACT.Sqrt, scale=1.0 / D, bias=eps).then_inc(rooted, 1)
                if late_rows:
                    late_rows(eng)
                if shift is not None:
                    for k in range(KT):
                        eng.wait_ge(scaled, KT * r + k + 1)
                        eng.activation(dst(k), dst(k), ACT.Identity, bias=shift(k)).then_inc(shifted, 1)

            def pool(eng, steps):
                for k in range(1, KT - 1):
                    eng.wait_ge(squared, KT * r + k + 1)
                    steps.link(eng.tensor_tensor(sqr[:, 0, 0:n], sqr[:, 0, 0:n], sqr[:, k, 0:n], ALU.add))
                eng.sem_inc(added, 1)

            def pe(eng, steps):
                if before_sum:
                    before_sum(eng)
                if pooled:
                    eng.wait_ge(added, sums)
                    eng.matmul(ps[7][:, 0:n], ones, sqr[:, 0, 0:n], start=True, stop=False)
                    eng.wait_ge(squared, KT * r + KT)
                    last = eng.matmul(ps[7][:, 0:n], ones, sqr[:, KT - 1, 0:n], start=False, stop=True)
                else:
                    for k in range(KT):
                        eng.wait_ge(squared, KT * r + k + 1)
                        last = eng.matmul(ps[7][:, 0:n], ones, sqr[:, k, 0:n], start=(k == 0), stop=(k == KT - 1))
                last.then_inc(summed, 1)
                if after_sum:
                    after_sum(eng)

            def dve(eng, steps):
                eng.wait_ge(rooted, r + 1)
                steps.link(eng.reciprocal(rstd[:, 0:n], rstd2[:, 0:n]))
                for k in range(KT):
                    eng.scalar_tensor_tensor(dst(k), src(k), g(k), rstd[:, 0:n], ALU.mult,
                                             ALU.mult).then_inc(scaled, 1)
                if columns:
                    columns(eng, steps)

            norms[2] = (scaled, KT * r) if shift is None else (shifted, shifts)
            return dict(act=act, pe=pe, dve=dve, **(dict(pool=pool) if pooled else {}))

        def normed():
            s, n = norms[2]

            def ready(eng, k):
                eng.wait_ge(s, n + k + 1)
            return ready

        @stage
        def start():
            biased, bias_put = sem("biased"), sem("bias_put")

            def act(eng, steps):
                load(eng, "start", xT, A["xT"])
                load(eng, "start", mem[:, ident.offset:ident.offset + 3 * P], A["consts"])
                load(eng, "start", cols, A["cols"])
                load(eng, "start", onehot[0:32, :], A["onehot"])
                load(eng, "start", relb[0:32, :], A["rel_bias"])
                load(eng, "start", negmask[0:8, :], A["negmask"])
                load(eng, "wn", wn, A["wn"])
                for n in range(2):
                    load(eng, "compress", cw1[n], A["cw1"][n])
                    load(eng, "compress", cw2[n], A["cw2"][n])

            def pe(eng, steps):
                arrived(eng, "start")
                for n in range(2):
                    last = eng.matmul(ps[1 + n][0:8, 0:320], relb[0:32, :], onehot[0:32, 320 * n:320 * n + 320],
                                      start=True, stop=True)
                last.then_inc(biased, 1)

            def dve(eng, steps):
                eng.memset(eps, EPS)
                steps.link(eng.memset(eps_rw, 64e-5))
                eng.sem_inc(sem("eps_set"), 1)
                arrived(eng, "start")
                eng.wait_ge(biased, 1)
                for n in range(2):
                    steps.did(eng.tensor_tensor(bvec[0:8, 320 * n:320 * n + 320], ps[1 + n][0:8, 0:320],
                                                negmask[0:8, 320 * n:320 * n + 320], ALU.add))
                steps.wait()
                eng.sem_inc(bias_put, 1)
                arrived(eng, "start")

            return dict(act=act, pe=pe, dve=dve)

        @joined
        def norm1():
            return norm(lambda k: xT[:, k, :], lambda k: hT[:, k, 0:S], lambda k: col("mix_g", k),
                        source=lambda eng, k: arrived(eng, "start"), pooled=False)

        cv = Events(sem, "conv", {
            "act": (("gated", 2), ("squared", 2), ("rooted", 1),),
            "pe": (("meaned", 1), ("summed", 1),),
            "dve": (("convolved", 2), ("centred", 2), ("varied", 1), ("scaled", 2),),
        })

        def conv_gate(eng):
            for m in range(2):
                eng.activation(cvt[:, m, :], zT[:, ZCU + 2 + m, :], ACT.Sigmoid).then_inc(cv.of("gated"), 1)

        def conv_square(eng):
            for m in range(2):
                eng.wait_ge(*cv("centred", m + 1))
                eng.activation(cvt[:, m, :], cvx[:, m, :], ACT.Square).then_inc(cv.of("squared"), 1)

        def conv_swish(eng):
            eng.wait_ge(*cv("varied", 1))
            eng.activation(rstd2, rstd, ACT.Sqrt).then_inc(cv.of("rooted"), 1)
            for m in range(2):
                eng.wait_ge(*cv("scaled", m + 1))
                eng.activation(mixT[:, 4 + m, :], cvx[:, m, :], ACT.Silu, bias=col("ln_b", m))

        def conv_sum(eng, b, src, ready, done):
            for m in range(2):
                eng.wait_ge(*cv(ready, m + 1))
                last = eng.matmul(ps[b], ones, src[:, m, :], start=(m == 0), stop=(m == 1))
            last.then_inc(cv.of(done), 1)

        def conv_taps(eng, steps):
            for m in range(2):
                eng.memset(cvh[:, m, 0:CONV_W - 1], 0.0)
                eng.wait_ge(*cv("gated", m + 1))
                steps.did(eng.tensor_tensor(cvh[:, m, CONV_W - 1:CONV_W - 1 + S], zT[:, ZCU + m, :], cvt[:, m, :],
                                            ALU.mult))
            steps.wait()
            for k in range(CONV_W):
                for m in range(2):
                    w = col("conv_w", 2 * k + m)
                    if k == 0:
                        steps.did(eng.tensor_scalar(cva[:, m, :], cvh[:, m, 0:S], w, col("conv_b", m), ALU.mult, ALU.add))
                        continue
                    tap = lambda: eng.scalar_tensor_tensor(cva[:, m, :], cvh[:, m, k:k + S], w, cva[:, m, :],
                                                           ALU.mult, ALU.add)
                    if k < CONV_W - 1:
                        steps.did_but(1, tap)
                    else:
                        if m == 0:
                            steps.wait()
                        tap().then_inc(cv.of("convolved"), 1)
            eng.wait_ge(*cv("convolved", 2))
            eng.wait_ge(*cv("meaned", 1))
            for m in range(2):
                eng.scalar_tensor_tensor(cvx[:, m, :], ps[1], -1.0 / 256, cva[:, m, :], ALU.mult,
                                         ALU.add).then_inc(cv.of("centred"), 1)

        def conv_scale(eng, steps):
            eng.wait_ge(*cv("summed", 1))
            eng.tensor_scalar(rstd, ps[2], 1.0 / 256, EPS, ALU.mult, ALU.add).then_inc(cv.of("varied"), 1)
            eng.wait_ge(*cv("rooted", 1))
            eng.wait_ge(*cv("centred", 2))
            steps.link(eng.reciprocal(rstd, rstd2))
            for m in range(2):
                eng.scalar_tensor_tensor(cvx[:, m, :], cvx[:, m, :], col("ln_g", m), rstd, ALU.mult,
                                         ALU.mult).then_inc(cv.of("scaled"), 1)

        @joined
        def project1():
            free, nat = sem("in1_free"), sem("in1_nat")
            nat_copied, gates_read = sem("in1_nat_copied"), sem("in1_gates_read")
            u0 = UNIT0["in1"]
            ready = normed()

            def pe(eng, steps):
                linear_pe(eng, u0, 17, lambda k: hT[:, k, 0:S], free, ready=ready)
                eng.wait_ge(free, 20)
                conv_sum(eng, 1, cva, "convolved", "meaned")
                arrived(eng, "wn")
                for t in range(QT):
                    if t >= 2:
                        eng.wait_ge(nat_copied, t - 1)
                        eng.wait_ge(gates_read, t - 1)
                    for k in range(8):
                        eng.matmul(ps[4 + 2 * (t % 2)], hT[:, k, t * P:(t + 1) * P], wn[:, k, 0:512],
                                   start=(k == 0), stop=(k == 7))
                    for k in range(8):
                        last = eng.matmul(ps[5 + 2 * (t % 2)][:, 0:24], hT[:, k, t * P:(t + 1) * P],
                                          wn[:, k, 512:536], start=(k == 0), stop=(k == 7))
                    last.then_inc(nat, 1)
                conv_sum(eng, 2, cvt, "squared", "summed")

            def act(eng, steps):
                def tile(i, j):
                    eng.wait_ge(units_done, u0 + 1 + j + 4 * i)
                    eng.copy(zT[:, 4 * i + j, :], ps[j]).then_inc(free, 1)

                eng.sem_inc(free, 4)
                for j in range(4):
                    tile(0, j)
                eng.wait_ge(free, 8)
                conv_gate(eng)
                eng.wait_ge(sem("bias_put"), 1)
                load(eng, "bias_dram", bias_dram, bvec[0:8, :])
                arrived(eng, "bias_dram")
                load(eng, "bias_tiles", bias_tiles,
                     bass.AP(bias_dram.tensor, bias_dram.offset + 127, [[TOEP + 1, 8], [-1, P], [1, S]]))
                with eng.Fori(1, 4) as i:
                    for j in range(4):
                        tile(i, j)
                eng.wait_ge(units_done, u0 + 17)
                eng.copy(zT[:, 16, :], ps[0])
                conv_square(eng)
                for t in range(QT):
                    eng.wait_ge(nat, t + 1)
                    eng.activation(gates[:, t].rearrange("p h b -> p (h b)"), ps[5 + 2 * (t % 2)][:, 0:24],
                                   ACT.Sigmoid).then_inc(gates_read, 1)
                conv_swish(eng)

            def dve(eng, steps):
                conv_taps(eng, steps)
                for t in range(QT):
                    eng.wait_ge(nat, t + 1)
                    eng.tensor_copy(znat[:, t, :], ps[4 + 2 * (t % 2)]).then_inc(nat_copied, 1)
                conv_scale(eng, steps)

            return dict(pe=pe, act=act, dve=dve)

        @stage
        def compress():
            swap, laid, hidden, acted, small = (sem("cmp_" + x) for x in ("swap", "laid", "hidden", "acted", "small"))

            def act(eng, steps):
                for n, z in enumerate((ZKC, ZVC)):
                    eng.dma_start(swapped[0:64, n, :], zT[64:128, z, :]).then_inc(swap, 16)
                    eng.dma_start(swapped[64:128, n, :], zT[0:64, z, :]).then_inc(swap, 16)
                for n in range(2):
                    eng.wait_ge(hidden, n + 1)
                    for m in range(2):
                        eng.activation(hid[n][:, m, :], ps[2 * n + m][:, 0:2 * NCMP], ACT.Silu,
                                       bias=col("b1" + "kv"[n], m)).then_inc(acted, 1)

            def dve(eng, steps):
                eng.wait_ge(swap, 64)
                for n, z in enumerate((ZKC, ZVC)):
                    pos = "pos" + "kv"[n]
                    for par in range(2):
                        lo = 64 * par
                        for g in range(2):
                            src = zT[lo:lo + 64, z, :] if par == g else swapped[lo:lo + 64, n, :]
                            eng.tensor_tensor(blocks[n][lo:lo + 64, :, g, :], view(src, par, [[2, 16], [16, NCMP]]),
                                              view(col(pos)[lo:lo + 64], 0, [[1, 16], [0, NCMP]]),
                                              ALU.add).then_inc(laid, 1)
                eng.wait_ge(small, 1)
                eng.tensor_copy(kcmpT[:, 0:NCMP], ps[4][:, 0:NCMP])
                eng.tensor_copy(vcmp[0:NCMP, :], ps[5][0:NCMP, 0:P])

            def pe(eng, steps):
                arrived(eng, "compress")
                for n in range(2):
                    eng.wait_ge(laid, 4 * n + 4)
                    for m in range(2):
                        for jj in range(16):
                            last = eng.matmul(ps[2 * n + m][:, 0:2 * NCMP], cw1[n][:, jj, m * P:(m + 1) * P],
                                              blocks[n][:, jj].rearrange("p g n -> p (g n)"),
                                              start=(jj == 0), stop=(jj == 15))
                    last.then_inc(hidden, 1)
                eng.wait_ge(acted, 4)
                for g in range(2):
                    for m in range(2):
                        eng.matmul(ps[4][64 * g:64 * g + 64, 0:NCMP], cw2[0][:, m, :],
                                   hid[0][:, m, g * NCMP:(g + 1) * NCMP], start=(m == 0), stop=(m == 1))
                for g in range(2):
                    for m in range(2):
                        last = eng.matmul(ps[5][0:NCMP, 64 * g:64 * g + 64], hid[1][:, m, g * NCMP:(g + 1) * NCMP],
                                          cw2[1][:, m, :], start=(m == 0), stop=(m == 1))
                last.then_inc(small, 1)

            return dict(act=act, dve=dve, pe=pe)

        @stage
        def attention():
            qs_ready, bias_in, scored, read_s, neg, exped, coef, scaled, scaled_sel, turned, kept, kept_sel, summed, y_free = (
                sem("at_" + x) for x in ("qs", "bias", "scored", "read", "neg", "exped", "coef",
                                         "scaled", "scaled_sel", "turned", "kept", "kept_sel", "summed", "yfree"))
            order = [(g, i) for i in range(QT) for g in range(2)]
            NU = len(order)

            def nkeys(i):
                return [8 * i + 7, (i + 1) * P, (i + 1) * P]

            def full(u):
                return order[u][1] == QT - 1

            def score_bank(u, b):
                par = u % 2
                if b == 0:
                    return ps[4][:, 64 * par:64 * par + 32] if full(u) else ps[2 * par + 1][:, 384:416]
                return ps[2 * par + b - 1]

            def turned_cmp(u):
                return ps[4][:, P:2 * P] if full(u) else ps[6][:, 384:512]

            def pe(eng, steps):
                keys = [kcmpT, zT[:, ZKS, :], zT[:, ZKW, :]]

                def scores(u, j):
                    g, i = order[u]
                    if full(u) and full(u - 1):
                        eng.wait_ge(read_s, NU * j + u + 1)
                        eng.wait_ge(scored, NU * j + u + 1)
                    else:
                        eng.wait_ge(read_s, NU * j + max(u - 1, 0) + 1)
                    for b in range(3):
                        n = nkeys(i)[b]
                        last = eng.matmul(score_bank(u, b)[:, 0:n], qs[64 * g:64 * g + 64, i * P:(i + 1) * P],
                                          keys[b][64 * g:64 * g + 64, 0:n], start=True, stop=True)
                    last.then_inc(scored, 1)

                def turn(u, j):
                    g, i = order[u]
                    for s in (scaled, scaled_sel):
                        eng.wait_ge(s, NU * j + u + 1)
                    for s in (kept, kept_sel):
                        eng.wait_ge(s, NU * j + u + 1)
                    if full(u):
                        eng.wait_ge(read_s, NU * j + NU + 1)
                    eng.transpose(turned_cmp(u)[0:nkeys(i)[0], :], sc[u % 3][0][:, 0:nkeys(i)[0]], ident)
                    for b in (1, 2):
                        for kb in range(i + 1):
                            last = eng.transpose(ps[4 + b][:, kb * P:(kb + 1) * P],
                                                 sc[u % 3][b][:, kb * P:(kb + 1) * P], ident)
                    last.then_inc(turned, 1)

                def weigh(u, j):
                    g, i = order[u]
                    for s in (kept, kept_sel):
                        eng.wait_ge(s, NU * j + u + 2)
                    if u == 0:
                        eng.wait_ge(y_free, j + 1)
                    dst = ps[7][64 * g:64 * g + 64, i * P:(i + 1) * P]
                    n = nkeys(i)[0]
                    eng.matmul(dst, vcmp[0:n, 64 * g:64 * g + 64], pt[u % 2][0][0:n, :], start=True, stop=False)
                    for b in (1, 2):
                        for kb in range(i + 1):
                            last = eng.matmul(dst, znat[:, kb, P * (b - 1) + 64 * g:P * (b - 1) + 64 * g + 64],
                                              pt[u % 2][b][:, kb * P:(kb + 1) * P], start=False,
                                              stop=(b == 2 and kb == i))
                    last.then_inc(summed, 1)

                for s in (scored, turned, summed):
                    eng.sem_inc(s, 1)
                with eng.Fori(0, NPAIR) as j:
                    eng.wait_ge(qs_ready, j + 1)
                    for u in range(NU + 3):
                        if u < NU:
                            scores(u, j)
                        if u >= 3:
                            weigh(u - 3, j)
                        if 2 <= u < NU + 2:
                            turn(u - 2, j)

            def dve(eng, steps):
                def maxima(u, j):
                    g, i = order[u]
                    st = stat[u % 3]
                    eng.wait_ge(scored, NU * j + u + 2)
                    eng.wait_ge(turned, NU * j + max(u - 2, 0) + 1)
                    passed(eng, "dve")
                    for b in range(3):
                        n = nkeys(i)[b]
                        at = 415 - 128 * i
                        bb = bias[:, g, at:at + 16 * (n - 1) + 1:16] if b == 0 else bias[:, g, 128 * (3 - i):512]
                        last = eng.tensor_tensor_reduce(sc[u % 3][b][:, 0:n], score_bank(u, b)[:, 0:n], bb, 1.0,
                                                        -1e20, ALU.add, ALU.max, st[:, b:b + 1])
                    last.then_inc(read_s, 1)
                    eng.wait_ge(read_s, NU * j + u + 2)
                    eng.tensor_scalar(st[:, 3:6], st[:, 0:3], -1.0, None, ALU.mult).then_inc(neg, 1)

                def weights(u, j):
                    g, i = order[u]
                    st, n = stat[u % 3], nkeys(i)
                    eng.wait_ge(exped, NU * j + u + 1)
                    steps.link(eng.tensor_scalar(st[:, 9:12], st[:, 6:9], 1e-30, None, ALU.max))
                    steps.link(eng.reciprocal(st[:, 12:15], st[:, 9:12]))
                    eng.tensor_tensor(st[:, 9:12], st[:, 12:15], gates[:, i, 4 * g + j, :], ALU.mult).then_inc(coef, 1)
                    eng.wait_ge(coef, NU * j + u + 1)
                    eng.tensor_scalar(sc[u % 3][0][:, 0:n[0]], sc[u % 3][0][:, 0:n[0]], st[:, 9:10], None, ALU.mult)
                    eng.tensor_scalar(sc[u % 3][2][:, 0:n[2]], sc[u % 3][2][:, 0:n[2]], st[:, 11:12], None,
                                      ALU.mult).then_inc(scaled, 1)

                def keep(u, j):
                    n = nkeys(order[u][1])
                    eng.wait_ge(turned, NU * j + u + 2)
                    eng.wait_ge(summed, NU * j + max(u - 1, 0) + 1)
                    eng.tensor_copy(pt[u % 2][0][0:n[0], :], turned_cmp(u)[0:n[0], :])
                    eng.tensor_copy(pt[u % 2][2][:, 0:n[2]], ps[6][:, 0:n[2]]).then_inc(kept, 1)

                for s in (read_s, kept):
                    eng.sem_inc(s, 1)
                with steps.loop(NPAIR, 2 * NU) as j:
                    eng.wait_ge(bias_in, 32 * j + 32)
                    for u in range(NU + 3):
                        if u >= 3:
                            keep(u - 3, j)
                        if u < NU:
                            maxima(u, j)
                        if 1 <= u <= NU:
                            weights(u - 1, j)

            def pool(eng, steps):
                with eng.Fori(0, NPAIR) as j:
                    for u in range(NU):
                        n = nkeys(order[u][1])[1]
                        eng.wait_ge(coef, NU * j + u + 1)
                        passed(eng, "pool")
                        eng.tensor_scalar(sc[u % 3][1][:, 0:n], sc[u % 3][1][:, 0:n], stat[u % 3][:, 10:11], None,
                                          ALU.mult).then_inc(scaled_sel, 1)

            def act(eng, steps):
                arrived(eng, "bias_tiles")
                for s in (kept_sel, y_free):
                    eng.sem_inc(s, 1)
                with eng.Fori(0, NPAIR) as j:
                    eng.wait_ge(read_s, NU * j + 1)
                    eng.wait_ge(scored, NU * j + 1)
                    for g in range(2):
                        eng.dma_start(bias[:, g, :], bias_tiles[4 * g + j]).then_inc(bias_in, 16)
                    eng.activation(qs[:, :], zT[:, ZQ + j, :], ACT.Copy, scale=0.125).then_inc(qs_ready, 1)
                    for u in range(NU + 3):
                        if u >= 3:
                            n = nkeys(order[u - 3][1])[1]
                            eng.wait_ge(turned, NU * j + u - 1)
                            eng.wait_ge(summed, NU * j + max(u - 4, 0) + 1)
                            eng.copy(pt[(u - 3) % 2][1][:, 0:n], ps[5][:, 0:n]).then_inc(kept_sel, 1)
                        if u < NU:
                            g, i = order[u]
                            st = stat[u % 3]
                            eng.wait_ge(neg, NU * j + u + 1)
                            for b in range(3):
                                n = nkeys(i)[b]
                                last = eng.activation(sc[u % 3][b][:, 0:n], sc[u % 3][b][:, 0:n], ACT.Exp,
                                                      bias=st[:, 3 + b:4 + b], accum_out=st[:, 6 + b:7 + b])
                            last.then_inc(exped, 1)
                    eng.wait_ge(summed, NU * j + NU + 1)
                    eng.copy(mixT[:, j, :], ps[7]).then_inc(y_free, 1)

            return dict(pe=pe, dve=dve, act=act, pool=pool)


        cond, got, turned_, ctx_squared, ctx_summed, ctx_varied, ctx_rooted = (sem("ada_" + x) for x in (
            "cond", "got", "turned", "ctx_squared", "ctx_summed", "ctx_varied", "ctx_rooted"))

        def ada_unit0(b):
            return UNIT0["ada"] + 4 * b if b < 6 else UNIT0[f"ada{b}"]

        def ada_bank(b):
            return 6 if b == 11 else 2 + b % 2 + 2 * (b >= 6)

        def ada_start(eng):
            load(eng, "ctxT", ctxT, A["ctxT"])
            eng.activation(cs, col("c", 0, 16), ACT.Silu).then_inc(cond, 1)
            eng.sem_inc(got, 2)

        def ctx_squares(eng):
            arrived(eng, "ctxT")
            for k in range(KT):
                eng.activation(sqc[:, k, :], ctxT[:, k, :], ACT.Square).then_inc(ctx_squared, 1)

        def ctx_sum(eng):
            for k in range(KT):
                eng.wait_ge(ctx_squared, k + 1)
                last = eng.matmul(ps[1][:, 0:CTX], ones, sqc[:, k, :], start=(k == 0), stop=(k == KT - 1))
            last.then_inc(ctx_summed, 1)

        def ada_units(eng, n, count):
            def use(slot, j, i):
                b, q = (n + j) // 4, (n + j) % 4
                if q == 0 and b < 11:
                    eng.wait_ge(got, b + 1)
                for k in range(2):
                    last = eng.matmul(ps[ada_bank(b)][0:2, :], cs[:, 2 * q + k:16:8],
                                      ring[:, slot, 4 * k:4 * k + 4, :].rearrange("p a b -> p (a b)"),
                                      start=(q == 0 and k == 0), stop=(q == 3 and k == 1))
                return last
            per_unit(eng, ada_unit0(n // 4) + n % 4, count, use, 100)

        def ada_turn(eng, first, last_, bank):
            eng.wait_ge(got, last_ + 3)
            for t in range(4 * first, 4 * last_ + 4):
                last = eng.transpose(ps[bank][:, 2 * t:2 * t + 2], modrow[0:2, t // 4, P * (t % 4):P * (t % 4) + P],
                                     ident[0:2, 0:2])
            last.then_inc(turned_, 1)

        def ada_row(eng, b):
            eng.wait_ge(units_done, ada_unit0(b) + 4)
            eng.copy(modrow[0:2, b, :], ps[ada_bank(b)][0:2, :]).then_inc(got, 1)

        def ada_columns(eng, steps, turn, lo, hi, bank, gained):
            eng.wait_ge(turned_, turn)
            steps.link(eng.tensor_tensor(mod[:, lo:hi, :], ps[bank][:, 2 * lo:2 * hi].rearrange("p (t v) -> p t v", v=2),
                                         view(col("ada_b", lo), 0, [[1, hi - lo], [0, 2]]), ALU.add))
            for n, at, v, g in gained:
                eng.scalar_tensor_tensor(gains[:, n, :], mod[:, at:at + 8, v], 1.0, col(g, 0, 8), ALU.add, ALU.mult)

        def ctx_root(eng, steps):
            eng.wait_ge(ctx_summed, 1)
            eng.tensor_scalar(rstdc2, ps[1][:, 0:CTX], 1.0 / D, EPS, ALU.mult, ALU.add).then_inc(ctx_varied, 1)

        @stage
        def gla():
            e = Events(sem, "gla", {
                "act": (("logged", 1), ("eq", 1), ("decays", 1), ("ek", 1), ("kept", 1), ("silued", 2), ("copied", 2),
                        ("squared", 2), ("rooted", 2)),
                "pe": (("alpha", 1), ("turned", 1), ("attn", 4), ("inter", 1)),
                "dve": (("shifted", 1), ("cummed", 1), ("laid", 2), ("masked", 4), ("added", 4), ("varied", 2)),
            }, alone=("summed", "stated", "updated", "sq_summed"))
            t0, t1, t2 = gl_t

            def act(eng, steps):
                load(eng, "gla", gl_wa[0:16, :], A["gla_wa"])
                load(eng, "gla", gl_reset, A["gl_reset"])
                load(eng, "gla", gl_mask, A["gl_mask"])
                ada_start(eng)
                eng.wait_ge(*e("shifted", 1))
                steps.link(eng.activation(t1, t0, ACT.Abs))
                steps.link(eng.activation(t1, t1, ACT.Exp, scale=-1.0))
                eng.activation(t2, t1, ACT.Ln, bias=ones[:, 0:1]).then_inc(e.of("logged"), 1)
                ctx_squares(eng)
                eng.wait_ge(*e("cummed", 1))
                eng.activation(t1, gl_cum, ACT.Exp, scale=1.0 / 16).then_inc(e.of("eq"), 1)
                eng.activation(gl_dn, gl_cum[:, C - 1:S:C], ACT.Exp, scale=1.0 / 16).then_inc(e.of("decays"), 1)
                eng.activation(t2, gl_cum, ACT.Exp, scale=-1.0 / 16).then_inc(e.of("ek"), 1)
                eng.wait_ge(ctx_varied, 1)
                eng.activation(rstdc2, rstdc2, ACT.Sqrt).then_inc(ctx_rooted, 1)
                ada_row(eng, 0)
                eng.wait_ge(*e("turned", 1))
                eng.copy(gl_kn.rearrange("p t c -> p (t c)"), ps[7]).then_inc(e.of("kept"), 1)
                for m in range(2):
                    eng.activation(gl_silu[:, m, :], zT[:, ZGR + m, :], ACT.Silu).then_inc(e.of("silued"), 1)
                ada_row(eng, 1)
                ada_row(eng, 2)
                eng.wait_ge(*e("summed", NCH))
                for hp in range(2):
                    eng.copy(gl_o[:, hp, :], ps[6 + hp]).then_inc(e.of("copied"), 1)
                for hp in range(2):
                    eng.wait_ge(*e("added", 2 * hp + 2))
                    eng.activation(sqr[:, hp, :], gl_o[:, hp, :], ACT.Square).then_inc(e.of("squared"), 1)
                ada_row(eng, 3)
                for hp in range(2):
                    eng.wait_ge(*e("varied", hp + 1))
                    eng.activation(sqr[:, 2 + hp, :], sqr[:, 4 + hp, :], ACT.Sqrt).then_inc(e.of("rooted"), 1)
                ada_row(eng, 4)
                ada_row(eng, 5)

            def pe(eng, steps):
                arrived(eng, "gla")
                eng.matmul(ps[0], gl_wa[0:16, :], zT[0:16, ZGA, :], start=True, stop=True).then_inc(e.of("alpha"), 1)
                eng.wait_ge(cond, 1)
                ada_units(eng, 0, 4)
                ctx_sum(eng)
                eng.wait_ge(*e("laid", 2))
                for t in range(QT):
                    last = eng.transpose(ps[7][:, t * P:(t + 1) * P], gl_k[:, t * P:(t + 1) * P], ident)
                last.then_inc(e.of("turned"), 1)
                eng.wait_ge(got, 3)
                eng.wait_ge(ctx_rooted, 1)
                for h in range(4):
                    for n in range(NCH):
                        par, t = n % 2, n // 2
                        r = slice(32 * h, 32 * h + 32)
                        last = eng.matmul(ps[h][64 * par:64 * par + 64, t * C:(t + 1) * C], gl_k[r, n * C:(n + 1) * C],
                                          gl_q[r, n * C:(n + 1) * C], start=True, stop=True)
                    last.then_inc(e.of("attn"), 1)
                eng.wait_ge(*e("masked", 4))
                for h in range(4):
                    for n in range(NCH):
                        par, t = n % 2, n // 2
                        r, o = slice(64 * par, 64 * par + 64), 64 * (h % 2)
                        last = eng.matmul(ps[4 + par][o:o + 64, (h // 2) * 256 + t * C:(h // 2) * 256 + (t + 1) * C],
                                          znat[r, t, 256 + C * h:256 + C * h + C], gl_at4[r, h, t, :],
                                          start=True, stop=True)
                last.then_inc(e.of("inter"), 1)
                eng.wait_ge(*e("kept", 1))
                for n in range(NCH):
                    par, t = n % 2, n // 2
                    eng.wait_ge(*e("updated", n + 1))
                    for h in range(4):
                        r, o = slice(32 * h, 32 * h + 32), 64 * (h % 2)
                        last = eng.matmul(ps[6 + h // 2][o:o + 64, n * C:(n + 1) * C], gl_st[r, :],
                                          gl_q[r, n * C:(n + 1) * C], start=True, stop=True)
                    last.then_inc(e.of("summed"), 1)
                    ada_units(eng, 4 + n, 1)
                    for h in range(4):
                        r, o = slice(64 * par, 64 * par + 64), 32 * h
                        last = eng.matmul(ps[par][o:o + 32, 0:C], gl_kn[r, t, o:o + 32],
                                          znat[r, t, 256 + C * h:256 + C * h + C], start=True, stop=True)
                    last.then_inc(e.of("stated"), 1)
                ada_units(eng, 12, 4)
                for hp in range(2):
                    eng.wait_ge(*e("squared", hp + 1))
                    eng.wait_ge(*e("updated", NCH + 1))
                    eng.matmul(ps[hp], ones64, sqr[:, hp, :], start=True, stop=True).then_inc(e.of("sq_summed"), 1)
                ada_units(eng, 16, 8)
                ada_turn(eng, 0, 5, 2)

            def dve(eng, steps):
                eng.memset(gl_st, 0.0).then_inc(e.of("updated"), 1)
                eng.wait_ge(*e("alpha", 1))
                eng.tensor_scalar(t0, ps[0], col("gla_b"), None, ALU.add).then_inc(e.of("shifted"), 1)
                eng.wait_ge(*e("shifted", 1))
                steps.link(eng.tensor_scalar(gl_q, t0, 0.0, None, ALU.min))
                eng.wait_ge(*e("logged", 1))
                steps.link(eng.tensor_tensor(gl_k, gl_q, t2, ALU.subtract))
                arrived(eng, "gla")
                eng.tensor_tensor_scan(gl_cum, gl_reset, gl_k, 0.0, ALU.mult, ALU.add).then_inc(e.of("cummed"), 1)
                eng.wait_ge(*e("cummed", 1))
                ctx_root(eng, steps)
                eng.wait_ge(*e("eq", 1))
                eng.scalar_tensor_tensor(gl_q, t1, 32.0 ** -0.5, zT[:, ZGQ, :], ALU.mult, ALU.mult).then_inc(e.of("laid"), 1)
                eng.wait_ge(*e("ek", 1))
                eng.tensor_tensor(gl_k, t2, zT[:, ZGK, :], ALU.mult).then_inc(e.of("laid"), 1)
                for h in range(4):
                    eng.wait_ge(*e("attn", h + 1))
                    eng.tensor_tensor(gl_at4[:, h], ps[h][:, 0:QT * C].rearrange("p (t c) -> p t c", t=QT),
                                      view(gl_mask, 0, [[0, QT], [1, C]]), ALU.mult).then_inc(e.of("masked"), 1)
                eng.wait_ge(*e("decays", 1))
                for n in range(NCH):
                    eng.wait_ge(*e("stated", n + 1))
                    eng.wait_ge(*e("summed", n + 1))
                    eng.wait_ge(*e("updated", n + 1))
                    steps.link(eng.tensor_tensor(gl_st, gl_st, ps[n % 2][:, 0:C], ALU.add))
                    eng.tensor_scalar(gl_st, gl_st, gl_dn[:, n:n + 1], None, ALU.mult).then_inc(e.of("updated"), 1)
                eng.wait_ge(*e("inter", 1))
                for hp in range(2):
                    eng.wait_ge(*e("copied", hp + 1))
                    for par in range(2):
                        o = view(gl_o[:, hp, :], par * C, [[2 * C, QT], [1, C]])
                        eng.tensor_tensor(o, o, ps[4 + par][:, hp * 256:hp * 256 + 256].rearrange(
                            "p (t c) -> p t c", t=QT), ALU.add).then_inc(e.of("added"), 1)
                for hp in range(2):
                    eng.wait_ge(*e("sq_summed", hp + 1))
                    eng.tensor_scalar(sqr[:, 4 + hp, :], ps[hp], 1.0 / 64, EPS, ALU.mult, ALU.add).then_inc(e.of("varied"), 1)
                for hp in range(2):
                    eng.wait_ge(*e("rooted", hp + 1))
                    steps.link(eng.reciprocal(sqr[:, 6 + hp, :], sqr[:, 2 + hp, :]))
                    steps.link(eng.scalar_tensor_tensor(gl_o[:, hp, :], gl_o[:, hp, :], col("gla_g", hp),
                                                        sqr[:, 6 + hp, :], ALU.mult, ALU.mult))
                    eng.wait_ge(*e("silued", hp + 1))
                    eng.tensor_tensor(mixT[:, 6 + hp, :], gl_o[:, hp, :], gl_silu[:, hp, :], ALU.mult)
                eng.wait_ge(ctx_rooted, 1)
                eng.reciprocal(rstdc, rstdc2)
                ada_columns(eng, steps, 1, 0, 24, 2, ((0, 8, 0, "n1_g"), (1, 8, 1, "n1_g")))
                eng.tensor_scalar(omka, col("k_a", 0, 4), -1.0, 1.0, ALU.mult, ALU.add)

            return dict(act=act, pe=pe, dve=dve)

        def residual(tag, rhs, ktiles=8, gate=None, ready=None, primed=False):
            free = sem("residual_free")
            u0, per, r = UNIT0[tag], -(-ktiles // 8), 12 * residuals[0]
            residuals[0] += 1

            def pe(eng, steps):
                def use(slot, j, i):
                    m, part = (j, 0) if per == 1 else (j // 2, j % 2) if j < 8 else (j - 8, 2)
                    if part == 0:
                        eng.wait_ge(free, r + 4 * i + m + 1)
                    for k in range(8 * part, min(8 * part + 8, ktiles)):
                        if ready:
                            ready(eng, k)
                        last = eng.matmul(ps[m % 4], ring[:, slot, k - 8 * part, :], rhs(k), start=(k == 0),
                                          stop=(k == ktiles - 1))
                    return last
                per_unit(eng, u0, 8 * per, use, body=4 * per)

            def dve(eng, steps):
                if not primed:
                    eng.sem_inc(free, 4)
                with eng.Fori(0, 2) as i:
                    for m in range(4):
                        eng.wait_ge(units_done, u0 + 4 * (per - 1) + m + 1 + 4 * per * i)
                        x = xT[:, 4 * i + m, :]
                        if gate is None:
                            ins = eng.tensor_tensor(x, x, ps[m], ALU.add)
                        else:
                            ins = eng.scalar_tensor_tensor(x, ps[m], gate(4 * i + m), x, ALU.mult, ALU.add)
                        ins.then_inc(free, 1)

            return dict(pe=pe, dve=dve)

        def added():
            s, n = sem("residual_free"), 12 * (residuals[0] - 1) + 4

            def source(eng, k):
                eng.wait_ge(s, n + k + 1)
            return source

        @stage
        def out1():
            return residual("out1", lambda k: mixT[:, k, :])

        r2 = base.remainder()
        actT = r2.take(FT, S)
        sil = r2.take(2, S)

        @joined
        def norm_ffn():
            return norm(lambda k: xT[:, k, :], lambda k: hT[:, k, 0:S], lambda k: col("ffn_g", k), source=added(),
                        after_sum=lambda eng: ada_units(eng, 24, 4), late_rows=lambda eng: ada_row(eng, 6))

        @joined
        def ffn1():
            free_gate, free_up, silued, used = (sem("f1_" + x) for x in ("free_gate", "free_up", "silued", "used"))
            u0 = UNIT0["ffn1"]
            ready = normed()

            def pe(eng, steps):
                def use(slot, j, i):
                    eng.wait_ge((free_gate, free_up)[j % 2], 2 * i + j // 2 + 1)
                    return product(eng, slot, lambda k: hT[:, k, 0:S], ps[j], ready)
                per_unit(eng, u0, 2 * FT, use)

            def act(eng, steps):
                eng.sem_inc(free_gate, 2)
                with eng.Fori(0, FT // 2) as i:
                    for f in range(2):
                        eng.wait_ge(units_done, u0 + 4 * i + 2 * f + 1)
                        eng.wait_ge(used, 2 * i + f + 1)
                        eng.activation(sil[:, f, :], ps[2 * f], ACT.Silu).then_inc(silued, 1)
                        eng.wait_ge(silued, 2 * i + f + 1)
                        eng.sem_inc(free_gate, 1)

            def dve(eng, steps):
                eng.sem_inc(free_up, 2)
                eng.sem_inc(used, 2)
                with eng.Fori(0, FT // 2) as i:
                    for f in range(2):
                        eng.wait_ge(units_done, u0 + 4 * i + 2 * f + 2)
                        eng.wait_ge(silued, 2 * i + f + 1)
                        eng.tensor_tensor(actT[:, 2 * i + f, :], sil[:, f, :], ps[2 * f + 1], ALU.mult).then_inc(free_up, 1)
                        eng.wait_ge(free_up, 2 * i + f + 3)
                        eng.sem_inc(used, 1)

            return dict(pe=pe, act=act, dve=dve)

        r3 = r2.remainder()
        pT = r3.take(2, S)
        pj = r3.take(KT, S)
        gt = r3.take(4, S)

        @joined
        def ple_project():
            free = sem("pp_free")
            u0 = UNIT0["pleproj"]

            def pe(eng, steps):
                arrived(eng, "pT")
                eng.wait_ge(got, 9)

                def use(slot, j, i):
                    for m in range(4):
                        eng.wait_ge(free, 4 * j + m + 1)
                        for k in range(2):
                            last = eng.matmul(ps[4 + m], ring[:, slot, 2 * m + k, :], pT[:, k, :], start=(k == 0),
                                              stop=(k == 1))
                    return last
                per_unit(eng, u0, 2, use)

            def act(eng, steps):
                load(eng, "pT", pT, A["pT"])
                eng.sem_inc(free, 4)
                for j in range(2):
                    eng.wait_ge(units_done, u0 + j + 1)
                    for m in range(4):
                        eng.copy(pj[:, 4 * j + m, :], ps[4 + m]).then_inc(free, 1)

            return dict(pe=pe, act=act)

        @joined
        def down1():
            used = sem("f1_used")

            def ready(eng, k):
                if k == 0:
                    eng.wait_ge(used, 2 + FT)
            return residual("down1", lambda k: actT[:, k, :], ktiles=FT, ready=ready)

        @joined
        def norm_ple():
            def between(eng):
                eng.wait_ge(sem("pp_free"), 12)

            return norm(lambda k: xT[:, k, :], lambda k: hT[:, k, 0:S], lambda k: col("ple_g", k), source=added(),
                        before_sum=between, after_sum=lambda eng: ada_units(eng, 28, 4), late_rows=lambda eng: ada_row(eng, 7))

        @joined
        def ple_gate():
            free, sig, mixed = sem("pg_free"), sem("pg_sig"), sem("pg_mixed")
            u0 = UNIT0["ple"]
            ready = normed()

            def pe(eng, steps):
                linear_pe(eng, u0, 8, lambda k: hT[:, k, 0:S], free, ready=ready)

            def act(eng, steps):
                eng.sem_inc(free, 4)
                with eng.Fori(0, 2) as i:
                    for m in range(4):
                        eng.wait_ge(units_done, u0 + 4 * i + m + 1)
                        eng.wait_ge(mixed, 4 * i + m + 1)
                        eng.activation(gt[:, m, :], ps[m], ACT.Sigmoid).then_inc(sig, 1)
                        eng.wait_ge(sig, 4 * i + m + 1)
                        eng.sem_inc(free, 1)

            def dve(eng, steps):
                eng.sem_inc(mixed, 4)
                with steps.loop(2, 4) as i:
                    for m in range(4):
                        eng.wait_ge(sig, 4 * i + m + 1)
                        steps.link(eng.tensor_tensor(gt[:, m, :], gt[:, m, :], pj[:, 4 * i + m, :], ALU.mult))
                        eng.tensor_tensor(xT[:, 4 * i + m, :], xT[:, 4 * i + m, :], gt[:, m, :], ALU.add)\
                           .then_inc(mixed, 1)

            return dict(pe=pe, act=act, dve=dve)

        @joined
        def norm_final1():
            def between(eng):
                ada_units(eng, 32, 4)

            def rows(eng):
                ada_row(eng, 8)

            return norm(lambda k: xT[:, k, :], lambda k: xT[:, k, :], lambda k: col("fin_g", k),
                        source=lambda eng, k: eng.wait_ge(sem("pg_mixed"), 4 + k + 1),
                        before_sum=between, rows=rows)


        r4 = base.remainder()
        rC = r4.take(NCH, 4, C)
        kC = r4.take(12, 4, C)
        vC = r4.take(12, 4, C)
        kkC = r4.take(12, 4, C)
        yC = r4.take(NCH, 4, C)
        fT = r4.take(4, S)
        gdT = r4.take(S)
        r5 = r4.remainder()
        RAW = T2 + 3
        raw = r5.take(12, RAW)
        dft = r5.take(2, 4, S)
        r6 = r4.remainder()
        sig = [r6.take(12, 4, C) for _ in range(2)]
        kka = [r6.take(12, 4, C) for _ in range(2)]
        kd0 = r6.take(12, 4, C)
        kd = [kd0, kC]
        r7 = Region(hT.offset, hT.offset + KT * T2)
        lw = r7.take(T2)
        la = r7.take(T2)
        aT = r7.take(2, T2)
        mixed = Region(r7.end - 4096, r7.end).take(4, 2, S)
        lowT = sqr[:, 0:3, :].rearrange("p a b -> p (a b)")
        dft64 = sqr[:, 3, 0:256]
        r8 = Region(yC.offset, yC.offset + NCH * 4 * C)
        wl = r8.take(512)
        al = r8.take(512)
        r9 = Region(raw.offset, raw.offset + 4 * RAW)
        kroot = r9.take(2, T2)
        ksq = r9.take(2, T2)
        krec = Region(raw.offset + 4 * RAW, raw.offset + 6 * RAW).take(2, T2)

        @joined
        def norm_x():
            s, n = norms[2]

            def between(eng):
                for b in (9, 10, 11):
                    ada_units(eng, 4 * b, 4)

            def rows(eng):
                for b in (9, 10, 11):
                    ada_row(eng, b)
                eng.sem_inc(sem("in2_free"), 4)

            def columns(eng, steps):
                ada_columns(eng, steps, 2, 24, 48, 4, ((2, 32, 0, "n2_g"),))

            return norm(lambda k: xT[:, k, :], lambda k: hT[:, k, CTX:T2], lambda k: gains[:, 0, k:k + 1],
                        shift=lambda k: mod[:, k, 0:1], source=lambda eng, k: eng.wait_ge(s, n + k + 1), pooled=False,
                        before_sum=between, after_sum=lambda eng: ada_turn(eng, 6, 11, 4), rows=rows, columns=columns)

        ctx_scaled, ctx_shifted = sem("ctx_scaled"), sem("ctx_shifted")

        @joined
        def norm_ctx():
            def dve(eng, steps):
                for k in range(KT):
                    eng.scalar_tensor_tensor(hT[:, k, 0:CTX], ctxT[:, k, :], gains[:, 1, k:k + 1], rstdc, ALU.mult,
                                             ALU.mult).then_inc(ctx_scaled, 1)

            def act(eng, steps):
                for k in range(KT):
                    eng.wait_ge(ctx_scaled, k + 1)
                    eng.activation(hT[:, k, 0:CTX], hT[:, k, 0:CTX], ACT.Identity, bias=mod[:, k, 1:2]).then_inc(ctx_shifted, 1)

            return dict(dve=dve, act=act)

        low_rank_waits = []

        @joined
        def project2():
            free, free_ctx, tapped = sem("in2_free"), sem("in2_free_ctx"), sem("in2_tapped")
            scaled_, squared, summed, varied, rooted = (sem("kk_" + x) for x in (
                "scaled", "squared", "summed", "varied", "rooted"))
            u0 = UNIT0["in2"]
            ready = normed()
            both = range(4, 14)

            def dest(m):
                if m < 12:
                    return raw[:, m, CTX + 2:CTX + 2 + S], raw[:, m, 1:1 + CTX]
                if m < 14:
                    return lowT[:, (m - 12) * T2 + CTX:(m - 11) * T2], lowT[:, (m - 12) * T2:(m - 12) * T2 + CTX]
                return (gdT, None) if m == 14 else (fT[:, m - 15, :], None)

            def pieces(m):
                q, hp = m // 4, m % 4
                dst = (rC, kC, vC)[q]
                lo = 0 if q == 0 else 4
                out_ = [(dst[:, lo:lo + NCH, hp, :], raw[:, m, CTX + 1:CTX + 1 + S], NCH)]
                if q:
                    out_.append((dst[:, 0:4, hp, :], raw[:, m, 0:CTX], 4))
                return out_

            def pe(eng, steps):
                def use(m):
                    def f(slot, j, i):
                        eng.wait_ge(free, m + 1)
                        last = product(eng, slot, lambda k: hT[:, k, CTX:T2], ps[m % 4], ready)
                        if m in both:
                            eng.wait_ge(free_ctx, m - 3)
                            last = product(eng, slot, lambda k: hT[:, k, 0:CTX], ps[4 + m % 4][:, 0:CTX],
                                           lambda eng, k: eng.wait_ge(ctx_shifted, k + 1))
                        return last
                    return f

                def key_sums(hp):
                    eng.wait_ge(squared, hp + 1)
                    if hp >= 2:
                        eng.wait_ge(varied, hp - 1)
                    b = 4 + 2 * (hp % 2)
                    eng.matmul(ps[b], ones64, ksq[:, hp % 2, 0:512], start=True, stop=True)
                    eng.matmul(ps[b + 1][:, 0:256], ones64, ksq[:, hp % 2, 512:T2], start=True, stop=True).then_inc(summed, 1)

                for m in range(19):
                    per_unit(eng, u0 + m, 1, use(m))
                    if m in (15, 17):
                        eng.wait_ge(free_ctx, 14)
                        for hp in (m - 15, m - 14):
                            key_sums(hp)

            def act(eng, steps):
                taps = [0]

                def first_taps(m):
                    eng.wait_ge(free, m + 5)
                    eng.wait_ge(free_ctx, max(m - 3, 0) + 4)
                    for dst, src, n in pieces(m):
                        eng.activation(dst, view(src, 0, [[C, n], [1, C]]), ACT.Copy, scale=col("rconv", m)).then_inc(tapped, 1)

                def key_squares(hp):
                    eng.wait_ge(scaled_, hp + 1)
                    if hp >= 2:
                        eng.wait_ge(summed, hp - 1)
                        eng.wait_ge(varied, hp + 1 - 2)
                    eng.activation(ksq[:, hp % 2, :].rearrange("p (c t) -> p c t", c=12), kkC[:, :, hp, :], ACT.Square)\
                       .then_inc(squared, 1)

                def key_roots(hp):
                    eng.wait_ge(varied, hp + 1)
                    eng.activation(kroot[:, hp % 2, :], kroot[:, hp % 2, :], ACT.Sqrt).then_inc(rooted, 1)

                for m in range(19):
                    eng.wait_ge(units_done, u0 + m + 1)
                    eng.copy(dest(m)[0], ps[m % 4]).then_inc(free, 1)
                    if m == 0:
                        eng.wait_ge(ctx_shifted, 8)
                        load(eng, "x_out", x_dram, xT.rearrange("p a b -> p (a b)"))
                        load(eng, "fourier", dft, A["dft"])
                        load(eng, "fourier", dft64, A["dft64"])
                        load(eng, "low_rank", wl[:, :], A["w_low"])
                        load(eng, "low_rank", al[:, :], A["a_low"])
                    if 1 <= m <= 12:
                        first_taps(m - 1)
                    if m == 14:
                        key_squares(0)
                        key_squares(1)
                    if m == 16:
                        key_roots(0)
                        key_roots(1)
                        key_squares(2)
                        key_squares(3)
                key_roots(2)
                key_roots(3)

            def dve(eng, steps):
                for at in (0, CTX + 1, RAW - 1):
                    steps.did(eng.memset(raw[:, :, at:at + 1], 0.0))
                steps.wait()
                eng.sem_inc(free_ctx, 4)
                n_ = 0
                for m in range(14):
                    if m in both:
                        eng.wait_ge(units_done, u0 + m + 1)
                        eng.tensor_copy(dest(m)[1], ps[4 + m % 4][:, 0:CTX]).then_inc(free_ctx, 1)
                    for dst, src, n in pieces(m - 1) if 1 <= m <= 12 else ():
                        n_ += 1
                        eng.wait_ge(tapped, n_)
                        for tap in (1, 2):
                            steps.link(eng.scalar_tensor_tensor(dst, view(src, tap, [[C, n], [1, C]]),
                                                                col("rconv", 12 * tap + m - 1), dst, ALU.mult, ALU.add))
                for hp in range(4):
                    eng.tensor_scalar(kkC[:, :, hp, :], kC[:, :, hp, :], col("k_k", hp), None, ALU.mult).then_inc(scaled_, 1)
                eng.wait_ge(scaled_, 4)
                for hp0 in (0, 2):
                    for hp in (hp0, hp0 + 1):
                        b = 4 + 2 * (hp % 2)
                        eng.wait_ge(summed, hp + 1)
                        if hp >= 2:
                            steps.wait()
                        eng.tensor_scalar(kroot[:, hp % 2, 0:512], ps[b], 1e-12, None, ALU.add)
                        eng.tensor_scalar(kroot[:, hp % 2, 512:T2], ps[b + 1][:, 0:256], 1e-12, None, ALU.add).then_inc(varied, 1)
                    for hp in (hp0, hp0 + 1):
                        eng.wait_ge(rooted, hp + 1)
                        steps.link(eng.reciprocal(krec[:, hp % 2, :], kroot[:, hp % 2, :]))
                        steps.did(eng.tensor_tensor(kkC[:, :, hp, :], kkC[:, :, hp, :],
                                                    krec[:, hp % 2, :].rearrange("p (c t) -> p c t", c=12), ALU.mult))
                steps.wait()

            return dict(pe=pe, act=act, dve=dve)

        @joined
        def fourier():
            e = Events(sem, "fourier", {
                "act": (("firsts", 16), ("squared", 4), ("rooted", 1),),
                "pe": (("first", 16), ("second", 4), ("summed", 1),),
                "dve": (("varied", 1), ("out", 4)),
            })
            projected = sem("in2_free")

            def act(eng, steps):
                eng.wait_ge(*e("first", 1))
                eng.activation(lw, lowT[:, 0:T2], ACT.Tanh)
                eng.copy(la, lowT[:, T2:2 * T2]).then_inc(sem("low_moved"), 1)
                for n in range(16):
                    ct, tt = n // 4, n % 4
                    eng.wait_ge(*e("first", n + 1))
                    for q in range(2):
                        last = eng.copy(mixed[:, tt, q, ct * P:(ct + 1) * P], ps[n % 4][:, q * P:(q + 1) * P])
                    last.then_inc(e.of("firsts"), 1)
                for ct in range(4):
                    eng.wait_ge(*e("second", ct + 1))
                    eng.activation(sqr[:, 4 + ct, :], ps[4 + ct], ACT.Square).then_inc(e.of("squared"), 1)
                eng.wait_ge(*e("varied", 1))
                eng.activation(rstd2, rstd, ACT.Sqrt).then_inc(e.of("rooted"), 1)

            def pe(eng, steps):
                arrived(eng, "fourier")
                eng.wait_ge(projected, 23)
                for n in range(16):
                    ct, tt = n // 4, n % 4
                    if n >= 4:
                        eng.wait_ge(*e("firsts", n - 3))
                    eng.matmul(ps[n % 4][:, 0:256], fT[:, ct, tt * P:(tt + 1) * P], dft64, start=True, stop=True)\
                       .then_inc(e.of("first"), 1)
                eng.wait_ge(*e("firsts", 16))
                eng.wait_ge(sem("kk_varied"), 4)
                for ct in range(4):
                    for tt in range(4):
                        for q in range(2):
                            last = eng.matmul(ps[4 + ct], mixed[:, tt, q, ct * P:(ct + 1) * P], dft[:, q, tt, :],
                                              start=(tt + q == 0), stop=(tt == 3 and q == 1))
                    last.then_inc(e.of("second"), 1)
                for ct in range(4):
                    eng.wait_ge(*e("squared", ct + 1))
                    last = eng.matmul(ps[0], ones, sqr[:, 4 + ct, :], start=(ct == 0), stop=(ct == 3))
                last.then_inc(e.of("summed"), 1)

            def dve(eng, steps):
                eng.wait_ge(*e("summed", 1))
                eng.tensor_scalar(rstd, ps[0], 1.0 / 512, EPS, ALU.mult, ALU.add).then_inc(e.of("varied"), 1)
                eng.wait_ge(*e("rooted", 1))
                steps.link(eng.reciprocal(rstd, rstd2))
                for ct in range(4):
                    eng.scalar_tensor_tensor(fT[:, ct, :], ps[4 + ct], col("fo_g", ct), rstd, ALU.mult, ALU.mult)\
                       .then_inc(e.of("out"), 1)

            low_rank_waits.append((e("varied", 1), e("out", 4)))
            return dict(act=act, pe=pe, dve=dve)

        @joined
        def low_rank():
            made, read, rated, used = (sem("lr_" + x) for x in ("made", "read", "rated", "used"))

            def pe(eng, steps):
                arrived(eng, "low_rank")
                eng.wait_ge(sem("low_moved"), 1)
                varied, written = low_rank_waits[0]
                eng.wait_ge(*varied)
                n = 0
                for d in range(2):
                    r = slice(64 * d, 64 * d + 64)
                    for hp in range(4):
                        for wgt, src in ((wl, lw), (al, la)):
                            b = 2 * (n % 4)
                            if n >= 4:
                                eng.wait_ge(read, n - 3)
                            elif n == 2:
                                eng.wait_ge(*written)
                            w = wgt[r, hp * P:(hp + 1) * P]
                            eng.matmul(ps[b], w, src[r, 0:512], start=True, stop=True)
                            eng.matmul(ps[b + 1][:, 0:256], w, src[r, 512:T2], start=True, stop=True).then_inc(made, 1)
                            n += 1

            def act(eng, steps):
                n = 0
                for d in range(2):
                    for hp in range(4):
                        b = 2 * (n % 4)
                        eng.wait_ge(made, n + 1)
                        bias = col("w0", 4 * d + hp)
                        eng.activation(sig[d][:, 0:8, hp, :], ps[b].rearrange("p (c t) -> p c t", c=8), ACT.Sigmoid, bias=bias)
                        eng.activation(sig[d][:, 8:12, hp, :], ps[b + 1][:, 0:256].rearrange("p (c t) -> p c t", c=4),
                                       ACT.Sigmoid, bias=bias).then_inc(read, 1)
                        n += 1
                        b = 2 * (n % 4)
                        eng.wait_ge(made, n + 1)
                        k = 4 * d + hp
                        if k >= 2:
                            eng.wait_ge(used, k - 1)
                        bias = col("a0", k)
                        eng.activation(aT[:, k % 2, 0:512], ps[b], ACT.Sigmoid, bias=bias).then_inc(rated, 1)
                        eng.activation(aT[:, k % 2, 512:T2], ps[b + 1][:, 0:256], ACT.Sigmoid, bias=bias).then_inc(read, 1)
                        n += 1

            def dve(eng, steps):
                for d in range(2):
                    for hp in range(4):
                        k = 4 * d + hp
                        eng.wait_ge(read, 2 * k + 2)
                        a = aT[:, k % 2, :].rearrange("p (c t) -> p c t", c=12)
                        steps.link(eng.tensor_tensor(kka[d][:, :, hp, :], kkC[:, :, hp, :], a, ALU.mult))
                        steps.link(eng.tensor_scalar(a, a, col("k_a", hp), omka[:, hp:hp + 1], ALU.mult, ALU.add))
                        eng.tensor_tensor(kd[d][:, :, hp, :], kC[:, :, hp, :], a, ALU.mult).then_inc(used, 1)

            return dict(act=act, pe=pe, dve=dve)

        free_regions = [Region(hT.offset, hT.offset + KT * T2), Region(sqr.offset, sqr.offset + KT * S),
                        Region(xT.offset, xT.offset + KT * S),
                        Region(r6.at, SB_COLS)]

        def stage_take(*dims):
            for r in free_regions:
                if r.at + int(np.prod(dims)) <= r.end:
                    return r.take(*dims)
            raise AssertionError(dims)

        G = 4 * C
        masks = stage_take(2, 4, C)
        lev = stage_take(2, 6, C)
        eye = stage_take(C)
        reset = stage_take(2, G)
        st_ = []
        for d in range(2):
            st_.append(dict(
                cum=stage_take(4, C), prev=stage_take(4, C), e1=stage_take(4, C), e2=stage_take(4, C),
                e3=stage_take(4, C), ar=stage_take(4, 2, C), bT=stage_take(4, C), kT=stage_take(4, C),
                vT=stage_take(4, C), ab=stage_take(2, 4, C), kv=stage_take(2, 4, C), g1=stage_take(4, 2, C),
                g2=stage_take(2, 4, C), T=stage_take(4, C), Tt=stage_take(4, C), Z=stage_take(4, C),
                wtb=stage_take(2, 4, C), U=stage_take(4, C), M=stage_take(4, C), dk=stage_take(4)))
        DEC = math.exp(-0.5)
        LINKS = (17, 17)

        def bc(ap, n=4):
            return view(ap, 0, [[0, n], [1, C]])

        @stage
        def rwkv():
            e = [{n: sem(f"rwkv_{n}{d}") for n in (
                "cum", "prev",
                "ex",
                "laid", "laid2",
                "turned",
                "raw",
                "masked",
                "made", "kept",
                "acted",
                "fed",
                "mc",
                )} for d in range(2)]
            HB = (slice(0, 64), slice(64, 128))
            LAST = 11

            def chunk_of(d, it, y):
                return it if d == 0 else (15 - it if y else 3 - it)

            def wait(eng, s, value):
                if not (isinstance(value, int) and value <= 0):
                    eng.wait_ge(s, value)

            def walk(eng, steps, phase, per=(0, 0)):
                def turns(i, y, y_next):
                    phase((1, i, y), (0, i, y), (0, i + 1, y_next))
                    phase((0, i + 1, y_next), (1, i, y), (1, i + 1, y_next))

                def loop(n, first, y, per):
                    with steps.loop(n, per) if per else eng.Fori(0, n) as i:
                        turns(i + first, y, y)

                phase(None, None, (0, 0, False))
                phase((0, 0, False), None, (1, 0, False))
                loop(3, 0, False, per[0])
                turns(3, False, True)
                loop(7, 4, True, per[1])
                phase((1, LAST, True), (0, LAST, True), None)
                phase(None, (1, LAST, True), None)

            def pe(eng, steps):
                def each(fn):
                    for hp in range(4):
                        for b in range(2):
                            last = fn(hp, HB[b])
                    return last

                def parts(d):
                    return st_[d], e[d], ps[4 * d:4 * d + 4]

                def turn(bank, half, src, d, it):
                    s, q, B = parts(d)
                    if bank == 0 and half == 1:
                        eng.wait_ge(q["laid"], 2 * it + 1)
                    else:
                        eng.wait_ge(q["laid2"], it + 1)
                    passed(eng, "pe")
                    last = each(lambda hp, r: eng.matmul(B[bank][r, half * G + hp * C:half * G + (hp + 1) * C],
                                                         src(s)[r, hp], ident[r, r], start=True, stop=True))
                    if half:
                        last.then_inc(q["turned"], 1)

                def level(n, d, it):
                    s, q, B = parts(d)
                    if n == 0:
                        eng.wait_ge(q["acted"], 3 * it + 1)
                        eng.wait_ge(q["masked"], 2 * it + 1)
                    else:
                        eng.wait_ge(q["kept"], 10 * it + n)
                    passed(eng, "pe")
                    if n % 2 == 0:
                        each(lambda hp, r: eng.matmul(B[0][r, hp * C:(hp + 1) * C], s["g1"][r, hp, 0, :], s["T"][r, hp, :],
                                                      start=True, stop=True)).then_inc(q["made"], 1)
                    else:
                        a, b_ = (s["Tt"], s["Z"]) if n < 9 else (s["Z"], s["Tt"])
                        each(lambda hp, r: eng.matmul(B[1][r, hp * C:(hp + 1) * C], a[r, hp, :], b_[r, hp, :],
                                                      start=True, stop=True)).then_inc(q["made"], 1)

                def t_alpha(d, it, y):
                    s, q, B = parts(d)
                    eng.wait_ge(q["kept"], 10 * it + 10)
                    passed(eng, "pe")
                    each(lambda hp, r: eng.matmul(B[2][r, hp * C:(hp + 1) * C], s["ab"][r, 0, hp, :], s["Tt"][r, hp, :],
                                                  start=True, stop=True))

                def t_b(d, it, y):
                    s, q, B = parts(d)
                    eng.wait_ge(q["masked"], 2 * it + 2)
                    passed(eng, "pe")
                    each(lambda hp, r: eng.matmul(B[2][r, G + hp * C:G + (hp + 1) * C], s["g2"][r, 0, hp, :],
                                                  s["Tt"][r, hp, :], start=True, stop=True)).then_inc(q["fed"], 1)

                def u(d, it, y):
                    s, q, B = parts(d)
                    eng.wait_ge(q["acted"], 3 * it + 2)
                    eng.wait_ge(q["mc"], it + 1)
                    passed(eng, "pe")

                    def f(hp, r):
                        eng.matmul(B[3][r, hp * C:(hp + 1) * C], s["wtb"][r, 0, hp, :], s["M"][r, hp, :], start=True,
                                   stop=False)
                        return eng.matmul(B[3][r, hp * C:(hp + 1) * C], s["wtb"][r, 1, hp, :], s["kv"][r, 1, hp, :],
                                          start=False, stop=True)
                    each(f).then_inc(q["fed"], 1)

                def outputs(d, it, y):
                    s, q, B = parts(d)
                    eng.wait_ge(q["acted"], 3 * it + 3)
                    passed(eng, "pe")

                    def f(hp, r):
                        dst = B[2][r, hp * C:(hp + 1) * C]
                        eng.matmul(dst, s["M"][r, hp, :], s["ar"][r, hp, 1, :], start=True, stop=False)
                        eng.matmul(dst, s["U"][r, hp, :], s["g1"][r, hp, 1, :], start=False, stop=False)
                        return eng.matmul(dst, s["kv"][r, 1, hp, :], s["g2"][r, 1, hp, :], start=False, stop=True)
                    if y:
                        each(f)

                def state(d, it, y):
                    s, q, B = parts(d)

                    def f(hp, r):
                        dst = B[2][r, G + hp * C:G + (hp + 1) * C]
                        eng.matmul(dst, s["ab"][r, 1, hp, :], s["U"][r, hp, :], start=True, stop=False)
                        return eng.matmul(dst, s["kv"][r, 0, hp, :], s["kv"][r, 1, hp, :], start=False, stop=True)
                    each(f).then_inc(q["fed"], 1)

                def raw_kappa(d, it, y):
                    s, q, B = parts(d)
                    wait(eng, q["acted"], 3 * it)
                    passed(eng, "pe")
                    last = each(lambda hp, r: eng.matmul(B[3][r, hp * C:(hp + 1) * C], s["ar"][r, hp, 0, :],
                                                         s["kT"][r, hp, :], start=True, stop=True))
                    if y:
                        last = each(lambda hp, r: eng.matmul(B[3][r, G + hp * C:G + (hp + 1) * C], s["kT"][r, hp, :],
                                                             s["ar"][r, hp, 1, :], start=True, stop=True))
                    last.then_inc(q["raw"], 1)

                def raw_beta(d, it, y):
                    s, q, B = parts(d)
                    eng.wait_ge(q["laid"], 2 * it + 2)
                    eng.wait_ge(q["mc"], it + 1)
                    passed(eng, "pe")
                    n = 2 if y else 1
                    each(lambda hp, r: eng.matmul(B[2][r, hp * 2 * C:hp * 2 * C + n * C], s["bT"][r, hp, :],
                                                  s["ar"][r, hp, 0:n, :].rearrange("p a t -> p (a t)"), start=True,
                                                  stop=True)).then_inc(q["raw"], 1)

                def phase(grow, end, prep):
                    def other(f, what):
                        if what:
                            f(*what)

                    def turns(bank, half, src):
                        return lambda d, it, y: turn(bank, half, src, d, it)

                    alpha = turns(0, 0, lambda s: s["ar"][:, :, 0, :])
                    beta = turns(0, 1, lambda s: s["bT"])
                    kappa = turns(1, 0, lambda s: s["kT"])
                    values = turns(1, 1, lambda s: s["vT"])
                    after = {-1: ((t_alpha, end),), 0: ((t_b, end),), 1: ((kappa, prep),), 2: ((u, end),),
                             3: ((values, prep),), 4: ((alpha, prep),), 5: ((outputs, end),), 6: ((state, end),),
                             7: ((beta, prep),), 8: ((raw_beta, prep),), 9: ((raw_kappa, prep),)}
                    for n in range(-1, 10):
                        if n >= 0 and grow:
                            level(n, *grow[:2])
                        for f, what in after.get(n, ()):
                            other(f, what)
                walk(eng, steps, phase)

            def flat(ap):
                return ap.rearrange("p h t -> p (h t)")

            def dve(eng, steps):
                def parts(d):
                    return st_[d], e[d], ps[4 * d:4 * d + 4]

                def sums(d, it, y):
                    s, q, B = parts(d)
                    c = chunk_of(d, it, y)
                    wait(eng, q["ex"], it)
                    passed(eng, "dve")
                    eng.tensor_tensor_scan(flat(s["cum"]), reset[:, 0, :], flat(sig[d][:, c]), 0.0,
                                           ALU.mult, ALU.add).then_inc(q["cum"], 1)
                    eng.wait_ge(q["cum"], it + 1)
                    passed(eng, "dve")
                    if d:
                        steps.link(eng.tensor_tensor(s["prev"], view(s["cum"][:, 0, C - 1:C], 0, [[C, 4], [0, C]]), s["cum"],
                                                     ALU.subtract))
                        eng.tensor_tensor(s["cum"], s["prev"], sig[d][:, c], ALU.add).then_inc(q["prev"], 1)
                    else:
                        eng.tensor_tensor(s["prev"], s["cum"], sig[d][:, c], ALU.subtract).then_inc(q["prev"], 1)

                def beta(d, it, y):
                    s, q, B = parts(d)
                    eng.wait_ge(q["ex"], it + 1)
                    wait(eng, q["raw"], 2 * it)
                    passed(eng, "dve")
                    eng.tensor_tensor(s["bT"], kka[d][:, chunk_of(d, it, y)], s["e2"], ALU.mult).then_inc(q["laid"], 1)

                def growth(n, d, it):
                    s, q, B = parts(d)
                    eng.wait_ge(q["made"], 10 * it + n + 1)
                    x = B[n % 2][:, 0:G].rearrange("p (h t) -> p h t", h=4)
                    if n % 2 == 0:
                        eng.tensor_tensor(s["Z"], x, bc(lev[:, d, 1 + n // 2, :]), ALU.mult).then_inc(q["kept"], 1)
                    elif n < 9:
                        steps.link(eng.tensor_tensor(s["T"], s["T"], x, ALU.subtract))
                        eng.transpose(flat(s["Tt"]), flat(s["T"])).then_inc(q["kept"], 1)
                    else:
                        eng.tensor_tensor(s["Tt"], s["Tt"], x, ALU.subtract).then_inc(q["kept"], 1)

                def ended(d, it, y):
                    s, q, B = parts(d)
                    eng.wait_ge(q["fed"], 3 * it + 3)
                    passed(eng, "dve")
                    if y:
                        yy = yC[:, chunk_of(d, it, y) - 4]
                        eng.tensor_tensor(yy, yy, B[2][:, 0:G].rearrange("p (h t) -> p h t", h=4), ALU.add)
                    steps.link(eng.tensor_tensor(s["M"], s["M"], B[2][:, G:2 * G].rearrange("p (h t) -> p h t", h=4), ALU.add))
                    eng.tensor_tensor(s["M"], s["M"], view(s["dk"], 0, [[1, 4], [0, C]]), ALU.mult).then_inc(q["mc"], 1)

                def rho(d, it, y):
                    s, q, B = parts(d)
                    wait(eng, q["ex"], it + 1)
                    wait(eng, q["mc"], it + 1)
                    passed(eng, "dve")
                    if y:
                        eng.tensor_tensor(s["ar"][:, :, 1, :], rC[:, chunk_of(d, it, y) - 4], s["e3"], ALU.mult)
                    at = 0 if d else C - 1
                    eng.tensor_copy(s["dk"], s["e3"][:, :, at]).then_inc(q["laid"], 1)

                def mask_kappa(d, it, y):
                    s, q, B = parts(d)
                    eng.wait_ge(q["raw"], 2 * it + 2)
                    wait(eng, q["fed"], 3 * it)
                    passed(eng, "dve")
                    last = eng.tensor_tensor(s["g2"][:, 0], B[3][:, 0:G].rearrange("p (h t) -> p h t", h=4),
                                             bc(masks[:, d, 2, :]), ALU.mult)
                    if y:
                        last = eng.tensor_tensor(s["g2"][:, 1], B[3][:, G:2 * G].rearrange("p (h t) -> p h t", h=4),
                                                 bc(masks[:, d, 1, :]), ALU.mult)
                    last.then_inc(q["masked"], 1)

                def mask_beta(d, it, y):
                    s, q, B = parts(d)
                    n = 2 if y else 1
                    eng.wait_ge(q["raw"], 2 * it + 1)
                    wait(eng, q["fed"], 3 * it)
                    passed(eng, "dve")
                    steps.link(eng.tensor_tensor(s["g1"][:, :, 0:n, :],
                                                 B[2].rearrange("p (h n t) -> p h n t", h=4, n=2)[:, :, 0:n, :],
                                                 view(masks[:, d, 0:2, :], 0, [[0, 4], [C, n], [1, C]]), ALU.mult))
                    steps.link(eng.tensor_tensor(s["Z"], s["g1"][:, :, 0, :], bc(lev[:, d, 0, :]), ALU.mult))
                    steps.link(eng.tensor_tensor(s["Tt"], s["Z"], bc(eye), ALU.add))
                    eng.transpose(flat(s["T"]), flat(s["Tt"])).then_inc(q["masked"], 1)

                def phase(grow, end, prep):
                    after = {-1: ((sums, prep),), 2: ((beta, prep),), 7: ((ended, end), (rho, prep)),
                             8: ((mask_beta, prep),), 9: ((mask_kappa, prep),)}
                    for n in range(-1, 10):
                        if n >= 0 and grow:
                            growth(n, *grow[:2])
                        for f, what in after.get(n, ()):
                            if what:
                                f(*what)

                arrived(eng, "rwkv")
                eng.memset(yC, 0.0)
                arrived(eng, "x_out")
                for d in range(2):
                    eng.memset(st_[d]["M"], 0.0).then_inc(e[d]["mc"], 1)
                walk(eng, steps, phase, per=LINKS)

            def act(eng, steps):
                def phase(grow, end, prep):
                    if prep:
                        d, it, y = prep
                        s, q = st_[d], e[d]
                        eng.wait_ge(q["prev"], it + 1)
                        wait(eng, q["laid"], 2 * it)
                        wait(eng, q["laid2"], it)
                        eng.activation(flat(s["e1"]), flat(s["prev"]), ACT.Exp, scale=-DEC)
                        eng.activation(flat(s["e2"]), flat(s["cum"]), ACT.Exp, scale=DEC)
                        eng.activation(flat(s["e3"]), flat(s["cum"]), ACT.Exp, scale=-DEC).then_inc(q["ex"], 1)
                    if end:
                        d, it, y = end
                        s, q, B = st_[d], e[d], ps[4 * d:4 * d + 4]
                        eng.wait_ge(q["fed"], 3 * it + 1)
                        eng.copy(s["wtb"].rearrange("p a h t -> p (a h t)"), B[2]).then_inc(q["acted"], 1)
                        eng.wait_ge(q["fed"], 3 * it + 2)
                        eng.activation(flat(s["U"]), B[3][:, 0:G], ACT.Copy, scale=-1.0).then_inc(q["acted"], 1)
                    if prep:
                        d, it, y = prep
                        s, q, B = st_[d], e[d], ps[4 * d:4 * d + 4]
                        eng.wait_ge(q["turned"], 2 * it + 2)
                        wait(eng, q["fed"], 3 * it)
                        eng.copy(s["ab"].rearrange("p a h t -> p (a h t)"), B[0])
                        eng.copy(s["kv"].rearrange("p a h t -> p (a h t)"), B[1]).then_inc(q["acted"], 1)

                arrived(eng, "x_out")
                load(eng, "rwkv", masks, A["masks"])
                load(eng, "rwkv", lev, A["lev"])
                load(eng, "rwkv", eye, A["eye"])
                load(eng, "rwkv", reset, A["reset"])
                walk(eng, steps, phase)

            def pool(eng, steps):
                def phase(grow, end, prep):
                    if prep:
                        d, it, y = prep
                        s, q, c = st_[d], e[d], chunk_of(*prep)
                        wait(eng, q["raw"], 2 * it)
                        passed(eng, "pool")
                        eng.tensor_copy(s["vT"], vC[:, c])
                        eng.wait_ge(q["ex"], it + 1)
                        passed(eng, "pool")
                        eng.tensor_tensor(s["ar"][:, :, 0, :], kkC[:, c], s["e1"], ALU.mult)
                        eng.tensor_tensor(s["kT"], kd[d][:, c], s["e2"], ALU.mult).then_inc(q["laid2"], 1)
                walk(eng, steps, phase)

            return dict(pe=pe, dve=dve, act=act, pool=pool)

        r9 = Region(hT.offset, hT.offset + KT * T2)
        rwT = r9.take(4, S)
        gcen = r9.take(4, S)
        g2w = r9.take(512)
        gsig = r9.take(S)
        r10 = Region(sqr.offset, sqr.offset + KT * S)
        gsq = r10.take(4, S)
        gvar = r10.take(2, S)
        groot = [r10.take(S), r10.take(S), r9.take(S), r9.take(S)]
        rw_ready = []

        @stage
        def rwkv_out():
            e = Events(sem, "rwout", {
                "act": (("gate", 1), ("squared", 4), ("rooted", 4)),
                "pe": (("mean", 4), ("summed", 4), ("bonus", 4), ("gated", 4)),
                "dve": (("centred", 4), ("keyed", 4), ("read_out", 4)),
                "pool": (("added", 4),),
            })

            def chunked(ap):
                return ap.rearrange("p (c t) -> p c t", c=NCH)

            def act(eng, steps):
                load(eng, "x_back", xT.rearrange("p a b -> p (a b)"), x_dram)
                load(eng, "g2w", g2w, A["g2w"])
                eng.activation(gsig, gdT, ACT.Sigmoid).then_inc(e.of("gate"), 1)
                for hp in range(4):
                    eng.wait_ge(*e("centred", hp + 1))
                    eng.activation(gsq[:, hp, :], gcen[:, hp, :], ACT.Square).then_inc(e.of("squared"), 1)
                for hp in range(4):
                    eng.wait_ge(*e("summed", hp + 1))
                    eng.activation(groot[hp], ps[4 + hp], ACT.Sqrt, scale=1.0 / 64, bias=eps_rw).then_inc(e.of("rooted"), 1)

            def pe(eng, steps):
                for hp in range(4):
                    eng.matmul(chunked(ps[hp]), ones64, yC[:, :, hp, :], start=True, stop=True).then_inc(e.of("mean"), 1)
                for hp in range(4):
                    eng.wait_ge(*e("squared", hp + 1))
                    eng.matmul(ps[4 + hp], ones64, gsq[:, hp, :], start=True, stop=True).then_inc(e.of("summed"), 1)
                for hp in range(4):
                    eng.wait_ge(*e("keyed", hp + 1))
                    eng.wait_ge(*e("centred", hp + 1))
                    eng.matmul(chunked(ps[hp]), ones64, kka[0][:, 0:NCH, hp, :], start=True, stop=True)\
                       .then_inc(e.of("bonus"), 1)
                arrived(eng, "g2w")
                eng.wait_ge(*e("gate", 1))
                for hp in range(4):
                    eng.wait_ge(*e("rooted", hp + 1))
                    eng.matmul(ps[4 + hp], g2w[:, hp * P:(hp + 1) * P], gsig, start=True, stop=True).then_inc(e.of("gated"), 1)

            def dve(eng, steps):
                for hp in range(4):
                    eng.wait_ge(*e("mean", hp + 1))
                    eng.scalar_tensor_tensor(chunked(gcen[:, hp, :]), chunked(ps[hp]), -1.0 / 64, yC[:, :, hp, :],
                                             ALU.mult, ALU.add).then_inc(e.of("centred"), 1)
                for hp in range(4):
                    t = kka[0][:, 0:NCH, hp, :]
                    eng.wait_ge(*e("added", hp + 1))
                    eng.scalar_tensor_tensor(t, t, col("r_k", hp), rC[:, :, hp, :], ALU.mult, ALU.mult)\
                       .then_inc(e.of("keyed"), 1)
                eng.wait_ge(*e("centred", 4))
                for hp in range(4):
                    g = gcen[:, hp, :]
                    eng.wait_ge(*e("rooted", hp + 1))
                    steps.did(eng.reciprocal(gvar[:, hp % 2, :], groot[hp]))
                    eng.wait_ge(*e("bonus", hp + 1))
                    steps.did(eng.tensor_tensor(chunked(rwT[:, hp, :]), chunked(ps[hp]), vC[:, 4:12, hp, :], ALU.mult))
                    steps.wait()
                    steps.link(eng.scalar_tensor_tensor(g, g, col("gn_g", hp), gvar[:, hp % 2, :], ALU.mult, ALU.mult))
                    steps.link(eng.scalar_tensor_tensor(rwT[:, hp, :], g, col("gn_b", hp), rwT[:, hp, :], ALU.add, ALU.add))
                    eng.wait_ge(*e("gated", hp + 1))
                    eng.tensor_tensor(rwT[:, hp, :], rwT[:, hp, :], ps[4 + hp], ALU.mult).then_inc(e.of("read_out"), 1)
                    eng.wait_ge(*e("read_out", hp + 1))
                    eng.sem_inc(sem("residual_free"), 1)
                arrived(eng, "x_back")

            def pool(eng, steps):
                for hp in range(4):
                    eng.tensor_tensor(kka[0][:, 0:NCH, hp, :], kd[0][:, 4:12, hp, :], kd[1][:, 4:12, hp, :], ALU.add)\
                       .then_inc(e.of("added"), 1)

            rw_ready.append(e("read_out", 0))
            return dict(act=act, pe=pe, dve=dve, pool=pool)

        @joined
        def out2():
            s, n = rw_ready[0]

            def ready(eng, k):
                if k >= 4:
                    eng.wait_ge(s, n + k - 3)
            return residual("out2", lambda k: fT[:, k, :] if k < 4 else rwT[:, k - 4, :], gate=lambda m: mod[:, 16 + m, 0:1],
                            ready=ready, primed=True)

        @joined
        def norm_ffn2():
            return norm(lambda k: xT[:, k, :], lambda k: hT[:, k, 0:S], lambda k: gains[:, 2, k:k + 1], source=added(),
                        rows=lambda eng: eng.sem_inc(sem("f2_free"), 4),
                        shift=lambda k: mod[:, 24 + k, 0:1])

        r11 = base.remainder()
        act2T = r11.take(FT, S)
        pad = r11.take(4, 10, 66)
        cacc = r11.take(4, 8, 64)
        csil = r11.take(2, S)
        fcw = cols[:, COL0["fc_w"]:COL0["fc_w"] + 396].rearrange("p (k t) -> p k t", k=9)
        fcb = cols[:, COL0["fc_b"]:COL0["fc_b"] + 44]

        @joined
        def ffn2():
            free, padded, convolved, silued, conv_used, used = (sem("f2_" + x) for x in (
                "free", "padded", "convolved", "silued", "conv_used", "used"))
            u0 = UNIT0["ffn2"]
            NI = FT // 2
            ready = normed()

            def pe(eng, steps):
                linear_pe(eng, u0, 2 * FT, lambda k: hT[:, k, 0:S], free, ready=ready)

            def act(eng, steps):
                def grids(i, f):
                    for j in (2 * f, 2 * f + 1):
                        eng.wait_ge(units_done, u0 + 4 * i + j + 1)
                        eng.wait_ge(conv_used, 4 * i + j + 1)
                        eng.copy(pad[:, j, 1:9, 1:65], ps[j].rearrange("p (y x) -> p y x", y=8)).then_inc(padded, 1)
                        eng.wait_ge(padded, 4 * i + j + 1)
                        eng.sem_inc(free, 1)

                def silu(i, f):
                    eng.wait_ge(convolved, 4 * i + 2 * f + 1)
                    eng.wait_ge(used, 2 * i + f + 1)
                    eng.activation(csil[:, f, :], cacc[:, 2 * f].rearrange("p y x -> p (y x)"), ACT.Silu,
                                   bias=fcb[:, bass.ds(2 * i + f, 1)]).then_inc(silued, 1)

                grids(0, 0)
                with eng.Fori(0, NI - 1) as i:
                    for f in range(2):
                        grids(i + f, 1 - f)
                        silu(i, f)
                grids(NI - 1, 1)
                silu(NI - 1, 0)
                silu(NI - 1, 1)

            def dve(eng, steps):
                def taps(i, f):
                    for j in (2 * f, 2 * f + 1):
                        eng.wait_ge(padded, 4 * i + j + 1)
                    for tap in range(9):
                        for j in (2 * f, 2 * f + 1):
                            w = fcw[:, tap, bass.ds(2 * i + f + FT * (j % 2), 1)]
                            src = pad[:, j, tap // 3:tap // 3 + 8, tap % 3:tap % 3 + 64]
                            if tap == 0:
                                steps.did(eng.tensor_scalar(cacc[:, j], src, w, None, ALU.mult))
                            else:
                                steps.did_but(1, lambda: eng.scalar_tensor_tensor(cacc[:, j], src, w, cacc[:, j],
                                                                                  ALU.mult, ALU.add))
                    steps.wait()
                    eng.sem_inc(conv_used, 2)
                    eng.sem_inc(convolved, 2)

                def gated(i, f):
                    eng.wait_ge(silued, 2 * i + f + 1)
                    passed(eng, "dve")
                    eng.scalar_tensor_tensor(act2T[:, bass.ds(2 * i + f, 1), :].rearrange("p a t -> p (a t)"),
                                             cacc[:, 2 * f + 1].rearrange("p y x -> p (y x)"),
                                             fcb[:, bass.ds(FT + 2 * i + f, 1)], csil[:, f, :], ALU.add, ALU.mult)\
                       .then_inc(used_dve, 1)
                    eng.wait_ge(used_dve, 2 * i + f + 1)
                    eng.sem_inc(used, 1)

                steps.link(eng.memset(pad, 0.0))
                eng.sem_inc(conv_used, 4)
                eng.sem_inc(used, 2)
                taps(0, 0)
                with steps.loop(NI - 1, 36) as i:
                    for f in range(2):
                        taps(i + f, 1 - f)
                        gated(i, f)
                eng.sem_inc(sem("residual_free"), 4)
                taps(NI - 1, 1)
                gated(NI - 1, 0)
                gated(NI - 1, 1)

            used_dve = sem("f2_act")
            return dict(pe=pe, act=act, dve=dve)

        @joined
        def down2():
            used = sem("f2_used")

            def ready(eng, k):
                if k == 0:
                    eng.wait_ge(sem("f2_free"), 4 + 2 * FT)
                eng.wait_ge(used, 2 + min(k + 1, FT))
            return residual("down2", lambda k: act2T[:, k, :], ktiles=FT, gate=lambda m: mod[:, 40 + m, 0:1], ready=ready,
                            primed=True)

        @joined
        def norm_final2():
            return norm(lambda k: xT[:, k, :], lambda k: xT[:, k, :], lambda k: col("fin2_g", k), source=added())

        named = dict(locals())
        @block.tensor
        def _(eng):
            run(eng, "pe", Steps(eng, sem("pe_steps")))

        @block.vector
        def _(eng):
            run(eng, "dve", Steps(eng, sem("dve_steps")))

        @block.scalar
        def _(eng):
            run(eng, "act", Steps(eng, sem("act_steps")))

        @block.gpsimd
        def _(eng):
            run(eng, "pool", Steps(eng, sem("pool_steps")))

        @block.sync
        def _(eng):
            for j in range(4):
                eng.dma_start(ring[:, j], units[j]).then_inc(landed[j], 16)
            with eng.Fori(1, nunits // 4) as i:
                for j in range(4):
                    eng.wait_ge(units_done, 4 * i + (j - 3))
                    eng.dma_start(ring[:, j], units[4 * i + j]).then_inc(landed[j], 16)
            eng.wait_ge(stage_done, 4 * len(stages))
            for n, (name, dst) in enumerate(dump or []):
                eng.dma_start(dst, named[name]).then_inc(sem("dumped"), 16)
            if out is not None:
                eng.dma_start(out, xT).then_inc(sem("stored"), 16)
                eng.wait_ge(sem("stored"), 16)
            if dump:
                arrived(eng, *loaded)
                eng.wait_ge(sem("dumped"), 16 * len(dump))



def _thirds_last(units):
    u = units.reshape(2, 4, 3, P, 8, P)
    return np.concatenate([u[:, :, 0:2].reshape(2, 8, P, 8, P), u[:, :, 2]], axis=1).reshape(-1, P, 8, P)


def _tiles(w):
    k, m = w.shape
    kp, mp = -(-k // D) * D, -(-m // P) * P
    full = np.zeros((kp, mp), np.float32)
    full[:k, :m] = w
    return full.reshape(kp // D, 8, P, mp // P, P).transpose(3, 0, 2, 1, 4).reshape(-1, P, 8, P)


def _columns(v):
    return np.ascontiguousarray(v.reshape(-1, P).T)


def t5_bucket(n):
    large = 16 + (np.log(np.maximum(n, 1) / np.float32(16)) / math.log(8) * 16).astype(np.int32)
    return np.where(n < 16, n, np.minimum(large, 31))


def layout(x):
    g = {k: np.asarray(v, np.float32) for k, v in x.items()}
    A = {}
    w = g["w_in"][0]
    cut = np.cumsum([0, 512, 128, 128, 128, 128, 128, 128, 24, 512, 128, 128, 256, 16, 256])
    nq, kc, vc, ks, vs, kw, vw, ng, cu, gq, gk, gv, ga, gr = (w[:, a:b] for a, b in zip(cut[:-1], cut[1:]))
    heads = [h for j in range(NPAIR) for h in (j, NPAIR + j)]
    nq = np.concatenate([nq[:, 64 * h:64 * h + 64] for h in heads], axis=1)
    ga = np.concatenate([ga, np.zeros((D, P - 16), np.float32)], axis=1)
    units = {}
    units["in1"] = _tiles(np.concatenate([cu, ks, kw, kc, vc, gq, gk, ga, nq, gr], axis=1))
    wo = g["w_out"][0]
    wo = np.concatenate([wo[64 * h:64 * h + 64] for h in heads] + [wo[512:]], axis=0)
    units["out1"] = _tiles(wo)

    def pairs(a, b):
        return np.stack([_tiles(a), _tiles(b)], axis=1).reshape(-1, P, 8, P)

    units["ffn1"] = pairs(g["ffn_w_gate"][0], g["ffn_w_up"][0])
    units["down1"] = _thirds_last(_tiles(g["ffn_w_down"][0]))
    pp = g["ple_w_proj"][0].reshape(2, P, 2, 4, P).transpose(2, 1, 3, 0, 4).reshape(2, P, 8, P)
    units["pleproj"] = pp
    units["ple"] = _tiles(g["ple_w_gate"][0])
    ada = g["ada_w_2"][0].reshape(4, 2, P, 12, 512).transpose(3, 0, 2, 1, 4).reshape(48, P, 8, P)
    units["ada"] = ada[0:24]
    for b in range(6, 12):
        units[f"ada{b}"] = ada[4 * b:4 * b + 4]
    w2 = g["w_in_2"][0]
    units["in2"] = _tiles(np.concatenate([w2[:, 512:], w2[:, :512]], axis=1))
    units["out2"] = _tiles(g["w_out_2"][0])
    units["ffn2"] = pairs(g["ffn_w_up_2"][0][:, :2816], g["ffn_w_up_2"][0][:, 2816:])
    units["down2"] = _thirds_last(_tiles(g["ffn_w_down_2"][0]))
    units = np.concatenate([units[name] for name, _ in STREAM])
    A["units"] = np.concatenate([units, np.zeros((NUNITS_PAD - len(units), P, 8, P), np.float32)])
    assert len(units) == NUNITS

    A["wn"] = np.concatenate([vs, vw, gv, ng], axis=1).reshape(8, P, 536).transpose(1, 0, 2)
    A["xT"] = g["x"][0].T.reshape(8, P, S).transpose(1, 0, 2)
    ident = np.eye(P, dtype=np.float32)
    two = np.kron(np.eye(2), np.ones((64, 64))).astype(np.float32)
    A["consts"] = np.concatenate([ident, np.ones((P, P), np.float32), two], axis=1)
    d = 511 - np.arange(640)
    A["onehot"] = (t5_bucket(np.maximum(d, 0))[None, :] == np.arange(32)[:, None]).astype(np.float32)
    A["negmask"] = np.tile(np.where(d < 0, NEG, 0.0).astype(np.float32), (8, 1))
    A["rel_bias"] = g["rel_bias"]
    A["cw1"] = np.stack([g["cmp_w1_" + n][0].reshape(16, P, 256).transpose(1, 0, 2) for n in "kv"])
    A["cw2"] = np.stack([g["cmp_w2_" + n][0].reshape(2, P, 64).transpose(1, 0, 2) for n in "kv"])
    A["gla_wa"] = g["gla_w_alpha"][0]
    A["gl_reset"] = np.tile((np.arange(S) % C != 0).astype(np.float32), (P, 1))
    tri = (np.arange(C)[:, None] <= np.arange(C)[None, :]).astype(np.float32)
    A["gl_mask"] = np.tile(tri, (2, 1))
    A["ctxT"] = g["ctx_2"][0].T.reshape(8, P, CTX).transpose(1, 0, 2)
    A["w_low"] = g["decay_w2_2"][0].reshape(P, 512)
    A["a_low"] = g["iclr_a2_2"][0].reshape(P, 512)
    A["g2w"] = g["gate_g2_2"][0]
    ang = 2 * np.pi * np.outer(np.arange(S), np.arange(S)) % (2 * np.pi * S) / S
    A["dft"] = (np.stack([np.cos(ang), -np.sin(ang)]) / math.sqrt(S)).reshape(2, 4, P, S).transpose(2, 0, 1, 3)
    ang = 2 * np.pi * np.outer(np.arange(C), np.arange(C)) / C
    A["dft64"] = np.concatenate([np.kron(np.eye(2), f(ang) / 8) for f in (np.cos, np.sin)], axis=1)
    s, t = np.arange(C)[:, None], np.arange(C)[None, :]
    before, upto = s < t, s <= t
    fwd = np.stack([before, upto, before.T, before.T])
    rev = np.stack([before.T, upto.T, before, before])
    A["masks"] = np.concatenate([np.stack([fwd, rev]).transpose(2, 0, 1, 3)] * 2, axis=0)
    lv = [-1.0 * (before & (s // 2 == t // 2))]
    for b in (2, 4, 8, 16, 32):
        lv.append(1.0 * (before & (s // (2 * b) == t // (2 * b)) & (s // b != t // b)).T)
    lv = np.stack(lv)
    lv2 = lv.transpose(0, 2, 1)
    A["lev"] = np.concatenate([np.stack([lv, lv2]).transpose(2, 0, 1, 3)] * 2, axis=0)
    A["eye"] = np.tile(np.eye(C), (2, 1))
    A["reset"] = np.tile((np.arange(4 * C) % C != 0), (P, 2, 1))
    A["pT"] = g["p"][0, 0].T.reshape(2, P, S).transpose(1, 0, 2)
    c = {"mix_g": g["mix_norm_g"], "ffn_g": g["ffn_norm_g"], "ple_g": g["ple_norm_g"], "fin_g": g["final_norm_g"],
         "b1k": g["cmp_b1_k"], "b1v": g["cmp_b1_v"], "conv_b": g["conv_b"], "ln_g": g["conv_ln_g"],
         "ln_b": g["conv_ln_b"], "gla_b": g["gla_b_alpha"], "gla_g": g["gla_norm_g"],
         "conv_w": g["conv_w"][0], "posk": g["cmp_pos_k"][0], "posv": g["cmp_pos_v"][0],
         "n1_g": g["norm1_g_2"], "n2_g": g["norm2_g_2"], "fin2_g": g["final_g_2"], "ada_b": g["ada_b_2"],
         "c": np.concatenate([g["c_2"], g["c_ctx_2"][None]]), "rconv": g["rwkv_conv_w_2"][0],
         "w0": g["decay_w0_2"][0], "a0": g["iclr_a0_2"][0], "k_k": g["k_k_2"], "k_a": g["k_a_2"],
         "r_k": g["r_k_2"].reshape(1, 512), "gn_g": g["gn_g_2"], "gn_b": g["gn_b_2"],
         "fc_w": g["ffn_conv_w_2"][0].reshape(9, -1), "fc_b": g["ffn_conv_b_2"],
         "fo_g": g["fourier_g_2"]}
    A["cols"] = np.concatenate([_columns(c[name]) for name, _ in COLS], axis=1)
    return {k: np.ascontiguousarray(v, dtype=np.float32) for k, v in A.items()}



def kernel(**inputs):
    import concourse.bacc as bacc
    from concourse.bass_utils import run_bass_kernel_spmd

    nc = bacc.Bacc("TRN2", target_bir_lowering=False, num_devices=1)
    arrays = {f"in_{k}": v for k, v in layout(inputs).items()}
    A = {k[3:]: nc.dram_tensor(k, v.shape, F32, kind="ExternalInput").ap() for k, v in arrays.items()}
    out = nc.dram_tensor("out_0", (P, KT, S), F32, kind="ExternalOutput").ap()
    build(nc, A, out)
    r = run_bass_kernel_spmd(nc, [arrays], core_ids=[0])
    return np.ascontiguousarray(r.results[0]["out_0"].transpose(2, 1, 0).reshape(1, S, D))
```
